# Optimizing a Trainium2 kernel written in Bass

```python
import jax, jax.numpy as jnp
from jax import lax
import numpy as np

D_MODEL = 1024
BATCH = 1
SEQ = 512
DEPTH = 2

CHUNK = 64
Q_BLOCK = 128
EPS = 1e-6
GDN_WIDTH = D_MODEL // 2
GDN_HEAD_DIM = 128
GDN_HEADS = GDN_WIDTH // GDN_HEAD_DIM
CONV_K = 4
FOX_WIDTH = D_MODEL - GDN_WIDTH
FOX_HEAD_DIM = 64
FOX_HEADS = FOX_WIDTH // FOX_HEAD_DIM
MEM_TOKENS = 256
MEM_HEADS = 4
MEM_HEAD_DIM = D_MODEL // MEM_HEADS
PEER_HEADS = 8
PEER_KEYS = 128
PEER_EXPERTS = PEER_KEYS * PEER_KEYS
PEER_QDIM = 256
PEER_HALF = PEER_QDIM // 2
PEER_TOPK = 16
PEER_TOKEN_BLOCK = 128
IN_COLS = 3 * GDN_WIDTH + GDN_WIDTH + 2 * GDN_HEADS + 3 * FOX_WIDTH + FOX_HEADS

kernel_name = "hybrid_gdn_fox_peer_trunk"

def rms_norm(x, gain):
    xf = x.astype(jnp.float32)
    y = xf * lax.rsqrt(jnp.mean(xf * xf, axis=-1, keepdims=True) + EPS)
    return (y * gain.astype(jnp.float32)).astype(x.dtype)

def l2_norm(x):
    xf = x.astype(jnp.float32)
    return xf * lax.rsqrt(jnp.sum(xf * xf, axis=-1, keepdims=True) + EPS)

def causal_depthwise_conv(x, w):
    return lax.conv_general_dilated(x, w.astype(x.dtype), window_strides=(1,),
                                    padding=[(CONV_K - 1, 0)],
                                    dimension_numbers=('NWC', 'WIO', 'NWC'),
                                    feature_group_count=x.shape[-1])

def gated_delta_rule(q, k, v, log_alpha, beta):
    B, T, H, dk = q.shape
    dv = v.shape[-1]
    n = T // CHUNK

    def chunks(a):
        return jnp.swapaxes(a.reshape(B, n, CHUNK, H, *a.shape[3:]), 2, 3)

    q = chunks(q) * (dk ** -0.5)
    k = chunks(k)
    v = chunks(v)
    g = jnp.cumsum(chunks(log_alpha), axis=-1)
    b = chunks(beta)
    causal = jnp.tril(jnp.ones((CHUNK, CHUNK), bool))
    strict = jnp.tril(jnp.ones((CHUNK, CHUNK), bool), -1)
    diff = g[..., :, None] - g[..., None, :]
    decay = jnp.where(causal, jnp.exp(jnp.where(causal, diff, 0.0)), 0.0)
    k_beta = k * b[..., None]
    a = jnp.where(strict, jnp.einsum('bnhik,bnhjk->bnhij', k_beta, k) * decay, 0.0)
    eye = jnp.eye(CHUNK, dtype=jnp.float32)
    t_inv = lax.linalg.triangular_solve(eye + a, jnp.broadcast_to(eye, a.shape),
                                        left_side=True, lower=True)
    w = jnp.einsum('bnhij,bnhjk->bnhik', t_inv, k_beta * jnp.exp(g)[..., None])
    u = jnp.einsum('bnhij,bnhjv->bnhiv', t_inv, v * b[..., None])
    qk = jnp.where(causal, jnp.einsum('bnhik,bnhjk->bnhij', q, k) * decay, 0.0)
    q_dec = q * jnp.exp(g)[..., None]
    k_dec = k * jnp.exp(g[..., -1:] - g)[..., None]
    g_last = jnp.exp(g[..., -1])

    def step(state, inp):
        w_c, u_c, qd_c, kd_c, qk_c, gl_c = inp
        v_new = u_c - jnp.einsum('bhck,bhkv->bhcv', w_c, state)
        o = jnp.einsum('bhck,bhkv->bhcv', qd_c, state) + jnp.einsum('bhij,bhjv->bhiv', qk_c, v_new)
        state = state * gl_c[..., None, None] + jnp.einsum('bhck,bhcv->bhkv', kd_c, v_new)
        return state, o

    xs = tuple(jnp.moveaxis(t, 1, 0) for t in (w, u, q_dec, k_dec, qk, g_last))
    s0 = jnp.zeros((B, H, dk, dv), jnp.float32)
    _, o = lax.scan(step, s0, xs)
    return jnp.swapaxes(jnp.moveaxis(o, 0, 1), 2, 3).reshape(B, T, H, dv)

def forgetting_attention(q, k, v, log_f):
    B, T, H, d = q.shape
    nb = T // Q_BLOCK
    c = jnp.cumsum(log_f, axis=1).transpose(0, 2, 1)
    kh = k.transpose(0, 2, 1, 3)
    vh = v.transpose(0, 2, 1, 3)
    qb = q.transpose(0, 2, 1, 3).reshape(B, H, nb, Q_BLOCK, d).transpose(2, 0, 1, 3, 4)
    cb = c.reshape(B, H, nb, Q_BLOCK).transpose(2, 0, 1, 3)
    pos_k = jnp.arange(T)
    scale = d ** -0.5

    def block(args):
        q_i, c_i, i = args
        pos_q = i * Q_BLOCK + jnp.arange(Q_BLOCK)
        s = jnp.einsum('bhqd,bhkd->bhqk', q_i, kh) * scale + c_i[..., :, None] - c[..., None, :]
        s = jnp.where(pos_k[None, :] <= pos_q[:, None], s, -jnp.inf)
        p = jax.nn.softmax(s, axis=-1)
        return jnp.einsum('bhqk,bhkd->bhqd', p, vh)

    o = lax.map(block, (qb, cb, jnp.arange(nb)))
    return o.transpose(1, 0, 3, 2, 4).reshape(B, T, H, d)

def hybrid_mixer(h, w_in, conv_w, a_log, dt_bias, gdn_out_norm, fox_q_norm, fox_k_norm, fox_f_bias, w_out):
    B, T, _ = h.shape
    f32 = jnp.float32
    proj = h @ w_in
    o1 = 3 * GDN_WIDTH
    o2 = o1 + GDN_WIDTH
    o3 = o2 + GDN_HEADS
    o4 = o3 + GDN_HEADS
    o5 = o4 + 3 * FOX_WIDTH
    gdn_qkv, gdn_gate, gdn_a, gdn_b, fox_qkv, fox_f = jnp.split(proj, [o1, o2, o3, o4, o5], axis=-1)
    gdn_qkv = jax.nn.silu(causal_depthwise_conv(gdn_qkv, conv_w))
    gq, gk, gv = jnp.split(gdn_qkv, 3, axis=-1)
    gq = l2_norm(gq.reshape(B, T, GDN_HEADS, GDN_HEAD_DIM))
    gk = l2_norm(gk.reshape(B, T, GDN_HEADS, GDN_HEAD_DIM))
    gv = gv.reshape(B, T, GDN_HEADS, GDN_HEAD_DIM).astype(f32)
    log_alpha = -jnp.exp(a_log.astype(f32)) * jax.nn.softplus(gdn_a.astype(f32) + dt_bias.astype(f32))
    beta = jax.nn.sigmoid(gdn_b.astype(f32))
    o_gdn = gated_delta_rule(gq, gk, gv, log_alpha, beta)
    o_gdn = rms_norm(o_gdn, gdn_out_norm) * jax.nn.silu(
        gdn_gate.reshape(B, T, GDN_HEADS, GDN_HEAD_DIM).astype(f32))
    fq, fk, fv = jnp.split(fox_qkv, 3, axis=-1)
    fq = rms_norm(fq.reshape(B, T, FOX_HEADS, FOX_HEAD_DIM), fox_q_norm).astype(f32)
    fk = rms_norm(fk.reshape(B, T, FOX_HEADS, FOX_HEAD_DIM), fox_k_norm).astype(f32)
    fv = fv.reshape(B, T, FOX_HEADS, FOX_HEAD_DIM).astype(f32)
    log_f = jax.nn.log_sigmoid(fox_f.astype(f32) + fox_f_bias.astype(f32))
    o_fox = forgetting_attention(fq, fk, fv, log_f)
    y = jnp.concatenate([o_gdn.reshape(B, T, GDN_WIDTH), o_fox.reshape(B, T, FOX_WIDTH)], axis=-1)
    return y.astype(h.dtype) @ w_out

def memory_cross_attention(h, mem, mem_norm, w_mq, w_mkv, mq_norm, mk_norm, w_mo):
    B, T, D = h.shape
    M = mem.shape[1]
    f32 = jnp.float32
    mem_h = rms_norm(mem, mem_norm)
    q = rms_norm((h @ w_mq).reshape(B, T, MEM_HEADS, MEM_HEAD_DIM), mq_norm).astype(f32)
    k, v = jnp.split(mem_h @ w_mkv, 2, axis=-1)
    k = rms_norm(k.reshape(B, M, MEM_HEADS, MEM_HEAD_DIM), mk_norm).astype(f32)
    v = v.reshape(B, M, MEM_HEADS, MEM_HEAD_DIM).astype(f32)
    s = jnp.einsum('bthd,bmhd->bhtm', q, k) * (MEM_HEAD_DIM ** -0.5)
    p = jax.nn.softmax(s, axis=-1)
    o = jnp.einsum('bhtm,bmhd->bthd', p, v).reshape(B, T, D).astype(h.dtype)
    return o @ w_mo

def peer_ffn(h, w_pq, sub_keys, expert_u, expert_v):
    B, T, D = h.shape
    M = B * T
    hf = h.reshape(M, D)
    q = (hf @ w_pq).reshape(M, PEER_HEADS, 2, PEER_HALF)
    s1 = jnp.einsum('mhd,hnd->mhn', q[:, :, 0], sub_keys[0]).astype(jnp.float32)
    s2 = jnp.einsum('mhd,hnd->mhn', q[:, :, 1], sub_keys[1]).astype(jnp.float32)
    v1, i1 = lax.top_k(s1, PEER_TOPK)
    v2, i2 = lax.top_k(s2, PEER_TOPK)
    cand_s = (v1[..., :, None] + v2[..., None, :]).reshape(M, PEER_HEADS, PEER_TOPK * PEER_TOPK)
    cand_i = (i1[..., :, None] * PEER_KEYS + i2[..., None, :]).reshape(M, PEER_HEADS, PEER_TOPK * PEER_TOPK)
    top_s, top_pos = lax.top_k(cand_s, PEER_TOPK)
    idx = jnp.take_along_axis(cand_i, top_pos, axis=-1)
    gate = jax.nn.softmax(top_s, axis=-1)
    nb = M // PEER_TOKEN_BLOCK

    def block(args):
        x_b, idx_b, g_b = args
        u = expert_u[idx_b]
        act = jax.nn.gelu(jnp.einsum('mhkd,md->mhk', u, x_b).astype(jnp.float32))
        return jnp.einsum('mhk,mhkd->md', act * g_b, expert_v[idx_b].astype(jnp.float32))

    y = lax.map(block, (hf.reshape(nb, PEER_TOKEN_BLOCK, D),
                        idx.reshape(nb, PEER_TOKEN_BLOCK, PEER_HEADS, PEER_TOPK),
                        gate.reshape(nb, PEER_TOKEN_BLOCK, PEER_HEADS, PEER_TOPK)))
    return y.reshape(B, T, D).astype(h.dtype)

def setup_inputs(seed: int = 0) -> dict:
    key = jax.random.key(seed)
    ks = jax.random.split(key, 26)
    nrm = jax.random.normal
    D = D_MODEL

    def gain(k, n):
        return 1.0 + 0.02 * nrm(k, (DEPTH, n), jnp.float32)

    dt = jnp.exp(jax.random.uniform(ks[5], (DEPTH, GDN_HEADS), jnp.float32,
                                    minval=np.log(1e-3), maxval=np.log(1e-1)))
    return {
        "x": nrm(ks[0], (BATCH, SEQ, D), jnp.float32),
        "mem": nrm(ks[1], (BATCH, MEM_TOKENS, D), jnp.float32),
        "mix_norm": gain(ks[2], D),
        "w_in": nrm(ks[3], (DEPTH, D, IN_COLS), jnp.float32) * D ** -0.5,
        "conv_w": nrm(ks[4], (DEPTH, CONV_K, 1, 3 * GDN_WIDTH), jnp.float32) * CONV_K ** -0.5,
        "a_log": jnp.log(jax.random.uniform(ks[6], (DEPTH, GDN_HEADS), jnp.float32, minval=1.0, maxval=16.0)),
        "dt_bias": dt + jnp.log(-jnp.expm1(-dt)),
        "gdn_out_norm": gain(ks[7], GDN_HEAD_DIM),
        "fox_q_norm": gain(ks[8], FOX_HEAD_DIM),
        "fox_k_norm": gain(ks[9], FOX_HEAD_DIM),
        "fox_f_bias": 2.0 + 0.5 * nrm(ks[10], (DEPTH, FOX_HEADS), jnp.float32),
        "w_out": nrm(ks[11], (DEPTH, D, D), jnp.float32) * D ** -0.5,
        "xattn_norm": gain(ks[12], D),
        "mem_norm": gain(ks[13], D),
        "w_mq": nrm(ks[14], (DEPTH, D, D), jnp.float32) * D ** -0.5,
        "w_mkv": nrm(ks[15], (DEPTH, D, 2 * D), jnp.float32) * D ** -0.5,
        "mq_norm": gain(ks[16], MEM_HEAD_DIM),
        "mk_norm": gain(ks[17], MEM_HEAD_DIM),
        "w_mo": nrm(ks[18], (DEPTH, D, D), jnp.float32) * D ** -0.5,
        "ffn_norm": gain(ks[19], D),
        "w_pq": nrm(ks[20], (DEPTH, D, PEER_HEADS * PEER_QDIM), jnp.float32) * D ** -0.5,
        "sub_keys": nrm(ks[21], (DEPTH, 2, PEER_HEADS, PEER_KEYS, PEER_HALF), jnp.float32) * PEER_HALF ** -0.5,
        "expert_u": nrm(ks[22], (DEPTH, PEER_EXPERTS, D), jnp.float32) * D ** -0.5,
        "expert_v": nrm(ks[23], (DEPTH, PEER_EXPERTS, D), jnp.float32) * PEER_HEADS ** -0.5,
    }

def reference(x, mem, mix_norm, w_in, conv_w, a_log, dt_bias, gdn_out_norm, fox_q_norm, fox_k_norm,
              fox_f_bias, w_out, xattn_norm, mem_norm, w_mq, w_mkv, mq_norm, mk_norm, w_mo,
              ffn_norm, w_pq, sub_keys, expert_u, expert_v):
    for l in range(DEPTH):
        h = rms_norm(x, mix_norm[l])
        x = x + hybrid_mixer(h, w_in[l], conv_w[l], a_log[l], dt_bias[l], gdn_out_norm[l],
                             fox_q_norm[l], fox_k_norm[l], fox_f_bias[l], w_out[l])
        h = rms_norm(x, xattn_norm[l])
        x = x + memory_cross_attention(h, mem, mem_norm[l], w_mq[l], w_mkv[l], mq_norm[l], mk_norm[l], w_mo[l])
        h = rms_norm(x, ffn_norm[l])
        x = x + peer_ffn(h, w_pq[l], sub_keys[l], expert_u[l], expert_v[l])
    return x


_drawn_inputs = setup_inputs


def setup_inputs(seed=0):
    import zlib

    import numpy as np

    out = dict(_drawn_inputs(seed))
    spreads = {}
    factors = {'xattn_norm': 3.627, 'mem_norm': 3.042, 'mq_norm': 3.55, 'mk_norm': 3.547}
    for name, (base, spread) in spreads.items():
        noise = np.random.default_rng([zlib.crc32(name.encode()), seed]).standard_normal(out[name].shape)
        drawn = base * np.exp(spread * noise) if base else spread * noise
        out[name] = __import__('jax').numpy.asarray(drawn.astype(out[name].dtype))
    for name, factor in factors.items():
        out[name] = (out[name] * factor).astype(out[name].dtype)
    return out
```

```python
import concourse.bass as bass
import numpy as np
from concourse import mybir
from contextlib import ExitStack

P = 128
D = 1024
SEQ = 512
DEPTH = 2
NT = SEQ // P
DC = D // P
CH = 64
GH = 4
FH = 8
FD = 64
MEM = 256
MT = MEM // P
MH = 4
PH = 8
TOPK = 16
CONV_K = 4
NEXP_HI = 128
EPS = 1e-6
N_PAIRS = 11
PAIR_VS, PAIR_OUT, PAIR_MQ, PAIR_MK, PAIR_MV, PAIR_MO, PAIR_PQ = 3, 4, 5, 6, 7, 8, 9
NEG = -1e30
GRP = 8
TOK_STEP = 8

PC = {}
_at = 0
for _name, _n in (("mix", DC), ("xattn", DC), ("mem", DC), ("ffn", DC), ("conv", 12 * CONV_K), ("gdn_out", 1),
                  ("fox_q", 1), ("fox_k", 1), ("mq", 2), ("mk", 2), ("dt", GH), ("a_log", GH), ("f_bias", FH)):
    PC[_name] = _at
    _at += _n
NPAR = _at

LEVELS = 6
CC = {}
_at = 0
for _name, _n in (("ident", P), ("ones", P), ("blk64", P), ("tri_chunk", P), ("tri", P), ("strict", P),
                  ("level", LEVELS * P), ("causal", P), ("iota", P), ("bias", 4)):
    CC[_name] = _at
    _at += _n
NCONST = _at


def constants():
    r = np.arange(P)
    a, b = r[:, None], r[None, :]
    same = (a // CH) == (b // CH)
    c = np.zeros((P, NCONST), np.float32)

    def put(name, m):
        c[:m.shape[0], CC[name]:CC[name] + m.shape[1]] = m

    put("ident", np.eye(P))
    put("ones", np.ones((P, P)))
    put("blk64", same)
    put("tri_chunk", same & (a <= b))
    put("tri", a <= b)
    put("strict", same & (a > b))
    put("level", np.concatenate([(a // (2 * m) == b // (2 * m)) & (a % (2 * m) >= m) & (b % (2 * m) < m)
                                 for m in (1, 2, 4, 8, 16, 32)], axis=1))
    put("causal", np.where(b <= a, 0.0, NEG))
    put("iota", np.broadcast_to(b, (P, P)))
    put("bias", np.broadcast_to(np.array([EPS, np.log(P ** -0.5), np.log(FD ** -0.5), 0.0]), (P, 4)))
    return c


def trunk_kernel(nc, x, mem, weights, params, consts, keys, expert_u, expert_v, out):
    f32, u32 = mybir.dt.float32, mybir.dt.uint32
    ALU, ACT, AX = mybir.AluOpType, mybir.ActivationFunctionType, mybir.AxisListType
    gates_dram = nc.dram_tensor("gates_dram", (NEXP_HI, P, SEQ), f32, kind="Internal").ap()

    ctx = ExitStack()
    with ctx:
        def sb(name, shape, dt=f32):
            return ctx.enter_context(nc.sbuf_tensor(name, shape, dt))

        def sem(name):
            return ctx.enter_context(nc.semaphore(name))

        X = sb("X", [P, NT, D])
        hT = sb("hT", [P, DC, SEQ])
        wring = sb("wring", [P, 2, DC, 512])
        cst = sb("cst", [P, NCONST])
        par = sb("par", [P, NPAR])
        stats = sb("stats", [P, 256])
        ARENA = 32700
        arena = sb("arena", [P, ARENA])
        PS = ctx.enter_context(nc.psum_tensor("PS", [P, 8, 512], f32))

        ident = cst[:, CC["ident"]:CC["ident"] + P]
        ones = cst[:, CC["ones"]:CC["ones"] + P]
        blk64 = cst[:, CC["blk64"]:CC["blk64"] + P]
        tri_chunk = cst[:, CC["tri_chunk"]:CC["tri_chunk"] + P]
        tri = cst[:, CC["tri"]:CC["tri"] + P]
        strict = cst[:, CC["strict"]:CC["strict"] + P]
        causal = cst[:, CC["causal"]:CC["causal"] + P]
        iota = cst[:, CC["iota"]:CC["iota"] + P]
        eps_col, lnq_gdn, lnq_fox = (cst[:, CC["bias"] + i:CC["bias"] + i + 1] for i in range(3))
        zero_col = cst[:, CC["bias"] + 3:CC["bias"] + 4]

        def level(i):
            return cst[:, CC["level"] + i * P:CC["level"] + (i + 1) * P]

        def sel(h, rows):
            return ident[0:rows, h:h + 1].to_broadcast([rows, P])

        def pcol(name, i=0):
            return par[:, PC[name] + i:PC[name] + i + 1]

        def area(offset, *dims):
            n = int(np.prod(dims))
            assert offset + n <= ARENA, (offset, dims)
            v = arena[:, offset:offset + n]
            if len(dims) == 2:
                v = v.rearrange("p (a b) -> p a b", b=dims[1])
            elif len(dims) == 3:
                v = v.rearrange("p (a b c) -> p a b c", b=dims[1], c=dims[2])
            return v

        def along(v, n):
            a = v.shape[1]
            return v.rearrange("p (a o) -> p a o", o=1).to_broadcast([P, a, n])

        def over(v, n):
            b = v.shape[1]
            return v.rearrange("p (o b) -> p o b", o=1).to_broadcast([P, n, b])

        def heads(bank):
            return PS[:, bank, :].rearrange("p (h n) -> p h n", n=P)

        hn = area(ARENA - 3 * D, 2, D)
        junk = area(ARENA - D, D)
        RW = SEQ + CONV_K - 1
        raw = area(0, 24, RW)
        o = 24 * RW
        conv = area(o, 12, SEQ); o += 12 * SEQ
        fox_v = area(o, NT, 512); o += NT * 512
        gb = area(o, GH, SEQ); o += GH * SEQ
        qk_t = area(o, NT, 512); o += NT * 512
        qd = area(o, GH, SEQ); o += GH * SEQ
        tmp = area(o, 8, 512); o += 8 * 512
        small = area(o, NT, 16); o += NT * 16
        kbg = area(0, NT, 512)
        kd = area(NT * 512, NT, 512)
        vb = area(2 * NT * 512, NT, 512)
        A = hT[:, 0:4, :]
        Dinv = hT[:, 4:8, :]
        Einv = gb
        u_tok = conv[:, 4:8, :]
        w_T = conv[:, 8:12, :]
        o_T = kbg
        yT = hT
        state = tmp[:, 0:2, :]
        v_new = tmp[:, 2:4, :]
        row_T = area(o, SEQ); o += SEQ
        crow_T = area(o, SEQ); o += SEQ
        ss_col = stats[:, 0:14]
        rstd_col = stats[:, 14:28]
        soft = stats[:, 32:96].rearrange("p (t n) -> p t n", n=16)
        la = stats[:, 96:112]
        lf = stats[:, 112:144]
        beta = stats[:, 144:160]
        gcol = stats[:, 160:176]
        beg = stats[:, 176:192]
        esuf = stats[:, 192:208]
        ccol = stats[:, 208:240]
        glast = sb("glast", [P, GH, SEQ // CH])
        nmax = sb("nmax", [P, 32])
        rsum = sb("rsum", [P, 32])
        rinv = sb("rinv", [P, 32])
        memx = area(0, MT, D)
        memT = area(2048, DC, MEM)
        qx = area(4096, DC, SEQ)
        kx = area(8192, DC, MEM)
        vx = area(10240, MT, D)
        xtmp = area(12288, 8, 512)
        qp = area(0, 16, SEQ)
        gstage = area(8192, NEXP_HI, P)
        po = 8192 + NEXP_HI * P
        keys_sb = area(po, 16, P)
        scores = area(po + 2048, 16, P)
        rest = area(po + 4096, 4, P)
        cand = area(po + 4608, 2 * P)
        cand2 = area(po + 4864, 2 * P)
        po += 5120
        top = sb("top", [P, 16, TOPK])
        topi = sb("topi", [P, 16, TOPK], u32)
        topf = sb("topf", [P, 16, TOPK])
        best = sb("best", [P, PH, TOPK])
        besti = sb("besti", [P, PH, TOPK], u32)
        onehot = scores
        picked = area(po, 3, P)
        digitf = area(po + 3 * P, 2, P)
        digits = area(po + 5 * P, 2, P).bitcast(u32)
        u_ring = area(0, 4, DC, P)
        v_grp = area(4096, GRP, D)
        w_grp = area(4096 + GRP * D, GRP, SEQ)
        g_ring = area(4096 + GRP * D + GRP * SEQ, 4, SEQ)
        act_ring = area(4096 + GRP * D + (GRP + 4) * SEQ, 2, SEQ)

        pickT = sb("pickT", [P, 3, P])
        hotA = area(po + 7 * P, 2, 4 * P)
        hotB = area(po + 15 * P, 2, 4 * P)

        x_loaded, const_loaded, out_stored = sem("x_loaded"), sem("const_loaded"), sem("out_stored")
        par_loaded, mem_loaded, keys_loaded = sem("par_loaded"), sem("mem_loaded"), sem("keys_loaded")
        w_loaded = [sem("w_loaded0"), sem("w_loaded1")]
        w_free = [sem("w_free0"), sem("w_free1")]
        layer_left, cleared, layer_entered = sem("layer_left"), sem("cleared"), sem("layer_entered")
        local = []

        def lsem(name):
            s = sem(name)
            local.append(s)
            return s

        stage_done = lsem("stage_done")
        rstd_ready, hn_ready, transposed, gained = lsem("rstd_ready"), lsem("hn_ready"), lsem("transposed"), lsem("gained")
        pad_zeroed, proj_done, raw_stored, conv_done = lsem("pad_zeroed"), lsem("proj_done"), lsem("raw_stored"), lsem("conv_done")
        silu_done = lsem("silu_done")
        softarg, softexp, gate_cols = lsem("softarg"), lsem("softexp"), lsem("gate_cols")
        sq_ready, ss_done, rs_ready, normed = lsem("sq_ready"), lsem("ss_done"), lsem("rs_ready"), lsem("normed")
        cums_done, cums_stored, cols_ready = lsem("cums_done"), lsem("cums_stored"), lsem("cols_ready")
        gb_done, gb_stored = lsem("gb_done"), lsem("gb_stored")
        kq_done, kq_used, diff_ready, decay_ready, mask_ready = (lsem("kq_done"), lsem("kq_used"), lsem("diff_ready"),
                                                                 lsem("decay_ready"), lsem("mask_ready"))
        eg_ready, qd_ready = lsem("eg_ready"), lsem("qd_ready")
        lev_ready, lev_used, p_done, p_stored = lsem("lev_ready"), lsem("lev_used"), lsem("p_done"), lsem("p_stored")
        inv_done, inv_stored = lsem("inv_done"), lsem("inv_stored")
        uw_done, u_stored, w_stored = lsem("uw_done"), lsem("u_stored"), lsem("w_stored")
        state_zero, ws_done, vnew_ready = lsem("state_zero"), lsem("ws_done"), lsem("vnew_ready")
        chunk_done, state_ready, o_stored = lsem("chunk_done"), lsem("state_ready"), lsem("o_stored")
        att_done, max_ready, exp_ready, prob_ready = lsem("att_done"), lsem("max_ready"), lsem("exp_ready"), lsem("prob_ready")
        pt_done, pt_stored, pv_done, o_ready = lsem("pt_done"), lsem("pt_stored"), lsem("pv_done"), lsem("o_ready")
        ot_done, ot_stored = lsem("ot_done"), lsem("ot_stored")
        gemm_done, added = lsem("gemm_done"), lsem("added")
        xg_done, xg_stored = lsem("xg_done"), lsem("xg_stored")
        sc_done, sc_stored = lsem("sc_done"), lsem("sc_stored")
        gate_diff, gate_exp, picks_ready, pickT_done, pickT_stored = (lsem("gate_diff"), lsem("gate_exp"), lsem("picks_ready"),
                                                                      lsem("pickT_done"), lsem("pickT_stored"))
        hot_ready, spread_done, spread_stored = lsem("hot_ready"), lsem("spread_done"), lsem("spread_stored")
        gates_out = lsem("gates_out")
        u_loaded = [lsem(f"u_loaded{i}") for i in range(4)]
        g_loaded = [lsem(f"g_loaded{i}") for i in range(4)]
        v_loaded = lsem("v_loaded")
        u_free, g_free, v_free = lsem("u_free"), lsem("g_free"), lsem("v_free")
        act_done, gelu_done, gated = lsem("act_done"), lsem("gelu_done"), lsem("gated")
        y_done, y_added = lsem("y_done"), lsem("y_added")

        (S_NORM1, S_PROJ, S_PREP, S_GATES, S_KQ, S_INV, S_UW, S_SCAN, S_ONORM, S_FOX, S_OUT1, S_NORM2, S_XPROJ, S_XNORM,
         S_XATT, S_OUT2, S_NORM3, S_PQ, S_PICK, S_PEER) = range(20)

        def stage_end(eng, l, k):
            eng.drain().then_inc(stage_done, 1)
            eng.wait_ge(stage_done, 4 * (k + 1))

        def layer_end(eng, l):
            eng.sem_inc(layer_left, 1)
            eng.wait_ge(cleared, l + 1)
            eng.sem_inc(layer_entered, 1)

        block = ctx.enter_context(nc.Block())

        @block.sync
        def _(sp):
            sp.dma_start(X[:], x.rearrange("(t p) d -> p t d", p=P)).then_inc(x_loaded, 16)
            with nc.sync.Fori(0, DEPTH) as l:
                w_layer = weights[bass.ds(l, 1)].rearrange("l q s p n -> (l q) s p n")
                with nc.sync.Fori(0, N_PAIRS) as q:
                    for s in range(2):
                        sp.wait_ge(w_free[s], l * N_PAIRS + q + 1)
                        sp.dma_start(wring[:, s].rearrange("p c n -> p (c n)"),
                                     w_layer[bass.ds(q, 1), s].rearrange("q p n -> (q p) n")).then_inc(w_loaded[s], 16)
                for t in range(NT):
                    sp.wait_ge(spread_stored, 2 + (t + 1) * (2 * P // TOK_STEP))
                    for i in range(0, NEXP_HI, 32):
                        sp.dma_start(gates_dram[i:i + 32, :, t * P:(t + 1) * P].rearrange("i j t -> j i t"),
                                     gstage[:, i:i + 32, :]).then_inc(gates_out, 16)
                sp.wait_ge(stage_done, 4 * (S_PICK + 1))
                sp.wait_ge(gates_out, NT * 64)
                u_layer = expert_u[bass.ds(l, 1)].rearrange("l i p n -> (l i) p n")
                v_layer = expert_v[bass.ds(l, 1)].rearrange("l (i p) n -> p (l i) n", p=P)
                with nc.sync.Fori(0, NEXP_HI // GRP) as g:
                    for r in range(GRP):
                        if r == 1:
                            sp.wait_ge(v_free, g + 1)
                            sp.dma_start(v_grp[:], v_layer[:, bass.ds(g * GRP, GRP), :]).then_inc(v_loaded, 16)
                        sp.wait_ge(u_free, g * GRP + r + 1)
                        sp.dma_start(u_ring[:, r % 4].rearrange("p c n -> p (c n)"),
                                     u_layer[bass.ds(g * GRP + r, 1)].rearrange("i p n -> (i p) n")).then_inc(u_loaded[r % 4], 16)
                        sp.wait_ge(g_free, g * GRP + r + 1)
                        sp.dma_start(g_ring[:, r % 4],
                                     gates_dram[bass.ds(g * GRP + r, 1)].rearrange("i p n -> (i p) n")).then_inc(g_loaded[r % 4], 16)
                sp.wait_ge(stage_done, 4 * (S_PEER + 1))
                layer_end(sp, l)
            sp.dma_start(out.rearrange("(t p) d -> p t d", p=P), X[:]).then_inc(out_stored, 16)
            sp.wait_ge(out_stored, 16)

        @block.tensor
        def _(pe):
            mm = nc.tensor.matmul

            def weights_ready(l, q, s):
                pe.wait_ge(w_loaded[s], l * (16 * N_PAIRS) + 16 * (q + 1))

            def norm_transposes(base, tiles):
                for t in range(tiles):
                    k = base + t
                    pe.wait_ge(hn_ready, k + 1)
                    if t >= 2:
                        pe.wait_ge(gained, k - 1)
                    for c in range(DC):
                        last = nc.tensor.transpose(PS[:, 2 * (k % 2) + c // 4, (c % 4) * P:(c % 4 + 1) * P],
                                                   hn[:, k % 2, c * P:(c + 1) * P], ident)
                    last.then_inc(transposed, 1)

            def channel_tile(bank, s, m, src, n, done):
                for c in range(DC):
                    last = mm(PS[:, bank, 0:n], wring[:, s, c, m * P:(m + 1) * P], src[:, c, 0:n], start=c == 0, stop=c == DC - 1)
                last.then_inc(done, 1)
                return last

            def token_tile(bank_ap, s, src, t, cols, done):
                for c in range(DC):
                    last = mm(bank_ap, src[:, c, t * P:(t + 1) * P], wring[:, s, c, 0:cols], start=c == 0, stop=c == DC - 1)
                last.then_inc(done, 1)
                return last

            def out_projection(l, q, n0):
                for s in range(2):
                    weights_ready(l, q, s)
                    for t in range(NT):
                        token_tile(PS[:, s * NT + t, :], s, yT, t, 512, gemm_done)
                    pe.drain().then_inc(w_free[s], 1)

            def sums(base, items, src_mat, n=SEQ):
                for i, mat in enumerate(items):
                    k = base + i
                    pe.wait_ge(sq_ready, k + 1)
                    if i >= 4:
                        pe.wait_ge(rs_ready, k - 3)
                    mm(PS[:, k % 4, 0:n], mat, src_mat[:, k % 2, 0:n], start=True, stop=True).then_inc(ss_done, 1)

            pe.wait_ge(const_loaded, 16)
            for s in range(2):
                pe.sem_inc(w_free[s], 1)
            with nc.tensor.Fori(0, DEPTH) as l:
                pe.sem_inc(v_free, 1)
                pe.sem_inc(u_free, 4)
                norm_transposes(0, NT)
                stage_end(pe, l, S_NORM1)
                with nc.tensor.Fori(0, 3) as q:
                    for s in range(2):
                        weights_ready(l, q, s)
                        for m in range(4):
                            pe.wait_ge(raw_stored, q * 8 + s * 4 + m + 1)
                            channel_tile(s * 4 + m, s, m, hT, SEQ, proj_done)
                        pe.drain().then_inc(w_free[s], 1)
                weights_ready(l, PAIR_VS, 0)
                pe.wait_ge(raw_stored, 8 + 16 + 4)
                for t in range(NT):
                    token_tile(PS[:, t, :], 0, hT, t, 512, proj_done)
                pe.drain().then_inc(w_free[0], 1)
                weights_ready(l, PAIR_VS, 1)
                pe.wait_ge(raw_stored, 8 + 16 + 5)
                for t in range(NT):
                    token_tile(PS[:, 4, t * 16:(t + 1) * 16], 1, hT, t, 16, proj_done)
                pe.drain().then_inc(w_free[1], 1)
                stage_end(pe, l, S_PROJ)
                sums(0, [ones] * 8 + [blk64] * 8, tmp[:, 0:2, :])
                stage_end(pe, l, S_PREP)
                pe.wait_ge(gate_cols, 1)
                for t in range(NT):
                    la_t, lf_t = la[:, t * GH:(t + 1) * GH], lf[:, t * FH:(t + 1) * FH]
                    mm(PS[:, 0, t * GH:(t + 1) * GH], tri_chunk, la_t, start=True, stop=True)
                    mm(PS[:, 1, t * GH:(t + 1) * GH], strict, la_t, start=True, stop=True)
                    mm(PS[0:GH, 2, t * P:(t + 1) * P], la_t, tri_chunk, start=True, stop=True)
                    for e in range(t + 1):
                        lf_e = lf[:, e * FH:(e + 1) * FH]
                        mm(PS[:, 3, t * FH:(t + 1) * FH], tri if e == t else ones, lf_e, start=e == 0, stop=e == t)
                    for e in range(t + 1):
                        lf_e = lf[:, e * FH:(e + 1) * FH]
                        last = mm(PS[0:FH, 4, t * P:(t + 1) * P], lf_e, tri if e == t else ones, start=e == 0, stop=e == t)
                last.then_inc(cums_done, 1)
                pe.wait_ge(cums_stored, 1)
                for h in range(GH):
                    bank = 5 + h % 3
                    if h >= 3:
                        pe.wait_ge(gb_stored, h - 2)
                    mm(PS[:, bank, :], sel(h, GH), row_T[0:GH, :], start=True, stop=True).then_inc(gb_done, 1)
                stage_end(pe, l, S_GATES)
                for t in range(NT):
                    b = 4 * (t % 2)
                    if t >= 2:
                        pe.wait_ge(kq_used, t - 1)
                    ts = slice(t * P, (t + 1) * P)
                    for h in range(GH):
                        hs = slice(h * P, (h + 1) * P)
                        q_h, k_h, v_h = conv[:, h, ts], conv[:, 4 + h, ts], conv[:, 8 + h, ts]
                        mm(PS[:, b, hs], k_h, k_h, start=True, stop=True)
                        mm(PS[:, b + 1, hs], k_h, q_h, start=True, stop=True)
                        nc.tensor.transpose(PS[:, b + 2, hs], k_h, ident)
                        last = nc.tensor.transpose(PS[:, b + 3, hs], v_h, ident)
                    last.then_inc(kq_done, 1)
                stage_end(pe, l, S_KQ)
                def first_level(t):
                    pe.wait_ge(lev_ready, t + 1)
                    if t >= 2:
                        pe.wait_ge(inv_stored, t - 1)
                    for h in range(GH):
                        last = nc.tensor.transpose(PS[:, 2 + t % 2, h * P:(h + 1) * P], tmp[:, t % 2, h * P:(h + 1) * P], ident)
                    last.then_inc(inv_done, 1)

                def level_product(k):
                    t = k % 4
                    pe.wait_ge(lev_ready, k + 1)
                    pe.wait_ge(inv_stored, k - 3)
                    if k >= 6:
                        pe.wait_ge(p_stored, k - 5)
                    for h in range(GH):
                        hs = slice(h * P, (h + 1) * P)
                        last = mm(PS[:, k % 2, hs], tmp[:, k % 2, hs], Einv[:, t, hs], start=True, stop=True)
                    last.then_inc(p_done, 1)

                for t in range(NT):
                    first_level(t)
                level_product(4)
                for k in range(4, 4 * LEVELS):
                    t = k % 4
                    if k + 1 < 4 * LEVELS:
                        level_product(k + 1)
                    pe.wait_ge(p_stored, k - 3)
                    pe.wait_ge(inv_stored, k - 1)
                    for h in range(GH):
                        hs = slice(h * P, (h + 1) * P)
                        last = mm(PS[:, 2 + k % 2, hs], Dinv[:, t, hs], tmp[:, 2 + k % 2, hs], start=True, stop=True)
                    if k < 4 * (LEVELS - 1):
                        for h in range(GH):
                            hs = slice(h * P, (h + 1) * P)
                            last = mm(PS[:, 4 + k % 2, hs], tmp[:, 2 + k % 2, hs], Dinv[:, t, hs], start=True, stop=True)
                    last.then_inc(inv_done, 1)
                stage_end(pe, l, S_INV)
                for t in range(NT):
                    for h in range(GH):
                        hs = slice(h * P, (h + 1) * P)
                        mm(PS[:, t, hs], Einv[:, t, hs], vb[:, t, hs], start=True, stop=True)
                        last = mm(PS[:, 4 + t, hs], kbg[:, t, hs], Einv[:, t, hs], start=True, stop=True)
                    last.then_inc(uw_done, 1)
                stage_end(pe, l, S_UW)
                for n in range(SEQ // CH):
                    t, r0 = n // 2, (n % 2) * CH
                    rows = slice(r0, r0 + CH)
                    cur = state[:, n % 2, :]
                    pe.wait_ge(state_ready, n + 1)
                    if n >= 2:
                        pe.wait_ge(o_stored, n - 1)
                    for h in range(GH):
                        hs = slice(h * P, (h + 1) * P)
                        last = mm(PS[:, n % 2, hs], w_T[:, h, t * P:(t + 1) * P], cur[:, hs], start=True, stop=True)
                    last.then_inc(ws_done, 1)
                    pe.wait_ge(vnew_ready, n + 1)
                    for h in range(GH):
                        hs = slice(h * P, (h + 1) * P)
                        last = mm(PS[:, 2 + n % 2, hs], kd[rows, t, hs], v_new[rows, n % 2, hs], start=True, stop=True)
                    last.then_inc(chunk_done, 1)
                    for h in range(GH):
                        hs = slice(h * P, (h + 1) * P)
                        oc = PS[:, 4 + n % 2, h * CH:(h + 1) * CH]
                        mm(oc, cur[:, hs], qd[:, h, n * CH:(n + 1) * CH], start=True, stop=False)
                        last = mm(oc, v_new[rows, n % 2, hs], qk_t[rows, t, h * P + r0:h * P + r0 + CH], start=False, stop=True)
                    last.then_inc(chunk_done, 1)
                stage_end(pe, l, S_SCAN)
                sums(16, [ones] * 4, tmp[:, 0:2, :])
                stage_end(pe, l, S_ONORM)
                def fox_scores(i):
                    t, h = i // FH, i % FH
                    rows = slice((h % 2) * FD, (h % 2) * FD + FD)
                    n = (t + 1) * P
                    if i >= 2:
                        pe.wait_ge(max_ready, i - 1)
                    mm(PS[:, i % 2, 0:n], raw[rows, 16 + h // 2, 3 + t * P:3 + (t + 1) * P],
                       raw[rows, 20 + h // 2, 3:3 + n], start=True, stop=False)
                    mm(PS[:, i % 2, 0:n], sel(h, FH), crow_T[0:FH, 0:n], start=False, stop=True).then_inc(att_done, 1)

                fox_scores(0)
                for i in range(NT * FH):
                    t, h = i // FH, i % FH
                    if i + 1 < NT * FH:
                        fox_scores(i + 1)
                    pe.wait_ge(exp_ready, i + 1)
                    if i >= 2:
                        pe.wait_ge(pt_stored, i - 1)
                    for j in range(t + 1):
                        last = nc.tensor.transpose(PS[:, 2 + i % 2, j * P:(j + 1) * P], tmp[:, i % 2, j * P:(j + 1) * P], ident)
                    last.then_inc(pt_done, 1)
                    pe.wait_ge(pt_stored, i + 1)
                    if h == 0 and t >= 2:
                        pe.wait_ge(o_ready, t - 1)
                    for j in range(t + 1):
                        last = mm(PS[:, 4 + t % 2, h * FD:(h + 1) * FD], tmp[:, 2 + i % 2, j * P:(j + 1) * P],
                                  fox_v[:, j, h * FD:(h + 1) * FD], start=j == 0, stop=j == t)
                    last.then_inc(pv_done, 1)
                    if h == FH - 1:
                        pe.wait_ge(o_ready, t + 1)
                        if t >= 2:
                            pe.wait_ge(ot_stored, t - 1)
                        for c in range(4):
                            last = nc.tensor.transpose(PS[:, 6 + t % 2, c * P:(c + 1) * P], tmp[:, 4 + t % 2, c * P:(c + 1) * P], ident)
                        last.then_inc(ot_done, 1)
                stage_end(pe, l, S_FOX)
                out_projection(l, PAIR_OUT, 0)
                stage_end(pe, l, S_OUT1)
                norm_transposes(NT, NT)
                norm_transposes(2 * NT, MT)
                stage_end(pe, l, S_NORM2)
                for s in range(2):
                    weights_ready(l, PAIR_MQ, s)
                    for m in range(4):
                        channel_tile(s * 4 + m, s, m, hT, SEQ, xg_done)
                    pe.drain().then_inc(w_free[s], 1)
                for s in range(2):
                    weights_ready(l, PAIR_MK, s)
                    for m in range(4):
                        pe.wait_ge(xg_stored, s * 4 + m + 1)
                        channel_tile(s * 4 + m, s, m, memT, MEM, xg_done)
                    pe.drain().then_inc(w_free[s], 1)
                for s in range(2):
                    weights_ready(l, PAIR_MV, s)
                    for m in range(MT):
                        pe.wait_ge(xg_stored, 8 + s * 2 + m + 1)
                        token_tile(PS[:, s * 2 + m, :], s, memT, m, 512, xg_done)
                    pe.drain().then_inc(w_free[s], 1)
                stage_end(pe, l, S_XPROJ)
                for i in range(2 * MH):
                    n = SEQ if i < MH else MEM
                    k = 20 + i
                    pe.wait_ge(sq_ready, k + 1)
                    if i >= 4:
                        pe.wait_ge(rs_ready, k - 3)
                    for e in range(2):
                        last = mm(PS[:, k % 4, 0:n], ones, xtmp[:, 2 * (k % 2) + e, 0:n], start=e == 0, stop=e == 1)
                    last.then_inc(ss_done, 1)
                stage_end(pe, l, S_XNORM)

                FI = NT * FH

                def mem_scores(i):
                    t, h = i // MH, i % MH
                    if i >= 2:
                        pe.wait_ge(exp_ready, FI + i - 1)
                    for e in range(2):
                        last = mm(PS[:, i % 2, 0:MEM], qx[:, 2 * h + e, t * P:(t + 1) * P], kx[:, 2 * h + e, :], start=e == 0, stop=e == 1)
                    last.then_inc(att_done, 1)

                mem_scores(0)
                for i in range(NT * MH):
                    t, h = i // MH, i % MH
                    if i + 1 < NT * MH:
                        mem_scores(i + 1)
                    pe.wait_ge(prob_ready, i + 1)
                    if i >= 2:
                        pe.wait_ge(pt_stored, FI + i - 1)
                    for j in range(MT):
                        last = nc.tensor.transpose(PS[:, 2 + i % 2, j * P:(j + 1) * P], xtmp[:, i % 2, j * P:(j + 1) * P], ident)
                    last.then_inc(pt_done, 1)
                    pe.wait_ge(pt_stored, FI + i + 1)
                    if i >= 2:
                        pe.wait_ge(ot_stored, NT + i - 1)
                    for e in range(2):
                        for j in range(MT):
                            last = mm(PS[:, 4 + i % 2, e * P:(e + 1) * P], vx[:, j, (2 * h + e) * P:(2 * h + e + 1) * P],
                                      xtmp[:, 2 + i % 2, j * P:(j + 1) * P], start=j == 0, stop=j == MT - 1)
                    last.then_inc(ot_done, 1)
                stage_end(pe, l, S_XATT)
                out_projection(l, PAIR_MO, 8)
                stage_end(pe, l, S_OUT2)
                norm_transposes(2 * NT + MT, NT)
                stage_end(pe, l, S_NORM3)
                for q in range(2):
                    for s in range(2):
                        weights_ready(l, PAIR_PQ + q, s)
                        for m in range(4):
                            if q:
                                pe.wait_ge(xg_stored, 20 + s * 4 + m + 1)
                            channel_tile(s * 4 + m, s, m, hT, SEQ, xg_done)
                        pe.drain().then_inc(w_free[s], 1)
                stage_end(pe, l, S_PQ)
                for t in range(NT):
                    if t == 0:
                        pe.wait_ge(keys_loaded, l * 16 + 16)
                    for k in range(16):
                        last = mm(PS[:, k // 4, (k % 4) * P:(k % 4 + 1) * P], qp[:, k, t * P:(t + 1) * P], keys_sb[:, k, :], start=True, stop=True)
                    last.then_inc(sc_done, 1)
                    pe.wait_ge(picks_ready, t + 1)
                    for k in range(3):
                        last = nc.tensor.transpose(PS[:, 4, k * P:(k + 1) * P], picked[:, k, :], ident)
                    last.then_inc(pickT_done, 1)
                    with nc.tensor.Fori(0, P // TOK_STEP) as j:
                        for half in range(2):
                            n = t * (2 * P // TOK_STEP)
                            pe.wait_ge(hot_ready, n + j * 2 + half + 1)
                            pe.wait_ge(spread_stored, n + j * 2 + half + 1)
                            for e in range(4):
                                es = slice(e * P, (e + 1) * P)
                                last = mm(PS[:, 5 + half, es], hotB[:, half, es], hotA[:, half, es], start=True, stop=True)
                            last.then_inc(spread_done, 1)
                    pe.wait_ge(sc_stored, t + 1)
                stage_end(pe, l, S_PICK)
                with nc.tensor.Fori(0, NEXP_HI // GRP) as g:
                    for r in range(GRP):
                        pe.wait_ge(u_loaded[r % 4], g * 32 + 16 * (r // 4) + 16)
                        pe.wait_ge(gelu_done, g * GRP + r + 1)
                        for c in range(DC):
                            last = mm(PS[:, r % 2, :], u_ring[:, r % 4, c, :], hT[:, c, :], start=c == 0, stop=c == DC - 1)
                        last.then_inc(act_done, 1)
                        pe.drain().then_inc(u_free, 1)
                    pe.wait_ge(v_loaded, g * 16 + 16)
                    for i in range(2 * NT):
                        t, half = i // 2, i % 2
                        pe.wait_ge(y_added, g * 8 + i + 1)
                        for r in range(GRP):
                            if i == 0:
                                pe.wait_ge(gated, g * GRP + r + 1)
                            last = mm(PS[:, 2 + i % 2, :], w_grp[:, r, t * P:(t + 1) * P], v_grp[:, r, half * 512:(half + 1) * 512],
                                      start=r == 0, stop=r == GRP - 1)
                        last.then_inc(y_done, 1)
                    pe.drain().then_inc(v_free, 1)
                stage_end(pe, l, S_PEER)
                layer_end(pe, l)

        @block.scalar
        def _(act):
            fn = nc.scalar.activation

            def rstd(base, src, tiles):
                for t in range(tiles):
                    k = base + t
                    fn(junk, src[:, t, :], ACT.Square, accum_out=ss_col[:, k:k + 1])
                    act.drain()
                    fn(rstd_col[:, k:k + 1], ss_col[:, k:k + 1], ACT.Ln, bias=eps_col, scale=1.0 / D)
                    act.drain()
                    fn(rstd_col[:, k:k + 1], rstd_col[:, k:k + 1], ACT.Exp, bias=zero_col, scale=-0.5).then_inc(rstd_ready, 1)

            def inv_norms(base, specs, dst, n=SEQ):
                for i, (scale, bias) in enumerate(specs):
                    k = base + i
                    act.wait_ge(ss_done, k + 1)
                    if i >= 2:
                        act.wait_ge(normed, k - 1)
                    fn(dst[:, k % 2, 0:n], PS[:, k % 4, 0:n], ACT.Ln, bias=eps_col, scale=scale)
                    act.drain()
                    fn(dst[:, k % 2, 0:n], dst[:, k % 2, 0:n], ACT.Exp, bias=bias, scale=-0.5).then_inc(rs_ready, 1)

            act.dma_start(cst[:], consts).then_inc(const_loaded, 16)
            act.wait_ge(const_loaded, 16)
            act.wait_ge(x_loaded, 16)
            with nc.scalar.Fori(0, DEPTH) as l:
                act.dma_start(par[:], params[bass.ds(l, 1)].rearrange("l p n -> (l p) n")).then_inc(par_loaded, 16)
                act.wait_ge(par_loaded, l * 16 + 16)
                act.sem_inc(raw_stored, 8)
                act.sem_inc(gelu_done, 2)
                act.sem_inc(spread_stored, 2)
                rstd(0, X, NT)
                stage_end(act, l, S_NORM1)
                with nc.scalar.Fori(0, 3) as q:
                    for b in range(8):
                        act.wait_ge(proj_done, q * 8 + b + 1)
                        fn(raw[:, bass.ds(q * 8 + b, 1), 3:RW].rearrange("p o n -> p (o n)"), PS[:, b, :], ACT.Copy).then_inc(raw_stored, 1)
                for t in range(NT):
                    act.wait_ge(proj_done, 24 + t + 1)
                    fn(fox_v[:, t, :], PS[:, t, :], ACT.Copy)
                act.wait_ge(proj_done, 24 + 2 * NT)
                fn(small.rearrange("p t n -> p (t n)"), PS[:, 4, 0:NT * 16], ACT.Copy)
                fn(raw[:, 12:16, 3:RW], raw[:, 12:16, 3:RW], ACT.Silu)
                for k in range(3):
                    act.wait_ge(conv_done, 4 * (k + 1))
                    fn(conv[:, 4 * k:4 * (k + 1), :], conv[:, 4 * k:4 * (k + 1), :], ACT.Silu)
                stage_end(act, l, S_PROJ)
                act.wait_ge(softarg, 1)
                fn(soft[:, :, :], soft[:, :, :], ACT.Exp, bias=zero_col, scale=-1.0)
                act.drain()
                fn(soft[:, :, 0:4], soft[:, :, 0:4], ACT.Ln, bias=1.0)
                fn(soft[:, :, 8:16], soft[:, :, 8:16], ACT.Ln, bias=1.0)
                fn(nmax[:, 0:GH], par[:, PC["a_log"]:PC["a_log"] + GH], ACT.Exp)
                act.drain().then_inc(softexp, 1)
                inv_norms(0, [(1.0, lnq_gdn)] * 4 + [(1.0, zero_col)] * 4 + [(1.0 / FD, lnq_fox)] * 4 + [(1.0 / FD, zero_col)] * 4,
                          tmp[:, 2:4, :])
                stage_end(act, l, S_PREP)
                act.wait_ge(cums_done, 1)
                fn(row_T[0:GH, :], PS[0:GH, 2, :], ACT.Copy)
                fn(crow_T[0:FH, :], PS[0:FH, 4, :], ACT.Copy, scale=-1.0)
                act.drain().then_inc(cums_stored, 1)
                fn(beg, PS[:, 0, 0:16], ACT.Exp)
                fn(esuf, PS[:, 1, 0:16], ACT.Exp)
                fn(gcol, PS[:, 0, 0:16], ACT.Copy)
                fn(ccol, PS[:, 3, 0:32], ACT.Copy)
                act.drain().then_inc(cols_ready, 1)
                for h in range(GH):
                    act.wait_ge(gb_done, h + 1)
                    fn(gb[:, h, :], PS[:, 5 + h % 3, :], ACT.Copy)
                    fn(tmp[:, h % 2 + 0, :], PS[:, 5 + h % 3, :], ACT.Exp) if False else None
                    act.drain().then_inc(gb_stored, 1)
                fn(glast[:, :, :], gb[:, :, CH - 1:SEQ:CH], ACT.Exp)
                stage_end(act, l, S_GATES)
                for t in range(NT):
                    act.wait_ge(diff_ready, t + 1)
                    fn(tmp[:, 0, :], tmp[:, 0, :], ACT.Exp, bias=zero_col, scale=-1.0)
                    fn(tmp[:, 1, :], tmp[:, 1, :], ACT.Exp)
                    act.drain().then_inc(decay_ready, 1)
                for h in range(GH):
                    if h >= 2:
                        act.wait_ge(qd_ready, h - 1)
                    fn(tmp[:, 6 + h % 2, :], gb[:, h, :], ACT.Exp).then_inc(eg_ready, 1)
                stage_end(act, l, S_KQ)
                for k in range(4, 4 * LEVELS):
                    act.wait_ge(p_done, k - 3)
                    if k >= 6:
                        act.wait_ge(inv_done, k - 1)
                    fn(tmp[:, 2 + k % 2, :], PS[:, k % 2, :], ACT.Copy).then_inc(p_stored, 1)
                stage_end(act, l, S_INV)
                for t in range(NT):
                    act.wait_ge(uw_done, t + 1)
                    fn(u_tok[:, t, :], PS[:, t, :], ACT.Copy)
                stage_end(act, l, S_UW)
                for n in range(SEQ // CH):
                    act.wait_ge(chunk_done, 2 * n + 2)
                    fn(o_T.rearrange("p h n -> p h n")[:, :, n * CH:(n + 1) * CH],
                       PS[:, 4 + n % 2, 0:GH * CH].rearrange("p (h n) -> p h n", n=CH), ACT.Copy).then_inc(o_stored, 1)
                stage_end(act, l, S_SCAN)
                inv_norms(16, [(1.0 / P, zero_col)] * 4, tmp[:, 2:4, :])
                stage_end(act, l, S_ONORM)
                for i in range(NT * FH):
                    t, h = i // FH, i % FH
                    n = (t + 1) * P
                    act.wait_ge(max_ready, i + 1)
                    fn(tmp[:, i % 2, 0:n], tmp[:, 6 + i % 2, 0:n], ACT.Exp, bias=nmax[:, i:i + 1],
                       accum_out=rsum[:, i:i + 1]).then_inc(exp_ready, 1)
                    act.wait_ge(pt_done, i + 1)
                    fn(tmp[:, 2 + i % 2, 0:n], PS[:, 2 + i % 2, 0:n], ACT.Copy).then_inc(pt_stored, 1)
                    if h == FH - 1:
                        act.wait_ge(ot_done, t + 1)
                        fn(yT[:, 4:8, t * P:(t + 1) * P], heads(6 + t % 2), ACT.Copy).then_inc(ot_stored, 1)
                stage_end(act, l, S_FOX)
                stage_end(act, l, S_OUT1)
                rstd(NT, X, NT)
                act.wait_ge(mem_loaded, l * 16 + 16)
                rstd(2 * NT, memx, MT)
                stage_end(act, l, S_NORM2)
                for b in range(8):
                    act.wait_ge(xg_done, b + 1)
                    fn(qx[:, b, :], PS[:, b, :], ACT.Copy).then_inc(xg_stored, 1)
                for b in range(8):
                    act.wait_ge(xg_done, 8 + b + 1)
                    fn(kx[:, b, :], PS[:, b, 0:MEM], ACT.Copy).then_inc(xg_stored, 1)
                for b in range(4):
                    act.wait_ge(xg_done, 16 + b + 1)
                    fn(vx[:, b % 2, (b // 2) * 512:(b // 2 + 1) * 512], PS[:, b, :], ACT.Copy).then_inc(xg_stored, 1)
                stage_end(act, l, S_XPROJ)
                for i in range(2 * MH):
                    n = SEQ if i < MH else MEM
                    k = 20 + i
                    act.wait_ge(ss_done, k + 1)
                    if i >= 2:
                        act.wait_ge(normed, k - 1)
                    fn(xtmp[:, 4 + k % 2, 0:n], PS[:, k % 4, 0:n], ACT.Ln, bias=eps_col, scale=1.0 / (2 * P))
                    act.drain()
                    fn(xtmp[:, 4 + k % 2, 0:n], xtmp[:, 4 + k % 2, 0:n], ACT.Exp, bias=zero_col, scale=-0.5).then_inc(rs_ready, 1)
                stage_end(act, l, S_XNORM)
                FI = NT * FH
                for i in range(NT * MH):
                    t, h = i // MH, i % MH
                    act.wait_ge(max_ready, FI + i + 1)
                    if i >= 2:
                        act.wait_ge(pt_done, FI + i - 1)
                    fn(xtmp[:, i % 2, 0:MEM], PS[:, i % 2, 0:MEM], ACT.Exp, bias=nmax[:, i:i + 1], scale=(2 * P) ** -0.5,
                       accum_out=rsum[:, i:i + 1]).then_inc(exp_ready, 1)
                    act.wait_ge(pt_done, FI + i + 1)
                    fn(xtmp[:, 2 + i % 2, 0:MEM], PS[:, 2 + i % 2, 0:MEM], ACT.Copy).then_inc(pt_stored, 1)
                    act.wait_ge(ot_done, NT + i + 1)
                    fn(yT[:, 2 * h:2 * h + 2, t * P:(t + 1) * P], PS[:, 4 + i % 2, 0:MEM].rearrange("p (e n) -> p e n", n=P),
                       ACT.Copy).then_inc(ot_stored, 1)
                stage_end(act, l, S_XATT)
                stage_end(act, l, S_OUT2)
                rstd(2 * NT + MT, X, NT)
                stage_end(act, l, S_NORM3)
                for b in range(16):
                    act.wait_ge(xg_done, 20 + b + 1)
                    fn(qp[:, b, :], PS[:, b % 8, :], ACT.Copy).then_inc(xg_stored, 1)
                stage_end(act, l, S_PQ)
                for t in range(NT):
                    act.wait_ge(sc_done, t + 1)
                    fn(scores[:, :, :].rearrange("p k n -> p (k n)"), PS[:, 0:4, :].rearrange("p b n -> p (b n)"), ACT.Copy).then_inc(sc_stored, 1)
                    act.wait_ge(gate_diff, t + 1)
                    fn(picked[:, 2, :], picked[:, 2, :], ACT.Exp).then_inc(gate_exp, 1)
                    act.wait_ge(pickT_done, t + 1)
                    fn(pickT[:, :, :].rearrange("p k n -> p (k n)"), PS[:, 4, 0:3 * P], ACT.Copy).then_inc(pickT_stored, 1)
                    if t:
                        act.wait_ge(gates_out, 64 * t)
                    with nc.scalar.Fori(0, P // TOK_STEP) as j:
                        for half in range(2):
                            n = t * (2 * P // TOK_STEP)
                            act.wait_ge(spread_done, n + j * 2 + half + 1)
                            fn(gstage[:, :, bass.ds(j * TOK_STEP + half * 4, 4)],
                               PS[:, 5 + half, :].rearrange("p (e i) -> p i e", i=P), ACT.Copy).then_inc(spread_stored, 1)
                stage_end(act, l, S_PICK)
                with nc.scalar.Fori(0, NEXP_HI // GRP) as g:
                    for r in range(GRP):
                        act.wait_ge(act_done, g * GRP + r + 1)
                        act.wait_ge(gated, g * GRP + r - 1) if False else None
                        act.wait_ge(g_free, g * GRP + r + 3)
                        fn(act_ring[:, r % 2, :], PS[:, r % 2, :], ACT.Gelu_apprx_tanh).then_inc(gelu_done, 1)
                stage_end(act, l, S_PEER)
                layer_end(act, l)

        @block.vector
        def _(dve):
            v = nc.vector

            def norm(base, src, tiles, gain, dst):
                def evacuate(t):
                    k = base + t
                    dve.wait_ge(transposed, k + 1)
                    for half in range(2):
                        last = v.tensor_tensor(dst[:, 4 * half:4 * half + 4, t * P:(t + 1) * P], heads(2 * (k % 2) + half),
                                               along(par[:, PC[gain] + 4 * half:PC[gain] + 4 * half + 4], P), ALU.mult)
                    last.then_inc(gained, 1)

                for t in range(tiles):
                    k = base + t
                    dve.wait_ge(rstd_ready, k + 1)
                    if k >= 2:
                        dve.wait_ge(transposed, k - 1)
                    v.tensor_scalar(hn[:, k % 2, :], src[:, t, :], rstd_col[:, k:k + 1], None, ALU.mult).then_inc(hn_ready, 1)
                    if t:
                        evacuate(t - 1)
                evacuate(tiles - 1)

            def add_residual(base):
                for s in range(2):
                    for t in range(NT):
                        dve.wait_ge(gemm_done, base + s * NT + t + 1)
                        xs = X[:, t, s * 512:(s + 1) * 512]
                        v.tensor_tensor(xs, PS[:, s * NT + t, :], xs, ALU.add)

            def norm_items(base, items, apply, buf):
                n = len(items)

                def square(i):
                    k = base + i
                    if i >= 2:
                        dve.wait_ge(ss_done, k - 1)
                    v.tensor_tensor(buf[:, k % 2, :], items[i], items[i], ALU.mult).then_inc(sq_ready, 1)

                square(0)
                for i in range(n):
                    if i + 1 < n:
                        square(i + 1)
                    dve.wait_ge(rs_ready, base + i + 1)
                    apply(i, base + i)

            dve.wait_ge(const_loaded, 16)
            dve.wait_ge(x_loaded, 16)
            with nc.vector.Fori(0, DEPTH) as l:
                dve.wait_ge(par_loaded, l * 16 + 16)
                dve.sem_inc(y_added, 2)
                dve.sem_inc(g_free, 4)
                norm(0, X, NT, "mix", hT)
                stage_end(dve, l, S_NORM1)
                dve.wait_ge(pad_zeroed, 1)
                with v.Fori(0, 12) as m:
                    dve.wait_ge(raw_stored, m + 9)
                    row = raw[:, bass.ds(m, 1), :].rearrange("p o n -> p (o n)")
                    dst = conv[:, bass.ds(m, 1), :].rearrange("p o n -> p (o n)")

                    def tap(j):
                        return par[:, bass.ds(m * CONV_K + PC["conv"] + j, 1)]

                    v.tensor_scalar(dst, row[:, 0:SEQ], tap(0), None, ALU.mult)
                    for j in range(1, CONV_K):
                        dve.drain()
                        last = v.scalar_tensor_tensor(dst, row[:, j:j + SEQ], tap(j), dst, ALU.mult, ALU.add)
                    last.then_inc(conv_done, 1)
                stage_end(dve, l, S_PROJ)
                dtb = over(par[:, PC["dt"]:PC["dt"] + GH], NT)
                fbb = over(par[:, PC["f_bias"]:PC["f_bias"] + FH], NT)
                v.tensor_tensor(small[:, :, 0:4], small[:, :, 0:4], dtb, ALU.add)
                v.tensor_tensor(small[:, :, 8:16], small[:, :, 8:16], fbb, ALU.add)
                dve.drain()
                v.tensor_scalar(small[:, :, 8:16], small[:, :, 8:16], -1.0, None, ALU.mult)
                dve.drain()
                v.scalar_tensor_tensor(soft[:, :, 0:4], small[:, :, 0:4], -1.0, small[:, :, 0:4], ALU.mult, ALU.max)
                v.scalar_tensor_tensor(soft[:, :, 8:16], small[:, :, 8:16], -1.0, small[:, :, 8:16], ALU.mult, ALU.max)
                v.tensor_copy(soft[:, :, 4:8], small[:, :, 4:8])
                dve.drain().then_inc(softarg, 1)
                dve.wait_ge(softexp, 1)
                v.tensor_scalar(small[:, :, 0:4], small[:, :, 0:4], 0.0, None, ALU.max)
                v.tensor_scalar(small[:, :, 8:16], small[:, :, 8:16], 0.0, None, ALU.max)
                v.tensor_scalar(soft[:, :, 4:8], soft[:, :, 4:8], 1.0, None, ALU.add)
                dve.drain()
                v.tensor_tensor(small[:, :, 0:4], small[:, :, 0:4], soft[:, :, 0:4], ALU.add)
                v.tensor_tensor(small[:, :, 8:16], small[:, :, 8:16], soft[:, :, 8:16], ALU.add)
                v.reciprocal(beta.rearrange("p (t h) -> p t h", h=GH), soft[:, :, 4:8])
                dve.drain()
                v.tensor_tensor(small[:, :, 0:4], small[:, :, 0:4], over(nmax[:, 0:GH], NT), ALU.mult)
                v.tensor_scalar(lf.rearrange("p (t h) -> p t h", h=FH), small[:, :, 8:16], -1.0, None, ALU.mult)
                dve.drain()
                v.tensor_scalar(la.rearrange("p (t h) -> p t h", h=GH), small[:, :, 0:4], -1.0, None, ALU.mult)
                dve.drain().then_inc(gate_cols, 1)
                qk_items = [conv[:, i, :] for i in range(8)] + [raw[:, 16 + i, 3:RW] for i in range(8)]

                def apply_qk(i, k):
                    x_i = qk_items[i]
                    rs = tmp[:, 2 + k % 2, :]
                    if i < 8:
                        v.tensor_tensor(x_i, x_i, rs, ALU.mult).then_inc(normed, 1)
                    else:
                        v.scalar_tensor_tensor(x_i, x_i, pcol("fox_q" if i < 12 else "fox_k"), rs, ALU.mult, ALU.mult).then_inc(normed, 1)

                norm_items(0, qk_items, apply_qk, tmp[:, 0:2, :])
                stage_end(dve, l, S_PREP)
                dve.wait_ge(cols_ready, 1)
                v.tensor_tensor(beg, beg, beta, ALU.mult)
                stage_end(dve, l, S_GATES)
                for t in range(NT):
                    b = 4 * (t % 2)
                    dve.wait_ge(kq_done, t + 1)
                    cols = slice(t * GH, (t + 1) * GH)

                    def grid(a):
                        return a[:, t, :].rearrange("p (h n) -> p h n", n=P)

                    v.tensor_tensor(grid(kbg), heads(b + 2), along(beg[:, cols], P), ALU.mult)
                    v.tensor_tensor(grid(kd), heads(b + 2), along(esuf[:, cols], P), ALU.mult)
                    v.tensor_tensor(grid(vb), heads(b + 3), along(beta[:, cols], P), ALU.mult)
                    dve.wait_ge(mask_ready, t + 1)
                    v.tensor_tensor(A[:, t, :], PS[:, b, :], tmp[:, 2, :], ALU.mult)
                    v.tensor_tensor(qk_t[:, t, :], PS[:, b + 1, :], tmp[:, 3, :], ALU.mult)
                    dve.drain().then_inc(kq_used, 1)
                stage_end(dve, l, S_KQ)

                def grid_t(a, t):
                    return a[:, t, :].rearrange("p (h n) -> p h n", n=P)

                for t in range(NT):
                    dve.wait_ge(lev_ready, t + 1)
                    v.tensor_tensor(grid_t(Dinv, t), over(ident, GH), grid_t(tmp, t % 2), ALU.subtract)
                    dve.wait_ge(inv_done, t + 1)
                    v.tensor_tensor(grid_t(Einv, t), over(ident, GH), heads(2 + t % 2), ALU.subtract)
                    dve.drain().then_inc(inv_stored, 1)
                for k in range(4, 4 * LEVELS):
                    t = k % 4
                    dve.wait_ge(inv_done, k + 1)
                    v.tensor_tensor(Einv[:, t, :], Einv[:, t, :], PS[:, 2 + k % 2, :], ALU.subtract)
                    if k < 4 * (LEVELS - 1):
                        v.tensor_tensor(Dinv[:, t, :], Dinv[:, t, :], PS[:, 4 + k % 2, :], ALU.subtract)
                    dve.drain().then_inc(inv_stored, 1)
                stage_end(dve, l, S_INV)
                for t in range(NT):
                    dve.wait_ge(uw_done, t + 1)
                    v.tensor_copy(w_T[:, :, t * P:(t + 1) * P], heads(4 + t))
                v.memset(state[:, 0, :], 0.0)
                dve.drain().then_inc(state_ready, 1)
                stage_end(dve, l, S_UW)
                for n in range(SEQ // CH):
                    t, r0 = n // 2, (n % 2) * CH
                    rows = slice(r0, r0 + CH)
                    dve.wait_ge(ws_done, n + 1)
                    v.tensor_tensor(v_new[rows, n % 2, :], u_tok[rows, t, :], PS[rows, n % 2, :], ALU.subtract).then_inc(vnew_ready, 1)
                    dve.wait_ge(chunk_done, 2 * n + 1)
                    if n:
                        dve.wait_ge(chunk_done, 2 * n)
                    for h in range(GH):
                        hs = slice(h * P, (h + 1) * P)
                        last = v.scalar_tensor_tensor(state[:, (n + 1) % 2, hs], state[:, n % 2, hs], glast[:, h, n:n + 1],
                                                      PS[:, 2 + n % 2, hs], ALU.mult, ALU.add)
                    dve.drain().then_inc(state_ready, 1)
                stage_end(dve, l, S_SCAN)

                def apply_o(i, k):
                    v.scalar_tensor_tensor(yT[:, i, :], o_T[:, i, :], pcol("gdn_out"), tmp[:, 2 + k % 2, :], ALU.mult, ALU.mult)
                    dve.drain()
                    v.tensor_tensor(yT[:, i, :], yT[:, i, :], raw[:, 12 + i, 3:RW], ALU.mult).then_inc(normed, 1)

                norm_items(16, [o_T[:, i, :] for i in range(4)], apply_o, tmp[:, 0:2, :])
                stage_end(dve, l, S_ONORM)

                def fox_close(t):
                    v.reciprocal(rinv[:, t * FH:(t + 1) * FH], rsum[:, t * FH:(t + 1) * FH])
                    dve.drain()
                    dve.wait_ge(pv_done, (t + 1) * FH)
                    if t >= 2:
                        dve.wait_ge(ot_done, t - 1)
                    v.tensor_tensor(tmp[:, 4 + t % 2, :].rearrange("p (h n) -> p h n", n=FD),
                                    PS[:, 4 + t % 2, :].rearrange("p (h n) -> p h n", n=FD),
                                    along(rinv[:, t * FH:(t + 1) * FH], FD), ALU.mult).then_inc(o_ready, 1)

                for i in range(NT * FH):
                    t, h = i // FH, i % FH
                    n = (t + 1) * P
                    s_i = tmp[:, 6 + i % 2, :]
                    dve.wait_ge(att_done, i + 1)
                    if i >= 2:
                        dve.wait_ge(exp_ready, i - 1)
                    v.tensor_scalar(s_i[:, 0:n], PS[:, i % 2, 0:n], ccol[:, i:i + 1], None, ALU.add)
                    dve.drain()
                    v.tensor_tensor(s_i[:, n - P:n], s_i[:, n - P:n], causal, ALU.add)
                    dve.drain()
                    v.tensor_reduce(nmax[:, i:i + 1], s_i[:, 0:n], AX.X, ALU.max, negate=True).then_inc(max_ready, 1)
                    if h == FH - 1:
                        dve.wait_ge(exp_ready, i + 1)
                        fox_close(t)
                stage_end(dve, l, S_FOX)
                add_residual(0)
                stage_end(dve, l, S_OUT1)
                norm(NT, X, NT, "xattn", hT)
                norm(2 * NT, memx, MT, "mem", memT)
                stage_end(dve, l, S_NORM2)
                stage_end(dve, l, S_XPROJ)

                def x_square(i):
                    k = 20 + i
                    src = (qx if i < MH else kx)[:, 2 * (i % MH):2 * (i % MH) + 2, :]
                    n = SEQ if i < MH else MEM
                    if i >= 2:
                        dve.wait_ge(ss_done, k - 1)
                    v.tensor_tensor(xtmp[:, 2 * (k % 2):2 * (k % 2) + 2, 0:n], src, src, ALU.mult).then_inc(sq_ready, 1)

                x_square(0)
                for i in range(2 * MH):
                    k = 20 + i
                    n = SEQ if i < MH else MEM
                    if i + 1 < 2 * MH:
                        x_square(i + 1)
                    dve.wait_ge(rs_ready, k + 1)
                    for e in range(2):
                        t_e = (qx if i < MH else kx)[:, 2 * (i % MH) + e, :]
                        last = v.scalar_tensor_tensor(t_e, t_e, pcol("mq" if i < MH else "mk", e), xtmp[:, 4 + k % 2, 0:n], ALU.mult, ALU.mult)
                    dve.drain().then_inc(normed, 1)
                stage_end(dve, l, S_XNORM)
                FI = NT * FH

                def mem_normalise(i):
                    dve.wait_ge(exp_ready, FI + i + 1)
                    v.reciprocal(rinv[:, i:i + 1], rsum[:, i:i + 1])
                    dve.drain()
                    v.tensor_scalar(xtmp[:, i % 2, 0:MEM], xtmp[:, i % 2, 0:MEM], rinv[:, i:i + 1], None, ALU.mult).then_inc(prob_ready, 1)

                for i in range(NT * MH):
                    dve.wait_ge(att_done, FI + i + 1)
                    v.tensor_reduce(nmax[:, i:i + 1], PS[:, i % 2, 0:MEM], AX.X, ALU.max, negate=True)
                    dve.drain()
                    v.tensor_scalar(nmax[:, i:i + 1], nmax[:, i:i + 1], (2 * P) ** -0.5, None, ALU.mult).then_inc(max_ready, 1)
                    mem_normalise(i)
                stage_end(dve, l, S_XATT)
                add_residual(8)
                stage_end(dve, l, S_OUT2)
                norm(2 * NT + MT, X, NT, "ffn", hT)
                stage_end(dve, l, S_NORM3)
                stage_end(dve, l, S_PQ)

                def top16(values, scratch, best_v, best_i):
                    v.max(best_v[:, 0:8], values)
                    dve.drain()
                    v.match_replace(scratch, best_v[:, 0:8], values, NEG)
                    v.max_index(best_i[:, 0:8], best_v[:, 0:8], values)
                    dve.drain()
                    v.max(best_v[:, 8:16], scratch)
                    dve.drain()
                    v.max_index(best_i[:, 8:16], best_v[:, 8:16], scratch)

                for t in range(NT):
                    dve.wait_ge(sc_stored, t + 1)
                    for k in range(16):
                        top16(scores[:, k, :], rest[:, k % 4, :], top[:, k, :], topi[:, k, :])
                    dve.drain()
                    v.tensor_copy(topf[:], topi[:])
                    for h in range(PH):
                        v.tensor_tensor(cand.rearrange("p (a b) -> p a b", b=TOPK), along(top[:, 2 * h, :], TOPK),
                                        over(top[:, 2 * h + 1, :], TOPK), ALU.add)
                        dve.drain()
                        top16(cand, cand2, best[:, h, :], besti[:, h, :])
                    dve.drain()
                    flat = besti[:].rearrange("p h k -> p (h k)")
                    v.tensor_scalar(digits[:, 0, :], flat, 4, None, ALU.logical_shift_right)
                    v.tensor_scalar(digits[:, 1, :], flat, 15, None, ALU.bitwise_and)
                    if t:
                        dve.wait_ge(pickT_done, t)
                    v.tensor_tensor(picked[:, 2, :].rearrange("p (h k) -> p h k", k=TOPK), best[:], 
                                    best[:, :, 0:1].to_broadcast([P, PH, TOPK]), ALU.subtract)
                    dve.drain().then_inc(gate_diff, 1)
                    v.tensor_copy(digitf[:], digits[:])
                    dve.drain()
                    for side in range(2):
                        hot = onehot.rearrange("p a b -> p (a b)").rearrange("p (k a) -> p k a", a=TOPK)
                        v.tensor_tensor(hot, along(digitf[:, side, :], TOPK), over(iota[:, 0:TOPK], P), ALU.is_equal)
                        dve.drain()
                        for h in range(PH):
                            v.tensor_tensor(hot[:, h * TOPK:(h + 1) * TOPK, :], hot[:, h * TOPK:(h + 1) * TOPK, :],
                                            over(topf[:, 2 * h + side, :], TOPK), ALU.mult)
                        dve.drain()
                        v.tensor_reduce(picked[:, side, :], hot, AX.X, ALU.add)
                        dve.drain()
                    dve.wait_ge(gate_exp, t + 1)
                    gate = picked[:, 2, :].rearrange("p (h k) -> p h k", k=TOPK)
                    v.tensor_reduce(rsum[:, 0:PH], gate, AX.X, ALU.add)
                    dve.drain()
                    v.reciprocal(rinv[:, 0:PH], rsum[:, 0:PH])
                    dve.drain()
                    v.tensor_tensor(gate, gate, along(rinv[:, 0:PH], TOPK), ALU.mult)
                    dve.drain().then_inc(picks_ready, 1)
                    dve.wait_ge(pickT_stored, t + 1)
                    with v.Fori(0, P // TOK_STEP) as j:
                        for half in range(2):
                            n = t * (2 * P // TOK_STEP)
                            dve.wait_ge(spread_stored, n + j * 2 + half + 1)
                            for e in range(4):
                                es = slice(e * P, (e + 1) * P)
                                tok = j * TOK_STEP + half * 4 + e
                                v.tensor_scalar(hotA[:, half, es], iota, pickT[:, 0, bass.ds(tok, 1)], pickT[:, 2, bass.ds(tok, 1)],
                                                ALU.is_equal, ALU.mult)
                                last = v.tensor_scalar(hotB[:, half, es], iota, pickT[:, 1, bass.ds(tok, 1)], None, ALU.is_equal)
                            dve.drain().then_inc(hot_ready, 1)
                stage_end(dve, l, S_PICK)
                with v.Fori(0, NEXP_HI // GRP) as g:
                    for r in range(GRP):
                        dve.wait_ge(gelu_done, g * GRP + r + 3)
                        dve.wait_ge(g_loaded[r % 4], g * 32 + 16 * (r // 4) + 16)
                        v.tensor_tensor(w_grp[:, r, :], act_ring[:, r % 2, :], g_ring[:, r % 4, :], ALU.mult)
                        dve.drain().then_inc(g_free, 1)
                        dve.sem_inc(gated, 1)
                    for i in range(2 * NT):
                        t, half = i // 2, i % 2
                        dve.wait_ge(y_done, g * 8 + i + 1)
                        xs = X[:, t, half * 512:(half + 1) * 512]
                        v.tensor_tensor(xs, PS[:, 2 + i % 2, :], xs, ALU.add).then_inc(y_added, 1)
                stage_end(dve, l, S_PEER)
                layer_end(dve, l)

        @block.gpsimd
        def _(pool):
            g = nc.gpsimd
            pool.wait_ge(const_loaded, 16)
            with g.Fori(0, DEPTH) as l:
                stage_end(pool, l, S_NORM1)
                g.memset(raw[:, 0:12, 0:CONV_K - 1], 0.0).then_inc(pad_zeroed, 1)
                stage_end(pool, l, S_PROJ)
                stage_end(pool, l, S_PREP)
                stage_end(pool, l, S_GATES)
                for t in range(NT):
                    cols = slice(t * GH, (t + 1) * GH)

                    def grid(i):
                        return tmp[:, i, :].rearrange("p (h n) -> p h n", n=P)

                    g.tensor_tensor(grid(4), gb[:, :, t * P:(t + 1) * P], along(gcol[:, cols], P), ALU.subtract)
                    g.tensor_tensor(grid(5), over(strict, GH), along(beta[:, cols], P), ALU.mult)
                    pool.drain()
                    g.tensor_scalar(tmp[:, 0, :], tmp[:, 4, :], 0.0, None, ALU.max)
                    g.tensor_scalar(tmp[:, 1, :], tmp[:, 4, :], 0.0, None, ALU.min)
                    pool.drain().then_inc(diff_ready, 1)
                    if t:
                        pool.wait_ge(kq_used, t)
                    pool.wait_ge(decay_ready, t + 1)
                    g.tensor_tensor(tmp[:, 2, :], tmp[:, 0, :], tmp[:, 5, :], ALU.mult)
                    g.tensor_tensor(grid(3), grid(1), over(tri_chunk, GH), ALU.mult)
                    pool.drain().then_inc(mask_ready, 1)
                for h in range(GH):
                    pool.wait_ge(eg_ready, h + 1)
                    g.tensor_tensor(qd[:, h, :], conv[:, h, :], tmp[:, 6 + h % 2, :], ALU.mult).then_inc(qd_ready, 1)
                stage_end(pool, l, S_KQ)
                for k in range(4 * LEVELS):
                    t = k % 4
                    if k >= 2:
                        if k < 6:
                            pool.wait_ge(inv_stored, k - 1)
                        else:
                            pool.wait_ge(p_done, k - 5)
                    g.tensor_tensor(tmp[:, k % 2, :].rearrange("p (h n) -> p h n", n=P),
                                    A[:, t, :].rearrange("p (h n) -> p h n", n=P), over(level(k // 4), GH), ALU.mult).then_inc(lev_ready, 1)
                stage_end(pool, l, S_INV)
                for k in (S_UW, S_SCAN, S_ONORM, S_FOX):
                    stage_end(pool, l, k)
                pool.dma_start(memx[:], mem.rearrange("(t p) d -> p t d", p=P)).then_inc(mem_loaded, 16)
                for k in (S_OUT1, S_NORM2, S_XPROJ, S_XNORM, S_XATT, S_OUT2, S_NORM3):
                    stage_end(pool, l, k)
                pool.dma_start(keys_sb.rearrange("p k n -> p (k n)"), keys[bass.ds(l, 1)].rearrange("l p n -> (l p) n")).then_inc(keys_loaded, 16)
                stage_end(pool, l, S_PQ)
                stage_end(pool, l, S_PICK)
                stage_end(pool, l, S_PEER)
                pool.wait_ge(layer_left, 4 * l + 4)
                pool.sem_inc(layer_entered, 1)
                for s in local:
                    pool.sem_clear(s)
                pool.sem_inc(cleared, 1)


def kernel(**inputs):
    import numpy as _np
    import concourse.bacc as _bacc
    from concourse import mybir as _mybir
    from concourse.bass_utils import run_bass_kernel_spmd as _run

    a = {k: _np.asarray(v) for k, v in inputs.items()}

    def groups(w):
        n = w.shape[1] // 512
        return w.reshape(DC, P, n, 512).transpose(2, 1, 0, 3).reshape(n, P, DC * 512)

    packs, pars = [], []
    for l in range(DEPTH):
        w = a["w_in"][l]
        small = _np.zeros((D, 512), w.dtype)
        small[:, 0:8] = w[:, 2048:2056]
        small[:, 8:16] = w[:, 3592:3600]
        parts = [w[:, 0:2048], w[:, 2056:3592], small, a["w_out"][l], a["w_mq"][l], a["w_mkv"][l], a["w_mo"][l], a["w_pq"][l]]
        packs.append(_np.concatenate([groups(p) for p in parts]).reshape(N_PAIRS, 2, P, DC * 512))

        def col(v):
            return v.reshape(-1, P).T

        def row(v):
            return _np.broadcast_to(v, (P, v.shape[0]))

        conv = a["conv_w"][l][:, 0, :].reshape(CONV_K, 12, P).transpose(2, 1, 0).reshape(P, 12 * CONV_K)
        pars.append(_np.concatenate([
            col(a["mix_norm"][l]), col(a["xattn_norm"][l]), col(a["mem_norm"][l]), col(a["ffn_norm"][l]), conv,
            col(a["gdn_out_norm"][l]), col(_np.tile(a["fox_q_norm"][l], 2)), col(_np.tile(a["fox_k_norm"][l], 2)),
            col(a["mq_norm"][l]), col(a["mk_norm"][l]), row(a["dt_bias"][l]), row(a["a_log"][l]), row(a["fox_f_bias"][l])], axis=1))
    arrays = {
        "x": a["x"][0], "mem": a["mem"][0], "weights": _np.stack(packs), "params": _np.stack(pars), "consts": constants(),
        "keys": a["sub_keys"].transpose(0, 4, 2, 1, 3).reshape(DEPTH, P, 16 * P),
        "expert_u": a["expert_u"].reshape(DEPTH, NEXP_HI, P, DC, P).transpose(0, 1, 4, 3, 2).reshape(DEPTH, NEXP_HI, P, DC * P),
        "expert_v": a["expert_v"],
    }
    nc = _bacc.Bacc("TRN2", target_bir_lowering=False, num_devices=1)
    feeds, args = {}, []
    for name, v in arrays.items():
        v = _np.ascontiguousarray(v)
        feeds[f"in_{name}"] = v
        args.append(nc.dram_tensor(f"in_{name}", v.shape, _mybir.dt.from_np(v.dtype), kind="ExternalInput").ap())
    out = nc.dram_tensor("out", (SEQ, D), _mybir.dt.float32, kind="ExternalOutput").ap()
    trunk_kernel(nc, *args, out)
    r = _run(nc, [feeds], core_ids=[0])
    return r.results[0]["out"].reshape(1, SEQ, D)
```

```python
import concourse.bass as bass
import numpy as np
from concourse import mybir
from contextlib import ExitStack

P = 128
D = 1024
SEQ = 512
DEPTH = 2
NT = SEQ // P
DC = D // P
CH = 64
GH = 4
FH = 8
FD = 64
MEM = 256
MT = MEM // P
MH = 4
PH = 8
TOPK = 16
CONV_K = 4
NEXP_HI = 128
EPS = 1e-6
N_PAIRS = 11
PAIR_VS, PAIR_OUT, PAIR_MQ, PAIR_MK, PAIR_MV, PAIR_MO, PAIR_PQ = 3, 4, 5, 6, 7, 8, 9
NEG = -1e30
HOT = 4
HOTS = P // HOT
SAVED = 64
U_PER_T = SAVED // NT
U_SPREAD = 4
QUAD = 4

PC = {}
_at = 0
for _name, _n in (("mix", DC), ("xattn", DC), ("mem", DC), ("ffn", DC), ("conv", 12 * CONV_K), ("gdn_out", 1),
                  ("fox_q", 1), ("fox_k", 1), ("mq", 2), ("mk", 2), ("dt", GH), ("a_log", GH), ("f_bias", FH)):
    PC[_name] = _at
    _at += _n
NPAR = _at

LEVELS = 6
CC = {}
_at = 0
for _name, _n in (("ident", P), ("ones", P), ("blk64", P), ("tri_chunk", P), ("tri", P), ("strict", P),
                  ("level", LEVELS * P), ("causal", P), ("iota", P), ("bias", 4)):
    CC[_name] = _at
    _at += _n
NCONST = _at


def constants():
    r = np.arange(P)
    a, b = r[:, None], r[None, :]
    same = (a // CH) == (b // CH)
    c = np.zeros((P, NCONST), np.float32)

    def put(name, m):
        c[:m.shape[0], CC[name]:CC[name] + m.shape[1]] = m

    put("ident", np.eye(P))
    put("ones", np.ones((P, P)))
    put("blk64", same)
    put("tri_chunk", same & (a <= b))
    put("tri", a <= b)
    put("strict", same & (a > b))
    put("level", np.concatenate([(a // (2 * m) == b // (2 * m)) & (a % (2 * m) >= m) & (b % (2 * m) < m)
                                 for m in (1, 2, 4, 8, 16, 32)], axis=1))
    put("causal", np.where(b <= a, 0.0, NEG))
    put("iota", np.broadcast_to(b, (P, P)))
    put("bias", np.broadcast_to(np.array([EPS, np.log(P ** -0.5), np.log(FD ** -0.5), 0.0]), (P, 4)))
    return c


def trunk_kernel(nc, x, mem, weights, params, consts, keys, expert_u, expert_v, out):
    f32, u32 = mybir.dt.float32, mybir.dt.uint32
    ALU, ACT, AX = mybir.AluOpType, mybir.ActivationFunctionType, mybir.AxisListType
    f32r = mybir.dt.float32r
    gates_dram = nc.dram_tensor("gates_dram", (NEXP_HI, P, SEQ), f32, kind="Internal").ap()
    acts_dram = nc.dram_tensor("acts_dram", (SAVED, P, SEQ), f32, kind="Internal").ap()

    ctx = ExitStack()
    with ctx:
        def sb(name, shape, dt=f32):
            return ctx.enter_context(nc.sbuf_tensor(name, shape, dt))

        def sem(name):
            return ctx.enter_context(nc.semaphore(name))

        X = sb("X", [P, NT, D])
        cst = sb("cst", [P, NCONST])
        par = sb("par", [P, NPAR])
        stats = sb("stats", [P, 256])
        ARENA = 45096
        WRING = ARENA - 2 * DC * 512
        HT = WRING - DC * SEQ
        base = nc.sbuf_base
        assert base % 32 == 0
        sb("arena", [P, ARENA])
        PS = ctx.enter_context(nc.psum_tensor("PS", [P, 8, 512], f32))

        ident = cst[:, CC["ident"]:CC["ident"] + P]
        ones = cst[:, CC["ones"]:CC["ones"] + P]
        blk64 = cst[:, CC["blk64"]:CC["blk64"] + P]
        tri_chunk = cst[:, CC["tri_chunk"]:CC["tri_chunk"] + P]
        tri = cst[:, CC["tri"]:CC["tri"] + P]
        strict = cst[:, CC["strict"]:CC["strict"] + P]
        causal = cst[:, CC["causal"]:CC["causal"] + P]
        iota = cst[:, CC["iota"]:CC["iota"] + P]
        eps_col, lnq_gdn, lnq_fox = (cst[:, CC["bias"] + i:CC["bias"] + i + 1] for i in range(3))
        zero_col = cst[:, CC["bias"] + 3:CC["bias"] + 4]

        def level(i):
            return cst[:, CC["level"] + i * P:CC["level"] + (i + 1) * P]

        def sel(h, rows):
            return ident[0:rows, h:h + 1].to_broadcast([rows, P])

        def pcol(name, i=0):
            return par[:, PC[name] + i:PC[name] + i + 1]

        def area(name, offset, *dims, dt=f32):
            n = int(np.prod(dims))
            assert offset + n <= ARENA, (name, offset, dims)
            return nc.alloc_sbuf_tensor_at(name, [P, *dims], dt, offset=base + 4 * offset)[:]

        def area_r(name, offset, *dims):
            return area(name, offset, *dims, dt=f32r)

        def along(v, n):
            a = v.shape[1]
            return v.rearrange("p (a o) -> p a o", o=1).to_broadcast([P, a, n])

        def over(v, n):
            b = v.shape[1]
            return v.rearrange("p (o b) -> p o b", o=1).to_broadcast([P, n, b])

        def heads(bank):
            return PS[:, bank, :].rearrange("p (h n) -> p h n", n=P)

        hT = area("hT", HT, DC, SEQ)
        wring = area("wring", WRING, 2, DC, 512)
        hn = area("hn", HT - 3 * D, 2, D)
        junk = area("junk", HT - D, D)
        RW = SEQ + CONV_K - 1
        raw = area("raw", 0, 24, RW)
        o = 24 * RW
        conv = area("conv", o, 12, SEQ); o += 12 * SEQ
        fox_v = area("fox_v", o, NT, 512); o += NT * 512
        gb = area("gb", o, GH, SEQ); o += GH * SEQ
        qk_t = area("qk_t", o, NT, 512); o += NT * 512
        qd = area("qd", o, GH, SEQ); o += GH * SEQ
        tmp = area("tmp", o, 8, 512); o += 8 * 512
        small = area("small", o, NT, 16); o += NT * 16
        kbg = area("kbg", 0, NT, 512)
        kd = area("kd", NT * 512, NT, 512)
        vb = area("vb", 2 * NT * 512, NT, 512)
        A = hT[:, 0:4, :]
        Dinv = hT[:, 4:8, :]
        Einv = gb
        u_tok = conv[:, 4:8, :]
        w_T = conv[:, 8:12, :]
        o_T = kbg
        yT = hT
        state = tmp[:, 0:2, :]
        v_new = tmp[:, 2:4, :]
        row_T = area("row_T", o, SEQ); o += SEQ
        crow_T = area("crow_T", o, SEQ); o += SEQ
        ss_col = stats[:, 0:14]
        rstd_col = stats[:, 14:28]
        soft = stats[:, 32:96].rearrange("p (t n) -> p t n", n=16)
        la = stats[:, 96:112]
        lf = stats[:, 112:144]
        beta = stats[:, 144:160]
        gcol = stats[:, 160:176]
        beg = stats[:, 176:192]
        esuf = stats[:, 192:208]
        ccol = stats[:, 208:240]
        glast = sb("glast", [P, GH, SEQ // CH])
        nmax = sb("nmax", [P, 32])
        rsum = sb("rsum", [P, 32])
        rinv = sb("rinv", [P, 32])
        memx = area("memx", 0, MT, D)
        memT = area("memT", 2048, DC, MEM)
        qx = area("qx", 4096, DC, SEQ)
        kx = area("kx", 8192, DC, MEM)
        vx = area("vx", 10240, MT, D)
        xtmp = area("xtmp", 12288, 8, 512)
        h_hi, h_lo = area_r("h_hi", 0, DC, SEQ), area_r("h_lo", 4096, DC, SEQ)
        qp = area("qp", 8192, 16, SEQ)
        keys_sb = area("keys_sb", 16384, 16, P)
        scores = area("scores", 18432, NT, 16 * P)
        hotA = area("hotA", 8192, 2, HOT * P)
        hotB = area("hotB", 9216, 2, HOT * P)
        u_raw = area("u_raw", 10240, 2, DC * P)
        u_hi, u_lo = area_r("u_hi", 12288, 2, DC * P), area_r("u_lo", 14336, 2, DC * P)
        act_ring = area("act_ring", 16384, 2, SEQ)
        picked = area("picked", 17408, 3, P)
        digitf = area("digitf", 17792, 2, P)
        digits = area("digits", 18048, 2, P, dt=u32)
        gstage = area("gstage", 26624, NEXP_HI, P)
        rest = area("rest", 43008, 4, P)
        cand = area("cand", 43520, 2 * P)
        cand2 = area("cand2", 43776, 2 * P)
        v_raw = area("v_raw", 8192, 2, D)
        v_hi, v_lo = area_r("v_hi", 17408, 2 * QUAD, D), area_r("v_lo", 25600, 2 * QUAD, D)
        g_hi, g_lo = area_r("g_hi", 33792, 2 * QUAD, SEQ), area_r("g_lo", 37888, 2 * QUAD, SEQ)
        gate_ring = area("gate_ring", 41984, 2, SEQ)
        saved_ring = area("saved_ring", 43008, 2, SEQ)
        wt_ring = area("wt_ring", 44032, 2, SEQ)
        top = sb("top", [P, 16, TOPK])
        topi = sb("topi", [P, 16, TOPK], u32)
        topf = sb("topf", [P, 16, TOPK])
        best = sb("best", [P, PH, TOPK])
        besti = sb("besti", [P, PH, TOPK], u32)
        pickT = sb("pickT", [P, 3, P])
        hot_cols = sb("hot_cols", [P, 2, HOT])

        x_loaded, const_loaded, out_stored = sem("x_loaded"), sem("const_loaded"), sem("out_stored")
        par_loaded, mem_loaded, keys_loaded = sem("par_loaded"), sem("mem_loaded"), sem("keys_loaded")
        w_loaded = [sem("w_loaded0"), sem("w_loaded1")]
        w_free = [sem("w_free0"), sem("w_free1")]
        layer_left, cleared, layer_entered = sem("layer_left"), sem("cleared"), sem("layer_entered")
        local = []

        def lsem(name):
            s = sem(name)
            local.append(s)
            return s

        stage_done = lsem("stage_done")
        rstd_ready, hn_ready, transposed, gained = lsem("rstd_ready"), lsem("hn_ready"), lsem("transposed"), lsem("gained")
        pad_zeroed, proj_done, raw_stored, conv_done = lsem("pad_zeroed"), lsem("proj_done"), lsem("raw_stored"), lsem("conv_done")
        silu_done = lsem("silu_done")
        softarg, softexp, gate_cols = lsem("softarg"), lsem("softexp"), lsem("gate_cols")
        sq_ready, ss_done, rs_ready, normed = lsem("sq_ready"), lsem("ss_done"), lsem("rs_ready"), lsem("normed")
        cums_done, cums_stored, cols_ready = lsem("cums_done"), lsem("cums_stored"), lsem("cols_ready")
        gb_done, gb_stored = lsem("gb_done"), lsem("gb_stored")
        kq_done, kq_used, diff_ready, decay_ready, mask_ready = (lsem("kq_done"), lsem("kq_used"), lsem("diff_ready"),
                                                                 lsem("decay_ready"), lsem("mask_ready"))
        eg_ready, qd_ready = lsem("eg_ready"), lsem("qd_ready")
        lev_ready, lev_used, p_done, p_stored = lsem("lev_ready"), lsem("lev_used"), lsem("p_done"), lsem("p_stored")
        inv_done, inv_stored = lsem("inv_done"), lsem("inv_stored")
        uw_done, u_stored, w_stored = lsem("uw_done"), lsem("u_stored"), lsem("w_stored")
        state_zero, ws_done, vnew_ready = lsem("state_zero"), lsem("ws_done"), lsem("vnew_ready")
        chunk_done, state_ready, o_stored = lsem("chunk_done"), lsem("state_ready"), lsem("o_stored")
        att_done, max_ready, exp_ready, prob_ready = lsem("att_done"), lsem("max_ready"), lsem("exp_ready"), lsem("prob_ready")
        pt_done, pt_stored, pv_done, o_ready = lsem("pt_done"), lsem("pt_stored"), lsem("pv_done"), lsem("o_ready")
        ot_done, ot_stored = lsem("ot_done"), lsem("ot_stored")
        gemm_done, added = lsem("gemm_done"), lsem("added")
        xg_done, xg_stored = lsem("xg_done"), lsem("xg_stored")
        sc_done, sc_stored = lsem("sc_done"), lsem("sc_stored")
        gate_diff, gate_exp, picks_ready, pickT_done, pickT_stored = (lsem("gate_diff"), lsem("gate_exp"), lsem("picks_ready"),
                                                                      lsem("pickT_done"), lsem("pickT_stored"))
        h_parts = lsem("h_parts")
        hotA_ready, hotB_ready, spread_done, spread_stored = lsem("hotA_ready"), lsem("hotB_ready"), lsem("spread_done"), lsem("spread_stored")
        gates_out = lsem("gates_out")
        act_saved = [lsem("act_saved0"), lsem("act_saved1")]
        u_loaded = [lsem("u_loaded0"), lsem("u_loaded1")]
        v_loaded = [lsem("v_loaded0"), lsem("v_loaded1")]
        gate_loaded = [lsem("gate_loaded0"), lsem("gate_loaded1")]
        saved_loaded = [lsem("saved_loaded0"), lsem("saved_loaded1")]
        uhi_ready, ulo_ready, vhi_ready, vlo_ready = lsem("uhi_ready"), lsem("ulo_ready"), lsem("vhi_ready"), lsem("vlo_ready")
        act_done, gelu_done, wt_ready, whi_ready, wlo_ready = (lsem("act_done"), lsem("gelu_done"), lsem("wt_ready"),
                                                               lsem("whi_ready"), lsem("wlo_ready"))
        half_free = [lsem("saved_half_free"), lsem("fresh_half_free")]
        y_done, y_added = lsem("y_done"), lsem("y_added")

        (S_NORM1, S_PROJ, S_PREP, S_GATES, S_KQ, S_INV, S_UW, S_SCAN, S_ONORM, S_FOX, S_OUT1, S_NORM2, S_XPROJ, S_XNORM,
         S_XATT, S_OUT2, S_NORM3, S_PQ, S_PICK, S_PEER) = range(20)

        def stage_end(eng, l, k):
            eng.drain().then_inc(stage_done, 1)
            eng.wait_ge(stage_done, 4 * (k + 1))

        def layer_end(eng, l):
            eng.sem_inc(layer_left, 1)
            eng.wait_ge(cleared, l + 1)
            eng.sem_inc(layer_entered, 1)

        block = ctx.enter_context(nc.Block())

        @block.sync
        def _(sp):
            sp.dma_start(X[:], x.rearrange("(t p) d -> p t d", p=P)).then_inc(x_loaded, 16)
            with nc.sync.Fori(0, DEPTH) as l:
                w_layer = weights[bass.ds(l, 1)].rearrange("l q s p n -> (l q) s p n")
                with nc.sync.Fori(0, N_PAIRS) as q:
                    for s in range(2):
                        sp.wait_ge(w_free[s], l * N_PAIRS + q + 1)
                        sp.dma_start(wring[:, s].rearrange("p c n -> p (c n)"),
                                     w_layer[bass.ds(q, 1), s].rearrange("q p n -> (q p) n")).then_inc(w_loaded[s], 16)
                u_layer = expert_u[bass.ds(l, 1)].rearrange("l i p n -> (l i) p n")
                v_layer = expert_v[bass.ds(l, 1)].rearrange("l (i p) n -> p (l i) n", p=P)

                def load_u(n, slot):
                    sp.wait_ge(uhi_ready, n + 1)
                    sp.wait_ge(ulo_ready, n + 1)
                    sp.dma_start(u_raw[:, slot], u_layer[bass.ds(n, 1)].rearrange("i p n -> (i p) n")).then_inc(u_loaded[slot], 16)

                sp.wait_ge(stage_done, 4 * (S_PQ + 1))
                with nc.sync.Fori(0, SAVED // 2) as j:
                    for slot in range(2):
                        load_u(j * 2 + slot, slot)
                sp.wait_ge(stage_done, 4 * (S_PICK + 1))
                with nc.sync.Fori(0, SAVED // QUAD) as g:
                    for k in range(2 * QUAD):
                        fresh, r, slot = k // QUAD, k % QUAD, k % 2
                        if not fresh:
                            load_u(g * QUAD + (SAVED + r), r % 2)
                        tile = g * QUAD + (SAVED * fresh + r)
                        sp.wait_ge(vhi_ready, g * (2 * QUAD) + k + 1)
                        sp.wait_ge(vlo_ready, g * (2 * QUAD) + k + 1)
                        sp.dma_start(v_raw[:, slot], v_layer[:, bass.ds(tile, 1), :].rearrange("p o n -> p (o n)")).then_inc(v_loaded[slot], 16)
                        sp.wait_ge(wt_ready, g * (2 * QUAD) + k + 1)
                        sp.dma_start(gate_ring[:, slot], gates_dram[bass.ds(tile, 1)].rearrange("i p n -> (i p) n")).then_inc(gate_loaded[slot], 16)
                        if not fresh:
                            sp.dma_start(saved_ring[:, slot], acts_dram[bass.ds(tile, 1)].rearrange("i p n -> (i p) n")).then_inc(saved_loaded[slot], 16)
                sp.wait_ge(stage_done, 4 * (S_PEER + 1))
                layer_end(sp, l)
            sp.dma_start(out.rearrange("(t p) d -> p t d", p=P), X[:]).then_inc(out_stored, 16)
            sp.wait_ge(out_stored, 16)

        @block.tensor
        def _(pe):
            mm = nc.tensor.matmul

            def weights_ready(l, q, s):
                pe.wait_ge(w_loaded[s], l * (16 * N_PAIRS) + 16 * (q + 1))

            def norm_transposes(base, tiles):
                for t in range(tiles):
                    k = base + t
                    pe.wait_ge(hn_ready, k + 1)
                    if t >= 2:
                        pe.wait_ge(gained, k - 1)
                    for c in range(DC):
                        last = nc.tensor.transpose(PS[:, 2 * (k % 2) + c // 4, (c % 4) * P:(c % 4 + 1) * P],
                                                   hn[:, k % 2, c * P:(c + 1) * P], ident)
                    last.then_inc(transposed, 1)

            def channel_tile(bank, s, m, src, n, done):
                for c in range(DC):
                    last = mm(PS[:, bank, 0:n], wring[:, s, c, m * P:(m + 1) * P], src[:, c, 0:n], start=c == 0, stop=c == DC - 1)
                last.then_inc(done, 1)
                return last

            def token_tile(bank_ap, s, src, t, cols, done):
                for c in range(DC):
                    last = mm(bank_ap, src[:, c, t * P:(t + 1) * P], wring[:, s, c, 0:cols], start=c == 0, stop=c == DC - 1)
                last.then_inc(done, 1)
                return last

            def out_projection(l, q, n0):
                for s in range(2):
                    weights_ready(l, q, s)
                    for t in range(NT):
                        token_tile(PS[:, s * NT + t, :], s, yT, t, 512, gemm_done)
                    pe.drain().then_inc(w_free[s], 1)

            def sums(base, items, src_mat, n=SEQ):
                for i, mat in enumerate(items):
                    k = base + i
                    pe.wait_ge(sq_ready, k + 1)
                    if i >= 4:
                        pe.wait_ge(rs_ready, k - 3)
                    mm(PS[:, k % 4, 0:n], mat, src_mat[:, k % 2, 0:n], start=True, stop=True).then_inc(ss_done, 1)

            pe.wait_ge(const_loaded, 16)
            for s in range(2):
                pe.sem_inc(w_free[s], 1)
            with nc.tensor.Fori(0, DEPTH) as l:
                pe.sem_inc(act_done, 2)
                pe.sem_inc(spread_done, 2)
                pe.sem_inc(half_free[0], 1)
                pe.sem_inc(half_free[1], 1)
                norm_transposes(0, NT)
                stage_end(pe, l, S_NORM1)
                with nc.tensor.Fori(0, 3) as q:
                    for s in range(2):
                        weights_ready(l, q, s)
                        for m in range(4):
                            pe.wait_ge(raw_stored, q * 8 + s * 4 + m + 1)
                            channel_tile(s * 4 + m, s, m, hT, SEQ, proj_done)
                        pe.drain().then_inc(w_free[s], 1)
                weights_ready(l, PAIR_VS, 0)
                pe.wait_ge(raw_stored, 8 + 16 + 4)
                for t in range(NT):
                    token_tile(PS[:, t, :], 0, hT, t, 512, proj_done)
                pe.drain().then_inc(w_free[0], 1)
                weights_ready(l, PAIR_VS, 1)
                pe.wait_ge(raw_stored, 8 + 16 + 5)
                for t in range(NT):
                    token_tile(PS[:, 4, t * 16:(t + 1) * 16], 1, hT, t, 16, proj_done)
                pe.drain().then_inc(w_free[1], 1)
                stage_end(pe, l, S_PROJ)
                sums(0, [ones] * 8 + [blk64] * 8, tmp[:, 0:2, :])
                stage_end(pe, l, S_PREP)
                pe.wait_ge(gate_cols, 1)
                for t in range(NT):
                    la_t, lf_t = la[:, t * GH:(t + 1) * GH], lf[:, t * FH:(t + 1) * FH]
                    mm(PS[:, 0, t * GH:(t + 1) * GH], tri_chunk, la_t, start=True, stop=True)
                    mm(PS[:, 1, t * GH:(t + 1) * GH], strict, la_t, start=True, stop=True)
                    mm(PS[0:GH, 2, t * P:(t + 1) * P], la_t, tri_chunk, start=True, stop=True)
                    for e in range(t + 1):
                        lf_e = lf[:, e * FH:(e + 1) * FH]
                        mm(PS[:, 3, t * FH:(t + 1) * FH], tri if e == t else ones, lf_e, start=e == 0, stop=e == t)
                    for e in range(t + 1):
                        lf_e = lf[:, e * FH:(e + 1) * FH]
                        last = mm(PS[0:FH, 4, t * P:(t + 1) * P], lf_e, tri if e == t else ones, start=e == 0, stop=e == t)
                last.then_inc(cums_done, 1)
                pe.wait_ge(cums_stored, 1)
                for h in range(GH):
                    bank = 5 + h % 3
                    if h >= 3:
                        pe.wait_ge(gb_stored, h - 2)
                    mm(PS[:, bank, :], sel(h, GH), row_T[0:GH, :], start=True, stop=True).then_inc(gb_done, 1)
                stage_end(pe, l, S_GATES)
                for t in range(NT):
                    b = 4 * (t % 2)
                    if t >= 2:
                        pe.wait_ge(kq_used, t - 1)
                    ts = slice(t * P, (t + 1) * P)
                    for h in range(GH):
                        hs = slice(h * P, (h + 1) * P)
                        q_h, k_h, v_h = conv[:, h, ts], conv[:, 4 + h, ts], conv[:, 8 + h, ts]
                        mm(PS[:, b, hs], k_h, k_h, start=True, stop=True)
                        mm(PS[:, b + 1, hs], k_h, q_h, start=True, stop=True)
                        nc.tensor.transpose(PS[:, b + 2, hs], k_h, ident)
                        last = nc.tensor.transpose(PS[:, b + 3, hs], v_h, ident)
                    last.then_inc(kq_done, 1)
                stage_end(pe, l, S_KQ)
                def first_level(t):
                    pe.wait_ge(lev_ready, t + 1)
                    if t >= 2:
                        pe.wait_ge(inv_stored, t - 1)
                    for h in range(GH):
                        last = nc.tensor.transpose(PS[:, 2 + t % 2, h * P:(h + 1) * P], tmp[:, t % 2, h * P:(h + 1) * P], ident)
                    last.then_inc(inv_done, 1)

                def level_product(k):
                    t = k % 4
                    pe.wait_ge(lev_ready, k + 1)
                    pe.wait_ge(inv_stored, k - 3)
                    if k >= 6:
                        pe.wait_ge(p_stored, k - 5)
                    for h in range(GH):
                        hs = slice(h * P, (h + 1) * P)
                        last = mm(PS[:, k % 2, hs], tmp[:, k % 2, hs], Einv[:, t, hs], start=True, stop=True)
                    last.then_inc(p_done, 1)

                for t in range(NT):
                    first_level(t)
                level_product(4)
                for k in range(4, 4 * LEVELS):
                    t = k % 4
                    if k + 1 < 4 * LEVELS:
                        level_product(k + 1)
                    pe.wait_ge(p_stored, k - 3)
                    pe.wait_ge(inv_stored, k - 1)
                    for h in range(GH):
                        hs = slice(h * P, (h + 1) * P)
                        last = mm(PS[:, 2 + k % 2, hs], Dinv[:, t, hs], tmp[:, 2 + k % 2, hs], start=True, stop=True)
                    if k < 4 * (LEVELS - 1):
                        for h in range(GH):
                            hs = slice(h * P, (h + 1) * P)
                            last = mm(PS[:, 4 + k % 2, hs], tmp[:, 2 + k % 2, hs], Dinv[:, t, hs], start=True, stop=True)
                    last.then_inc(inv_done, 1)
                stage_end(pe, l, S_INV)
                for t in range(NT):
                    for h in range(GH):
                        hs = slice(h * P, (h + 1) * P)
                        mm(PS[:, t, hs], Einv[:, t, hs], vb[:, t, hs], start=True, stop=True)
                        last = mm(PS[:, 4 + t, hs], kbg[:, t, hs], Einv[:, t, hs], start=True, stop=True)
                    last.then_inc(uw_done, 1)
                stage_end(pe, l, S_UW)
                for n in range(SEQ // CH):
                    t, r0 = n // 2, (n % 2) * CH
                    rows = slice(r0, r0 + CH)
                    cur = state[:, n % 2, :]
                    pe.wait_ge(state_ready, n + 1)
                    if n >= 2:
                        pe.wait_ge(o_stored, n - 1)
                    for h in range(GH):
                        hs = slice(h * P, (h + 1) * P)
                        last = mm(PS[:, n % 2, hs], w_T[:, h, t * P:(t + 1) * P], cur[:, hs], start=True, stop=True)
                    last.then_inc(ws_done, 1)
                    pe.wait_ge(vnew_ready, n + 1)
                    for h in range(GH):
                        hs = slice(h * P, (h + 1) * P)
                        last = mm(PS[:, 2 + n % 2, hs], kd[rows, t, hs], v_new[rows, n % 2, hs], start=True, stop=True)
                    last.then_inc(chunk_done, 1)
                    for h in range(GH):
                        hs = slice(h * P, (h + 1) * P)
                        oc = PS[:, 4 + n % 2, h * CH:(h + 1) * CH]
                        mm(oc, cur[:, hs], qd[:, h, n * CH:(n + 1) * CH], start=True, stop=False)
                        last = mm(oc, v_new[rows, n % 2, hs], qk_t[rows, t, h * P + r0:h * P + r0 + CH], start=False, stop=True)
                    last.then_inc(chunk_done, 1)
                stage_end(pe, l, S_SCAN)
                sums(16, [ones] * 4, tmp[:, 0:2, :])
                stage_end(pe, l, S_ONORM)
                def fox_scores(i):
                    t, h = i // FH, i % FH
                    rows = slice((h % 2) * FD, (h % 2) * FD + FD)
                    n = (t + 1) * P
                    if i >= 2:
                        pe.wait_ge(max_ready, i - 1)
                    mm(PS[:, i % 2, 0:n], raw[rows, 16 + h // 2, 3 + t * P:3 + (t + 1) * P],
                       raw[rows, 20 + h // 2, 3:3 + n], start=True, stop=False)
                    mm(PS[:, i % 2, 0:n], sel(h, FH), crow_T[0:FH, 0:n], start=False, stop=True).then_inc(att_done, 1)

                fox_scores(0)
                for i in range(NT * FH):
                    t, h = i // FH, i % FH
                    if i + 1 < NT * FH:
                        fox_scores(i + 1)
                    pe.wait_ge(exp_ready, i + 1)
                    if i >= 2:
                        pe.wait_ge(pt_stored, i - 1)
                    for j in range(t + 1):
                        last = nc.tensor.transpose(PS[:, 2 + i % 2, j * P:(j + 1) * P], tmp[:, i % 2, j * P:(j + 1) * P], ident)
                    last.then_inc(pt_done, 1)
                    pe.wait_ge(pt_stored, i + 1)
                    if h == 0 and t >= 2:
                        pe.wait_ge(o_ready, t - 1)
                    for j in range(t + 1):
                        last = mm(PS[:, 4 + t % 2, h * FD:(h + 1) * FD], tmp[:, 2 + i % 2, j * P:(j + 1) * P],
                                  fox_v[:, j, h * FD:(h + 1) * FD], start=j == 0, stop=j == t)
                    last.then_inc(pv_done, 1)
                    if h == FH - 1:
                        pe.wait_ge(o_ready, t + 1)
                        if t >= 2:
                            pe.wait_ge(ot_stored, t - 1)
                        for c in range(4):
                            last = nc.tensor.transpose(PS[:, 6 + t % 2, c * P:(c + 1) * P], tmp[:, 4 + t % 2, c * P:(c + 1) * P], ident)
                        last.then_inc(ot_done, 1)
                stage_end(pe, l, S_FOX)
                out_projection(l, PAIR_OUT, 0)
                stage_end(pe, l, S_OUT1)
                norm_transposes(NT, NT)
                norm_transposes(2 * NT, MT)
                stage_end(pe, l, S_NORM2)
                for s in range(2):
                    weights_ready(l, PAIR_MQ, s)
                    for m in range(4):
                        channel_tile(s * 4 + m, s, m, hT, SEQ, xg_done)
                    pe.drain().then_inc(w_free[s], 1)
                for s in range(2):
                    weights_ready(l, PAIR_MK, s)
                    for m in range(4):
                        pe.wait_ge(xg_stored, s * 4 + m + 1)
                        channel_tile(s * 4 + m, s, m, memT, MEM, xg_done)
                    pe.drain().then_inc(w_free[s], 1)
                for s in range(2):
                    weights_ready(l, PAIR_MV, s)
                    for m in range(MT):
                        pe.wait_ge(xg_stored, 8 + s * 2 + m + 1)
                        token_tile(PS[:, s * 2 + m, :], s, memT, m, 512, xg_done)
                    pe.drain().then_inc(w_free[s], 1)
                stage_end(pe, l, S_XPROJ)
                for i in range(2 * MH):
                    n = SEQ if i < MH else MEM
                    k = 20 + i
                    pe.wait_ge(sq_ready, k + 1)
                    if i >= 4:
                        pe.wait_ge(rs_ready, k - 3)
                    for e in range(2):
                        last = mm(PS[:, k % 4, 0:n], ones, xtmp[:, 2 * (k % 2) + e, 0:n], start=e == 0, stop=e == 1)
                    last.then_inc(ss_done, 1)
                stage_end(pe, l, S_XNORM)

                FI = NT * FH

                def mem_scores(i):
                    t, h = i // MH, i % MH
                    if i >= 2:
                        pe.wait_ge(exp_ready, FI + i - 1)
                    for e in range(2):
                        last = mm(PS[:, i % 2, 0:MEM], qx[:, 2 * h + e, t * P:(t + 1) * P], kx[:, 2 * h + e, :], start=e == 0, stop=e == 1)
                    last.then_inc(att_done, 1)

                mem_scores(0)
                for i in range(NT * MH):
                    t, h = i // MH, i % MH
                    if i + 1 < NT * MH:
                        mem_scores(i + 1)
                    pe.wait_ge(prob_ready, i + 1)
                    if i >= 2:
                        pe.wait_ge(pt_stored, FI + i - 1)
                    for j in range(MT):
                        last = nc.tensor.transpose(PS[:, 2 + i % 2, j * P:(j + 1) * P], xtmp[:, i % 2, j * P:(j + 1) * P], ident)
                    last.then_inc(pt_done, 1)
                    pe.wait_ge(pt_stored, FI + i + 1)
                    if i >= 2:
                        pe.wait_ge(ot_stored, NT + i - 1)
                    for e in range(2):
                        for j in range(MT):
                            last = mm(PS[:, 4 + i % 2, e * P:(e + 1) * P], vx[:, j, (2 * h + e) * P:(2 * h + e + 1) * P],
                                      xtmp[:, 2 + i % 2, j * P:(j + 1) * P], start=j == 0, stop=j == MT - 1)
                    last.then_inc(ot_done, 1)
                stage_end(pe, l, S_XATT)
                out_projection(l, PAIR_MO, 8)
                stage_end(pe, l, S_OUT2)
                norm_transposes(2 * NT + MT, NT)
                stage_end(pe, l, S_NORM3)
                for q in range(2):
                    for s in range(2):
                        weights_ready(l, PAIR_PQ + q, s)
                        for m in range(4):
                            if q:
                                pe.wait_ge(xg_stored, 20 + s * 4 + m + 1)
                            channel_tile(s * 4 + m, s, m, hT, SEQ, xg_done)
                        pe.drain().then_inc(w_free[s], 1)
                pe.wait_ge(keys_loaded, l * 16 + 16)
                pe.wait_ge(xg_stored, 36)
                for t in range(NT):
                    if t >= 2:
                        pe.wait_ge(sc_stored, t - 1)
                    for k in range(16):
                        last = mm(PS[:, 4 * (t % 2) + k // 4, (k % 4) * P:(k % 4 + 1) * P], qp[:, k, t * P:(t + 1) * P], keys_sb[:, k, :],
                                  start=True, stop=True)
                    last.then_inc(sc_done, 1)
                stage_end(pe, l, S_PQ)

                def parts_product(bank_ap, a_hi, a_lo, b_hi, b_lo, first, final):
                    mm(bank_ap, a_hi, b_hi, start=first, stop=False)
                    mm(bank_ap, a_hi, b_lo, start=False, stop=False)
                    return mm(bank_ap, a_lo, b_hi, start=False, stop=final)

                def expert_acts(n, slot):
                    pe.wait_ge(uhi_ready, n + 3)
                    pe.wait_ge(ulo_ready, n + 3)
                    pe.wait_ge(gelu_done, n + 1)
                    for c in range(DC):
                        cs = slice(c * P, (c + 1) * P)
                        last = parts_product(PS[:, slot, :], u_hi[:, slot, cs], u_lo[:, slot, cs], h_hi[:, c, :], h_lo[:, c, :],
                                             c == 0, c == DC - 1)
                    last.then_inc(act_done, 1)

                for t in range(NT):
                    with nc.tensor.Fori(0, (U_PER_T - U_SPREAD) // 2) as j:
                        for slot in range(2):
                            expert_acts(j * 2 + (t * U_PER_T + slot), slot)
                    pe.wait_ge(picks_ready, t + 1)
                    for k in range(3):
                        last = nc.tensor.transpose(PS[:, 4, k * P:(k + 1) * P], picked[:, k, :], ident)
                    last.then_inc(pickT_done, 1)
                    with nc.tensor.Fori(0, U_SPREAD // 2) as j:
                        for slot in range(2):
                            expert_acts(j * 2 + ((t + 1) * U_PER_T - U_SPREAD + slot), slot)
                            for m in range(HOTS // U_SPREAD):
                                step = j * (2 * HOTS // U_SPREAD) + (t * HOTS + slot * (HOTS // U_SPREAD) + m)
                                pe.wait_ge(hotA_ready, step + 1)
                                pe.wait_ge(hotB_ready, step + 1)
                                pe.wait_ge(spread_stored, step + 1)
                                for e in range(HOT):
                                    es = slice(e * P, (e + 1) * P)
                                    last = mm(PS[:, 5 + m % 2, es], hotB[:, m % 2, es], hotA[:, m % 2, es], start=True, stop=True)
                                last.then_inc(spread_done, 1)
                stage_end(pe, l, S_PICK)
                with nc.tensor.Fori(0, SAVED // QUAD) as g:
                    for r in range(QUAD):
                        expert_acts(g * QUAD + (SAVED + r), r % 2)
                    for fresh in range(2):
                        for i in range(2 * NT):
                            t, half = i // 2, i % 2
                            pe.wait_ge(y_added, g * (4 * NT) + fresh * 2 * NT + i + 1)
                            for r in range(QUAD):
                                k = fresh * QUAD + r
                                if i == 0:
                                    pe.wait_ge(vhi_ready, g * (2 * QUAD) + k + 3)
                                    pe.wait_ge(vlo_ready, g * (2 * QUAD) + k + 3)
                                    pe.wait_ge(whi_ready, g * (2 * QUAD) + k + 1)
                                    pe.wait_ge(wlo_ready, g * (2 * QUAD) + k + 3)
                                ts, hs = slice(t * P, (t + 1) * P), slice(half * 512, (half + 1) * 512)
                                last = parts_product(PS[:, 2 + i % 4, :], g_hi[:, k, ts], g_lo[:, k, ts], v_hi[:, k, hs], v_lo[:, k, hs],
                                                     r == 0, r == QUAD - 1)
                            last.then_inc(y_done, 1)
                        pe.drain().then_inc(half_free[fresh], 1)
                stage_end(pe, l, S_PEER)
                layer_end(pe, l)

        @block.scalar
        def _(act):
            fn = nc.scalar.activation

            def rstd(base, src, tiles):
                for t in range(tiles):
                    k = base + t
                    fn(junk, src[:, t, :], ACT.Square, accum_out=ss_col[:, k:k + 1])
                    act.drain()
                    fn(rstd_col[:, k:k + 1], ss_col[:, k:k + 1], ACT.Ln, bias=eps_col, scale=1.0 / D)
                    act.drain()
                    fn(rstd_col[:, k:k + 1], rstd_col[:, k:k + 1], ACT.Exp, bias=zero_col, scale=-0.5).then_inc(rstd_ready, 1)

            def inv_norms(base, specs, dst, n=SEQ):
                for i, (scale, bias) in enumerate(specs):
                    k = base + i
                    act.wait_ge(ss_done, k + 1)
                    if i >= 2:
                        act.wait_ge(normed, k - 1)
                    fn(dst[:, k % 2, 0:n], PS[:, k % 4, 0:n], ACT.Ln, bias=eps_col, scale=scale)
                    act.drain()
                    fn(dst[:, k % 2, 0:n], dst[:, k % 2, 0:n], ACT.Exp, bias=bias, scale=-0.5).then_inc(rs_ready, 1)

            act.dma_start(cst[:], consts).then_inc(const_loaded, 16)
            act.wait_ge(const_loaded, 16)
            act.wait_ge(x_loaded, 16)
            with nc.scalar.Fori(0, DEPTH) as l:
                act.dma_start(par[:], params[bass.ds(l, 1)].rearrange("l p n -> (l p) n")).then_inc(par_loaded, 16)
                act.wait_ge(par_loaded, l * 16 + 16)
                act.sem_inc(raw_stored, 8)
                act.sem_inc(gelu_done, 2)
                act.sem_inc(uhi_ready, 2)
                act.sem_inc(vhi_ready, 2)
                act.sem_inc(spread_stored, 2)
                rstd(0, X, NT)
                stage_end(act, l, S_NORM1)
                with nc.scalar.Fori(0, 3) as q:
                    for b in range(8):
                        act.wait_ge(proj_done, q * 8 + b + 1)
                        fn(raw[:, bass.ds(q * 8 + b, 1), 3:RW].rearrange("p o n -> p (o n)"), PS[:, b, :], ACT.Copy).then_inc(raw_stored, 1)
                for t in range(NT):
                    act.wait_ge(proj_done, 24 + t + 1)
                    fn(fox_v[:, t, :], PS[:, t, :], ACT.Copy)
                act.wait_ge(proj_done, 24 + 2 * NT)
                fn(small.rearrange("p t n -> p (t n)"), PS[:, 4, 0:NT * 16], ACT.Copy)
                fn(raw[:, 12:16, 3:RW], raw[:, 12:16, 3:RW], ACT.Silu)
                for k in range(3):
                    act.wait_ge(conv_done, 4 * (k + 1))
                    fn(conv[:, 4 * k:4 * (k + 1), :], conv[:, 4 * k:4 * (k + 1), :], ACT.Silu)
                stage_end(act, l, S_PROJ)
                act.wait_ge(softarg, 1)
                fn(soft[:, :, :], soft[:, :, :], ACT.Exp, bias=zero_col, scale=-1.0)
                act.drain()
                fn(soft[:, :, 0:4], soft[:, :, 0:4], ACT.Ln, bias=1.0)
                fn(soft[:, :, 8:16], soft[:, :, 8:16], ACT.Ln, bias=1.0)
                fn(nmax[:, 0:GH], par[:, PC["a_log"]:PC["a_log"] + GH], ACT.Exp)
                act.drain().then_inc(softexp, 1)
                inv_norms(0, [(1.0, lnq_gdn)] * 4 + [(1.0, zero_col)] * 4 + [(1.0 / FD, lnq_fox)] * 4 + [(1.0 / FD, zero_col)] * 4,
                          tmp[:, 2:4, :])
                stage_end(act, l, S_PREP)
                act.wait_ge(cums_done, 1)
                fn(row_T[0:GH, :], PS[0:GH, 2, :], ACT.Copy)
                fn(crow_T[0:FH, :], PS[0:FH, 4, :], ACT.Copy, scale=-1.0)
                act.drain().then_inc(cums_stored, 1)
                fn(beg, PS[:, 0, 0:16], ACT.Exp)
                fn(esuf, PS[:, 1, 0:16], ACT.Exp)
                fn(gcol, PS[:, 0, 0:16], ACT.Copy)
                fn(ccol, PS[:, 3, 0:32], ACT.Copy)
                act.drain().then_inc(cols_ready, 1)
                for h in range(GH):
                    act.wait_ge(gb_done, h + 1)
                    fn(gb[:, h, :], PS[:, 5 + h % 3, :], ACT.Copy)
                    fn(tmp[:, h % 2 + 0, :], PS[:, 5 + h % 3, :], ACT.Exp) if False else None
                    act.drain().then_inc(gb_stored, 1)
                fn(glast[:, :, :], gb[:, :, CH - 1:SEQ:CH], ACT.Exp)
                stage_end(act, l, S_GATES)
                for t in range(NT):
                    act.wait_ge(diff_ready, t + 1)
                    fn(tmp[:, 0, :], tmp[:, 0, :], ACT.Exp, bias=zero_col, scale=-1.0)
                    fn(tmp[:, 1, :], tmp[:, 1, :], ACT.Exp)
                    act.drain().then_inc(decay_ready, 1)
                for h in range(GH):
                    if h >= 2:
                        act.wait_ge(qd_ready, h - 1)
                    fn(tmp[:, 6 + h % 2, :], gb[:, h, :], ACT.Exp).then_inc(eg_ready, 1)
                stage_end(act, l, S_KQ)
                for k in range(4, 4 * LEVELS):
                    act.wait_ge(p_done, k - 3)
                    if k >= 6:
                        act.wait_ge(inv_done, k - 1)
                    fn(tmp[:, 2 + k % 2, :], PS[:, k % 2, :], ACT.Copy).then_inc(p_stored, 1)
                stage_end(act, l, S_INV)
                for t in range(NT):
                    act.wait_ge(uw_done, t + 1)
                    fn(u_tok[:, t, :], PS[:, t, :], ACT.Copy)
                stage_end(act, l, S_UW)
                for n in range(SEQ // CH):
                    act.wait_ge(chunk_done, 2 * n + 2)
                    fn(o_T.rearrange("p h n -> p h n")[:, :, n * CH:(n + 1) * CH],
                       PS[:, 4 + n % 2, 0:GH * CH].rearrange("p (h n) -> p h n", n=CH), ACT.Copy).then_inc(o_stored, 1)
                stage_end(act, l, S_SCAN)
                inv_norms(16, [(1.0 / P, zero_col)] * 4, tmp[:, 2:4, :])
                stage_end(act, l, S_ONORM)
                for i in range(NT * FH):
                    t, h = i // FH, i % FH
                    n = (t + 1) * P
                    act.wait_ge(max_ready, i + 1)
                    fn(tmp[:, i % 2, 0:n], tmp[:, 6 + i % 2, 0:n], ACT.Exp, bias=nmax[:, i:i + 1],
                       accum_out=rsum[:, i:i + 1]).then_inc(exp_ready, 1)
                    act.wait_ge(pt_done, i + 1)
                    fn(tmp[:, 2 + i % 2, 0:n], PS[:, 2 + i % 2, 0:n], ACT.Copy).then_inc(pt_stored, 1)
                    if h == FH - 1:
                        act.wait_ge(ot_done, t + 1)
                        fn(yT[:, 4:8, t * P:(t + 1) * P], heads(6 + t % 2), ACT.Copy).then_inc(ot_stored, 1)
                stage_end(act, l, S_FOX)
                stage_end(act, l, S_OUT1)
                rstd(NT, X, NT)
                act.wait_ge(mem_loaded, l * 16 + 16)
                rstd(2 * NT, memx, MT)
                stage_end(act, l, S_NORM2)
                for b in range(8):
                    act.wait_ge(xg_done, b + 1)
                    fn(qx[:, b, :], PS[:, b, :], ACT.Copy).then_inc(xg_stored, 1)
                for b in range(8):
                    act.wait_ge(xg_done, 8 + b + 1)
                    fn(kx[:, b, :], PS[:, b, 0:MEM], ACT.Copy).then_inc(xg_stored, 1)
                for b in range(4):
                    act.wait_ge(xg_done, 16 + b + 1)
                    fn(vx[:, b % 2, (b // 2) * 512:(b // 2 + 1) * 512], PS[:, b, :], ACT.Copy).then_inc(xg_stored, 1)
                stage_end(act, l, S_XPROJ)
                for i in range(2 * MH):
                    n = SEQ if i < MH else MEM
                    k = 20 + i
                    act.wait_ge(ss_done, k + 1)
                    if i >= 2:
                        act.wait_ge(normed, k - 1)
                    fn(xtmp[:, 4 + k % 2, 0:n], PS[:, k % 4, 0:n], ACT.Ln, bias=eps_col, scale=1.0 / (2 * P))
                    act.drain()
                    fn(xtmp[:, 4 + k % 2, 0:n], xtmp[:, 4 + k % 2, 0:n], ACT.Exp, bias=zero_col, scale=-0.5).then_inc(rs_ready, 1)
                stage_end(act, l, S_XNORM)
                FI = NT * FH
                for i in range(NT * MH):
                    t, h = i // MH, i % MH
                    act.wait_ge(max_ready, FI + i + 1)
                    if i >= 2:
                        act.wait_ge(pt_done, FI + i - 1)
                    fn(xtmp[:, i % 2, 0:MEM], PS[:, i % 2, 0:MEM], ACT.Exp, bias=nmax[:, i:i + 1], scale=(2 * P) ** -0.5,
                       accum_out=rsum[:, i:i + 1]).then_inc(exp_ready, 1)
                    act.wait_ge(pt_done, FI + i + 1)
                    fn(xtmp[:, 2 + i % 2, 0:MEM], PS[:, 2 + i % 2, 0:MEM], ACT.Copy).then_inc(pt_stored, 1)
                    act.wait_ge(ot_done, NT + i + 1)
                    fn(yT[:, 2 * h:2 * h + 2, t * P:(t + 1) * P], PS[:, 4 + i % 2, 0:MEM].rearrange("p (e n) -> p e n", n=P),
                       ACT.Copy).then_inc(ot_stored, 1)
                stage_end(act, l, S_XATT)
                stage_end(act, l, S_OUT2)
                rstd(2 * NT + MT, X, NT)
                stage_end(act, l, S_NORM3)
                for b in range(16):
                    act.wait_ge(xg_done, 20 + b + 1)
                    fn(qp[:, b, :], PS[:, b % 8, :], ACT.Copy).then_inc(xg_stored, 1)
                    if b < DC:
                        fn(h_hi[:, b, :], hT[:, b, :], ACT.Copy).then_inc(h_parts, 1)
                for t in range(NT):
                    act.wait_ge(sc_done, t + 1)
                    fn(scores[:, t, :], PS[:, 4 * (t % 2):4 * (t % 2) + 4, :].rearrange("p b n -> p (b n)"), ACT.Copy).then_inc(sc_stored, 1)
                stage_end(act, l, S_PQ)

                def split_u(n, half_n, slot):
                    act.wait_ge(u_loaded[slot], half_n * 16 + 16)
                    act.wait_ge(act_done, n + 1)
                    fn(u_hi[:, slot, :], u_raw[:, slot, :], ACT.Copy).then_inc(uhi_ready, 1)

                def gelu(n, slot):
                    act.wait_ge(act_done, n + 3)
                    fn(act_ring[:, slot, :], PS[:, slot, :], ACT.Gelu_apprx_tanh).then_inc(gelu_done, 1)

                def gelu_saved(n, half_n, slot, first=False):
                    if not first:
                        act.wait_ge(act_saved[slot], half_n * 16)
                    gelu(n, slot)
                    act.wait_ge(gelu_done, n + 3)
                    act.dma_start(acts_dram[bass.ds(n, 1)].rearrange("i p n -> (i p) n"), act_ring[:, slot]).then_inc(act_saved[slot], 16)

                def acts_pair(j, first=False, second=False):
                    split_u(j * 2, j, 0)
                    if not first:
                        gelu_saved(j * 2 - 1, j - 1, 1, second)
                    split_u(j * 2 + 1, j, 1)
                    gelu_saved(j * 2, j, 0, first)

                for t in range(NT):
                    j0 = t * U_PER_T // 2
                    pairs = (U_PER_T - U_SPREAD) // 2
                    if t == 0:
                        acts_pair(0, first=True)
                        acts_pair(1, second=True)
                    with nc.scalar.Fori(2 if t == 0 else 0, pairs) as j:
                        acts_pair(j + j0)
                    act.wait_ge(gate_diff, t + 1)
                    fn(picked[:, 2, :], picked[:, 2, :], ACT.Exp).then_inc(gate_exp, 1)
                    act.wait_ge(pickT_done, t + 1)
                    fn(pickT[:, :, :].rearrange("p k n -> p (k n)"), PS[:, 4, 0:3 * P], ACT.Copy).then_inc(pickT_stored, 1)
                    if t:
                        act.wait_ge(gates_out, 64 * t)
                    with nc.scalar.Fori(0, U_SPREAD // 2) as j:
                        for slot in range(2):
                            jj = j + (j0 + pairs)
                            if slot == 0:
                                split_u(jj * 2, jj, 0)
                                gelu_saved(jj * 2 - 1, jj - 1, 1)
                            else:
                                split_u(jj * 2 + 1, jj, 1)
                                gelu_saved(jj * 2, jj, 0)
                            for m in range(HOTS // U_SPREAD):
                                step = j * (2 * HOTS // U_SPREAD) + (slot * (HOTS // U_SPREAD) + m)
                                act.wait_ge(spread_done, step + (t * HOTS + 3))
                                fn(gstage[:, :, bass.ds(step * HOT, HOT)],
                                   PS[:, 5 + m % 2, :].rearrange("p (e i) -> p i e", i=P), ACT.Copy).then_inc(spread_stored, 1)
                    act.wait_ge(spread_stored, 2 + (t + 1) * HOTS)
                    for i in range(0, NEXP_HI, 32):
                        act.dma_start(gates_dram[i:i + 32, :, t * P:(t + 1) * P].rearrange("i j t -> j i t"),
                                      gstage[:, i:i + 32, :]).then_inc(gates_out, 16)
                gelu_saved(SAVED - 1, SAVED // 2 - 1, 1)
                act.wait_ge(gates_out, 64 * NT)
                for slot in range(2):
                    act.wait_ge(act_saved[slot], 16 * SAVED // 2)
                stage_end(act, l, S_PICK)
                with nc.scalar.Fori(0, SAVED // QUAD) as g:
                    def split_v(k):
                        act.wait_ge(v_loaded[k % 2], g * (16 * QUAD) + 16 * (k // 2) + 16)
                        act.wait_ge(half_free[k // QUAD], g + 1)
                        fn(v_hi[:, k, :], v_raw[:, k % 2, :], ACT.Copy).then_inc(vhi_ready, 1)

                    def split_w(k):
                        act.wait_ge(wt_ready, g * (2 * QUAD) + k + 3)
                        act.wait_ge(half_free[k // QUAD], g + 1)
                        fn(g_hi[:, k, :], wt_ring[:, k % 2, :], ACT.Copy).then_inc(whi_ready, 1)

                    def split_fresh_u(r):
                        split_u(g * QUAD + (SAVED + r), g * (QUAD // 2) + (SAVED + r) // 2, r % 2)

                    def gelu_fresh(r):
                        act.wait_ge(wt_ready, g * (2 * QUAD) + (QUAD + r + 1 if r >= 2 else r + 1))
                        gelu(g * QUAD + (SAVED + r), r % 2)

                    split_fresh_u(0)
                    split_fresh_u(1)
                    for k in range(QUAD):
                        split_v(k)
                        split_w(k)
                    gelu_fresh(0)
                    split_fresh_u(2)
                    split_v(4)
                    gelu_fresh(1)
                    split_fresh_u(3)
                    split_w(4)
                    split_v(5)
                    split_w(5)
                    gelu_fresh(2)
                    split_v(6)
                    split_w(6)
                    gelu_fresh(3)
                    split_v(7)
                    split_w(7)
                stage_end(act, l, S_PEER)
                layer_end(act, l)

        @block.vector
        def _(dve):
            v = nc.vector

            def norm(base, src, tiles, gain, dst):
                def evacuate(t):
                    k = base + t
                    dve.wait_ge(transposed, k + 1)
                    for half in range(2):
                        last = v.tensor_tensor(dst[:, 4 * half:4 * half + 4, t * P:(t + 1) * P], heads(2 * (k % 2) + half),
                                               along(par[:, PC[gain] + 4 * half:PC[gain] + 4 * half + 4], P), ALU.mult)
                    last.then_inc(gained, 1)

                for t in range(tiles):
                    k = base + t
                    dve.wait_ge(rstd_ready, k + 1)
                    if k >= 2:
                        dve.wait_ge(transposed, k - 1)
                    v.tensor_scalar(hn[:, k % 2, :], src[:, t, :], rstd_col[:, k:k + 1], None, ALU.mult).then_inc(hn_ready, 1)
                    if t:
                        evacuate(t - 1)
                evacuate(tiles - 1)

            def add_residual(base):
                for s in range(2):
                    for t in range(NT):
                        dve.wait_ge(gemm_done, base + s * NT + t + 1)
                        xs = X[:, t, s * 512:(s + 1) * 512]
                        v.tensor_tensor(xs, PS[:, s * NT + t, :], xs, ALU.add)

            def norm_items(base, items, apply, buf):
                n = len(items)

                def square(i):
                    k = base + i
                    if i >= 2:
                        dve.wait_ge(ss_done, k - 1)
                    v.tensor_tensor(buf[:, k % 2, :], items[i], items[i], ALU.mult).then_inc(sq_ready, 1)

                square(0)
                for i in range(n):
                    if i + 1 < n:
                        square(i + 1)
                    dve.wait_ge(rs_ready, base + i + 1)
                    apply(i, base + i)

            dve.wait_ge(const_loaded, 16)
            dve.wait_ge(x_loaded, 16)
            with nc.vector.Fori(0, DEPTH) as l:
                dve.wait_ge(par_loaded, l * 16 + 16)
                dve.sem_inc(y_added, 4)
                dve.sem_inc(wt_ready, 2)
                dve.sem_inc(wlo_ready, 2)
                norm(0, X, NT, "mix", hT)
                stage_end(dve, l, S_NORM1)
                dve.wait_ge(pad_zeroed, 1)
                with v.Fori(0, 12) as m:
                    dve.wait_ge(raw_stored, m + 9)
                    row = raw[:, bass.ds(m, 1), :].rearrange("p o n -> p (o n)")
                    dst = conv[:, bass.ds(m, 1), :].rearrange("p o n -> p (o n)")

                    def tap(j):
                        return par[:, bass.ds(m * CONV_K + PC["conv"] + j, 1)]

                    v.tensor_scalar(dst, row[:, 0:SEQ], tap(0), None, ALU.mult)
                    for j in range(1, CONV_K):
                        dve.drain()
                        last = v.scalar_tensor_tensor(dst, row[:, j:j + SEQ], tap(j), dst, ALU.mult, ALU.add)
                    last.then_inc(conv_done, 1)
                stage_end(dve, l, S_PROJ)
                dtb = over(par[:, PC["dt"]:PC["dt"] + GH], NT)
                fbb = over(par[:, PC["f_bias"]:PC["f_bias"] + FH], NT)
                v.tensor_tensor(small[:, :, 0:4], small[:, :, 0:4], dtb, ALU.add)
                v.tensor_tensor(small[:, :, 8:16], small[:, :, 8:16], fbb, ALU.add)
                dve.drain()
                v.tensor_scalar(small[:, :, 8:16], small[:, :, 8:16], -1.0, None, ALU.mult)
                dve.drain()
                v.scalar_tensor_tensor(soft[:, :, 0:4], small[:, :, 0:4], -1.0, small[:, :, 0:4], ALU.mult, ALU.max)
                v.scalar_tensor_tensor(soft[:, :, 8:16], small[:, :, 8:16], -1.0, small[:, :, 8:16], ALU.mult, ALU.max)
                v.tensor_copy(soft[:, :, 4:8], small[:, :, 4:8])
                dve.drain().then_inc(softarg, 1)
                dve.wait_ge(softexp, 1)
                v.tensor_scalar(small[:, :, 0:4], small[:, :, 0:4], 0.0, None, ALU.max)
                v.tensor_scalar(small[:, :, 8:16], small[:, :, 8:16], 0.0, None, ALU.max)
                v.tensor_scalar(soft[:, :, 4:8], soft[:, :, 4:8], 1.0, None, ALU.add)
                dve.drain()
                v.tensor_tensor(small[:, :, 0:4], small[:, :, 0:4], soft[:, :, 0:4], ALU.add)
                v.tensor_tensor(small[:, :, 8:16], small[:, :, 8:16], soft[:, :, 8:16], ALU.add)
                v.reciprocal(beta.rearrange("p (t h) -> p t h", h=GH), soft[:, :, 4:8])
                dve.drain()
                v.tensor_tensor(small[:, :, 0:4], small[:, :, 0:4], over(nmax[:, 0:GH], NT), ALU.mult)
                v.tensor_scalar(lf.rearrange("p (t h) -> p t h", h=FH), small[:, :, 8:16], -1.0, None, ALU.mult)
                dve.drain()
                v.tensor_scalar(la.rearrange("p (t h) -> p t h", h=GH), small[:, :, 0:4], -1.0, None, ALU.mult)
                dve.drain().then_inc(gate_cols, 1)
                qk_items = [conv[:, i, :] for i in range(8)] + [raw[:, 16 + i, 3:RW] for i in range(8)]

                def apply_qk(i, k):
                    x_i = qk_items[i]
                    rs = tmp[:, 2 + k % 2, :]
                    if i < 8:
                        v.tensor_tensor(x_i, x_i, rs, ALU.mult).then_inc(normed, 1)
                    else:
                        v.scalar_tensor_tensor(x_i, x_i, pcol("fox_q" if i < 12 else "fox_k"), rs, ALU.mult, ALU.mult).then_inc(normed, 1)

                norm_items(0, qk_items, apply_qk, tmp[:, 0:2, :])
                stage_end(dve, l, S_PREP)
                dve.wait_ge(cols_ready, 1)
                v.tensor_tensor(beg, beg, beta, ALU.mult)
                stage_end(dve, l, S_GATES)
                for t in range(NT):
                    b = 4 * (t % 2)
                    dve.wait_ge(kq_done, t + 1)
                    cols = slice(t * GH, (t + 1) * GH)

                    def grid(a):
                        return a[:, t, :].rearrange("p (h n) -> p h n", n=P)

                    v.tensor_tensor(grid(kbg), heads(b + 2), along(beg[:, cols], P), ALU.mult)
                    v.tensor_tensor(grid(kd), heads(b + 2), along(esuf[:, cols], P), ALU.mult)
                    v.tensor_tensor(grid(vb), heads(b + 3), along(beta[:, cols], P), ALU.mult)
                    dve.wait_ge(mask_ready, t + 1)
                    v.tensor_tensor(A[:, t, :], PS[:, b, :], tmp[:, 2, :], ALU.mult)
                    v.tensor_tensor(qk_t[:, t, :], PS[:, b + 1, :], tmp[:, 3, :], ALU.mult)
                    dve.drain().then_inc(kq_used, 1)
                stage_end(dve, l, S_KQ)

                def grid_t(a, t):
                    return a[:, t, :].rearrange("p (h n) -> p h n", n=P)

                for t in range(NT):
                    dve.wait_ge(lev_ready, t + 1)
                    v.tensor_tensor(grid_t(Dinv, t), over(ident, GH), grid_t(tmp, t % 2), ALU.subtract)
                    dve.wait_ge(inv_done, t + 1)
                    v.tensor_tensor(grid_t(Einv, t), over(ident, GH), heads(2 + t % 2), ALU.subtract)
                    dve.drain().then_inc(inv_stored, 1)
                for k in range(4, 4 * LEVELS):
                    t = k % 4
                    dve.wait_ge(inv_done, k + 1)
                    v.tensor_tensor(Einv[:, t, :], Einv[:, t, :], PS[:, 2 + k % 2, :], ALU.subtract)
                    if k < 4 * (LEVELS - 1):
                        v.tensor_tensor(Dinv[:, t, :], Dinv[:, t, :], PS[:, 4 + k % 2, :], ALU.subtract)
                    dve.drain().then_inc(inv_stored, 1)
                stage_end(dve, l, S_INV)
                for t in range(NT):
                    dve.wait_ge(uw_done, t + 1)
                    v.tensor_copy(w_T[:, :, t * P:(t + 1) * P], heads(4 + t))
                v.memset(state[:, 0, :], 0.0)
                dve.drain().then_inc(state_ready, 1)
                stage_end(dve, l, S_UW)
                for n in range(SEQ // CH):
                    t, r0 = n // 2, (n % 2) * CH
                    rows = slice(r0, r0 + CH)
                    dve.wait_ge(ws_done, n + 1)
                    v.tensor_tensor(v_new[rows, n % 2, :], u_tok[rows, t, :], PS[rows, n % 2, :], ALU.subtract).then_inc(vnew_ready, 1)
                    dve.wait_ge(chunk_done, 2 * n + 1)
                    if n:
                        dve.wait_ge(chunk_done, 2 * n)
                    for h in range(GH):
                        hs = slice(h * P, (h + 1) * P)
                        last = v.scalar_tensor_tensor(state[:, (n + 1) % 2, hs], state[:, n % 2, hs], glast[:, h, n:n + 1],
                                                      PS[:, 2 + n % 2, hs], ALU.mult, ALU.add)
                    dve.drain().then_inc(state_ready, 1)
                stage_end(dve, l, S_SCAN)

                def apply_o(i, k):
                    v.scalar_tensor_tensor(yT[:, i, :], o_T[:, i, :], pcol("gdn_out"), tmp[:, 2 + k % 2, :], ALU.mult, ALU.mult)
                    dve.drain()
                    v.tensor_tensor(yT[:, i, :], yT[:, i, :], raw[:, 12 + i, 3:RW], ALU.mult).then_inc(normed, 1)

                norm_items(16, [o_T[:, i, :] for i in range(4)], apply_o, tmp[:, 0:2, :])
                stage_end(dve, l, S_ONORM)

                def fox_close(t):
                    v.reciprocal(rinv[:, t * FH:(t + 1) * FH], rsum[:, t * FH:(t + 1) * FH])
                    dve.drain()
                    dve.wait_ge(pv_done, (t + 1) * FH)
                    if t >= 2:
                        dve.wait_ge(ot_done, t - 1)
                    v.tensor_tensor(tmp[:, 4 + t % 2, :].rearrange("p (h n) -> p h n", n=FD),
                                    PS[:, 4 + t % 2, :].rearrange("p (h n) -> p h n", n=FD),
                                    along(rinv[:, t * FH:(t + 1) * FH], FD), ALU.mult).then_inc(o_ready, 1)

                for i in range(NT * FH):
                    t, h = i // FH, i % FH
                    n = (t + 1) * P
                    s_i = tmp[:, 6 + i % 2, :]
                    dve.wait_ge(att_done, i + 1)
                    if i >= 2:
                        dve.wait_ge(exp_ready, i - 1)
                    v.tensor_scalar(s_i[:, 0:n], PS[:, i % 2, 0:n], ccol[:, i:i + 1], None, ALU.add)
                    dve.drain()
                    v.tensor_tensor(s_i[:, n - P:n], s_i[:, n - P:n], causal, ALU.add)
                    dve.drain()
                    v.tensor_reduce(nmax[:, i:i + 1], s_i[:, 0:n], AX.X, ALU.max, negate=True).then_inc(max_ready, 1)
                    if h == FH - 1:
                        dve.wait_ge(exp_ready, i + 1)
                        fox_close(t)
                stage_end(dve, l, S_FOX)
                add_residual(0)
                stage_end(dve, l, S_OUT1)
                norm(NT, X, NT, "xattn", hT)
                norm(2 * NT, memx, MT, "mem", memT)
                stage_end(dve, l, S_NORM2)
                stage_end(dve, l, S_XPROJ)

                def x_square(i):
                    k = 20 + i
                    src = (qx if i < MH else kx)[:, 2 * (i % MH):2 * (i % MH) + 2, :]
                    n = SEQ if i < MH else MEM
                    if i >= 2:
                        dve.wait_ge(ss_done, k - 1)
                    v.tensor_tensor(xtmp[:, 2 * (k % 2):2 * (k % 2) + 2, 0:n], src, src, ALU.mult).then_inc(sq_ready, 1)

                x_square(0)
                for i in range(2 * MH):
                    k = 20 + i
                    n = SEQ if i < MH else MEM
                    if i + 1 < 2 * MH:
                        x_square(i + 1)
                    dve.wait_ge(rs_ready, k + 1)
                    for e in range(2):
                        t_e = (qx if i < MH else kx)[:, 2 * (i % MH) + e, :]
                        last = v.scalar_tensor_tensor(t_e, t_e, pcol("mq" if i < MH else "mk", e), xtmp[:, 4 + k % 2, 0:n], ALU.mult, ALU.mult)
                    dve.drain().then_inc(normed, 1)
                stage_end(dve, l, S_XNORM)
                FI = NT * FH

                def mem_normalise(i):
                    dve.wait_ge(exp_ready, FI + i + 1)
                    v.reciprocal(rinv[:, i:i + 1], rsum[:, i:i + 1])
                    dve.drain()
                    v.tensor_scalar(xtmp[:, i % 2, 0:MEM], xtmp[:, i % 2, 0:MEM], rinv[:, i:i + 1], None, ALU.mult).then_inc(prob_ready, 1)

                for i in range(NT * MH):
                    dve.wait_ge(att_done, FI + i + 1)
                    v.tensor_reduce(nmax[:, i:i + 1], PS[:, i % 2, 0:MEM], AX.X, ALU.max, negate=True)
                    dve.drain()
                    v.tensor_scalar(nmax[:, i:i + 1], nmax[:, i:i + 1], (2 * P) ** -0.5, None, ALU.mult).then_inc(max_ready, 1)
                    mem_normalise(i)
                stage_end(dve, l, S_XATT)
                add_residual(8)
                stage_end(dve, l, S_OUT2)
                norm(2 * NT + MT, X, NT, "ffn", hT)
                stage_end(dve, l, S_NORM3)
                for c in range(DC):
                    dve.wait_ge(h_parts, c + 1)
                    v.tensor_tensor(h_lo[:, c, :], hT[:, c, :], h_hi[:, c, :].bitcast(f32), ALU.subtract)
                stage_end(dve, l, S_PQ)

                def top16(values, scratch, best_v, best_i):
                    v.max(best_v[:, 0:8], values)
                    dve.drain()
                    v.match_replace(scratch, best_v[:, 0:8], values, NEG)
                    v.max_index(best_i[:, 0:8], best_v[:, 0:8], values)
                    dve.drain()
                    v.max(best_v[:, 8:16], scratch)
                    dve.drain()
                    v.max_index(best_i[:, 8:16], best_v[:, 8:16], scratch)

                for t in range(NT):
                    for k in range(16):
                        top16(scores[:, t, k * P:(k + 1) * P], rest[:, k % 4, :], top[:, k, :], topi[:, k, :])
                    dve.drain()
                    v.tensor_copy(topf[:], topi[:])
                    for h in range(PH):
                        v.tensor_tensor(cand.rearrange("p (a b) -> p a b", b=TOPK), along(top[:, 2 * h, :], TOPK),
                                        over(top[:, 2 * h + 1, :], TOPK), ALU.add)
                        dve.drain()
                        top16(cand, cand2, best[:, h, :], besti[:, h, :])
                    dve.drain()
                    flat = besti[:].rearrange("p h k -> p (h k)")
                    v.tensor_scalar(digits[:, 0, :], flat, 4, None, ALU.logical_shift_right)
                    v.tensor_scalar(digits[:, 1, :], flat, 15, None, ALU.bitwise_and)
                    if t:
                        dve.wait_ge(pickT_done, t)
                    v.tensor_tensor(picked[:, 2, :].rearrange("p (h k) -> p h k", k=TOPK), best[:], 
                                    best[:, :, 0:1].to_broadcast([P, PH, TOPK]), ALU.subtract)
                    dve.drain().then_inc(gate_diff, 1)
                    v.tensor_copy(digitf[:], digits[:])
                    dve.drain()
                    for side in range(2):
                        hot = scores[:, t, :].rearrange("p (k a) -> p k a", a=TOPK)
                        v.tensor_tensor(hot, along(digitf[:, side, :], TOPK), over(iota[:, 0:TOPK], P), ALU.is_equal)
                        dve.drain()
                        for h in range(PH):
                            v.tensor_tensor(hot[:, h * TOPK:(h + 1) * TOPK, :], hot[:, h * TOPK:(h + 1) * TOPK, :],
                                            over(topf[:, 2 * h + side, :], TOPK), ALU.mult)
                        dve.drain()
                        v.tensor_reduce(picked[:, side, :], hot, AX.X, ALU.add)
                        dve.drain()
                    dve.wait_ge(gate_exp, t + 1)
                    gate = picked[:, 2, :].rearrange("p (h k) -> p h k", k=TOPK)
                    v.tensor_reduce(rsum[:, 0:PH], gate, AX.X, ALU.add)
                    dve.drain()
                    v.reciprocal(rinv[:, 0:PH], rsum[:, 0:PH])
                    dve.drain()
                    v.tensor_tensor(gate, gate, along(rinv[:, 0:PH], TOPK), ALU.mult)
                    dve.drain().then_inc(picks_ready, 1)
                    dve.wait_ge(pickT_stored, t + 1)
                    with v.Fori(0, HOTS // 2) as j:
                        for half in range(2):
                            dve.wait_ge(spread_done, j * 2 + (t * HOTS + half + 1))
                            for e in range(HOT):
                                tok = j * (2 * HOT) + (half * HOT + e)
                                last = v.tensor_scalar(hotA[:, half, e * P:(e + 1) * P], iota, pickT[:, 0, bass.ds(tok, 1)],
                                                       pickT[:, 2, bass.ds(tok, 1)], ALU.is_equal, ALU.mult)
                            dve.drain().then_inc(hotA_ready, 1)
                stage_end(dve, l, S_PICK)
                with v.Fori(0, SAVED // QUAD) as g:
                    def gated_acts(k):
                        fresh, r, slot = k // QUAD, k % QUAD, k % 2
                        dve.wait_ge(gate_loaded[slot], g * (16 * QUAD) + 16 * (k // 2) + 16)
                        if fresh:
                            dve.wait_ge(gelu_done, g * QUAD + (SAVED + r + 3))
                        else:
                            dve.wait_ge(saved_loaded[slot], g * (8 * QUAD) + 16 * (r // 2) + 16)
                        dve.wait_ge(wlo_ready, g * (2 * QUAD) + k + 1)
                        src = act_ring if fresh else saved_ring
                        v.tensor_tensor(wt_ring[:, slot, :], src[:, slot, :], gate_ring[:, slot, :], ALU.mult).then_inc(wt_ready, 1)

                    def low_part(k):
                        dve.wait_ge(whi_ready, g * (2 * QUAD) + k + 1)
                        v.tensor_tensor(g_lo[:, k, :], wt_ring[:, k % 2, :], g_hi[:, k, :].bitcast(f32), ALU.subtract).then_inc(wlo_ready, 1)

                    gated_acts(0)
                    for k in range(1, 2 * QUAD):
                        gated_acts(k)
                        low_part(k - 1)
                    low_part(2 * QUAD - 1)
                    for i in range(4 * NT):
                        t, half = (i % (2 * NT)) // 2, i % 2
                        dve.wait_ge(y_done, g * (4 * NT) + i + 1)
                        xs = X[:, t, half * 512:(half + 1) * 512]
                        v.tensor_tensor(xs, PS[:, 2 + i % 4, :], xs, ALU.add).then_inc(y_added, 1)
                stage_end(dve, l, S_PEER)
                layer_end(dve, l)

        @block.gpsimd
        def _(pool):
            g = nc.gpsimd
            pool.wait_ge(const_loaded, 16)
            with g.Fori(0, DEPTH) as l:
                pool.sem_inc(ulo_ready, 2)
                pool.sem_inc(vlo_ready, 2)
                stage_end(pool, l, S_NORM1)
                g.memset(raw[:, 0:12, 0:CONV_K - 1], 0.0).then_inc(pad_zeroed, 1)
                stage_end(pool, l, S_PROJ)
                stage_end(pool, l, S_PREP)
                stage_end(pool, l, S_GATES)
                for t in range(NT):
                    cols = slice(t * GH, (t + 1) * GH)

                    def grid(i):
                        return tmp[:, i, :].rearrange("p (h n) -> p h n", n=P)

                    g.tensor_tensor(grid(4), gb[:, :, t * P:(t + 1) * P], along(gcol[:, cols], P), ALU.subtract)
                    g.tensor_tensor(grid(5), over(strict, GH), along(beta[:, cols], P), ALU.mult)
                    pool.drain()
                    g.tensor_scalar(tmp[:, 0, :], tmp[:, 4, :], 0.0, None, ALU.max)
                    g.tensor_scalar(tmp[:, 1, :], tmp[:, 4, :], 0.0, None, ALU.min)
                    pool.drain().then_inc(diff_ready, 1)
                    if t:
                        pool.wait_ge(kq_used, t)
                    pool.wait_ge(decay_ready, t + 1)
                    g.tensor_tensor(tmp[:, 2, :], tmp[:, 0, :], tmp[:, 5, :], ALU.mult)
                    g.tensor_tensor(grid(3), grid(1), over(tri_chunk, GH), ALU.mult)
                    pool.drain().then_inc(mask_ready, 1)
                for h in range(GH):
                    pool.wait_ge(eg_ready, h + 1)
                    g.tensor_tensor(qd[:, h, :], conv[:, h, :], tmp[:, 6 + h % 2, :], ALU.mult).then_inc(qd_ready, 1)
                stage_end(pool, l, S_KQ)
                for k in range(4 * LEVELS):
                    t = k % 4
                    if k >= 2:
                        if k < 6:
                            pool.wait_ge(inv_stored, k - 1)
                        else:
                            pool.wait_ge(p_done, k - 5)
                    g.tensor_tensor(tmp[:, k % 2, :].rearrange("p (h n) -> p h n", n=P),
                                    A[:, t, :].rearrange("p (h n) -> p h n", n=P), over(level(k // 4), GH), ALU.mult).then_inc(lev_ready, 1)
                stage_end(pool, l, S_INV)
                for k in (S_UW, S_SCAN, S_ONORM, S_FOX):
                    stage_end(pool, l, k)
                pool.dma_start(memx[:], mem.rearrange("(t p) d -> p t d", p=P)).then_inc(mem_loaded, 16)
                for k in (S_OUT1, S_NORM2, S_XPROJ, S_XNORM, S_XATT, S_OUT2, S_NORM3):
                    stage_end(pool, l, k)
                pool.dma_start(keys_sb.rearrange("p k n -> p (k n)"), keys[bass.ds(l, 1)].rearrange("l p n -> (l p) n")).then_inc(keys_loaded, 16)
                stage_end(pool, l, S_PQ)

                def split_u(n, slot):
                    pool.wait_ge(uhi_ready, n + 3)
                    g.tensor_tensor(u_lo[:, slot, :], u_raw[:, slot, :], u_hi[:, slot, :].bitcast(f32), ALU.subtract).then_inc(ulo_ready, 1)

                for t in range(NT):
                    with g.Fori(0, (U_PER_T - U_SPREAD) // 2) as j:
                        for slot in range(2):
                            split_u(j * 2 + (t * U_PER_T + slot), slot)
                    pool.wait_ge(pickT_stored, t + 1)
                    with g.Fori(0, U_SPREAD // 2) as j:
                        for slot in range(2):
                            split_u(j * 2 + ((t + 1) * U_PER_T - U_SPREAD + slot), slot)
                            for m in range(HOTS // U_SPREAD):
                                step = j * (2 * HOTS // U_SPREAD) + (slot * (HOTS // U_SPREAD) + m)
                                pool.wait_ge(spread_done, step + (t * HOTS + 1))
                                g.tensor_copy(hot_cols[:, m % 2, :], pickT[:, 1, bass.ds(step * HOT, HOT)])
                                pool.drain()
                                for e in range(HOT):
                                    g.tensor_scalar(hotB[:, m % 2, e * P:(e + 1) * P], iota, hot_cols[:, m % 2, e:e + 1], None, ALU.is_equal)
                                pool.drain().then_inc(hotB_ready, 1)
                stage_end(pool, l, S_PICK)
                with g.Fori(0, SAVED // QUAD) as q:
                    def split_v(k):
                        pool.wait_ge(vhi_ready, q * (2 * QUAD) + k + 3)
                        g.tensor_tensor(v_lo[:, k, :], v_raw[:, k % 2, :], v_hi[:, k, :].bitcast(f32), ALU.subtract).then_inc(vlo_ready, 1)

                    for r in range(QUAD):
                        split_u(q * QUAD + (SAVED + r), r % 2)
                        if r:
                            split_v(r if r > 1 else 0)
                        if r == 1:
                            split_v(1)
                    for k in range(QUAD, 2 * QUAD):
                        split_v(k)
                stage_end(pool, l, S_PEER)
                pool.wait_ge(layer_left, 4 * l + 4)
                pool.sem_inc(layer_entered, 1)
                for s in local:
                    pool.sem_clear(s)
                pool.sem_inc(cleared, 1)


def kernel(**inputs):
    import numpy as _np
    import concourse.bacc as _bacc
    from concourse import mybir as _mybir
    from concourse.bass_utils import run_bass_kernel_spmd as _run

    a = {k: _np.asarray(v) for k, v in inputs.items()}

    def groups(w):
        n = w.shape[1] // 512
        return w.reshape(DC, P, n, 512).transpose(2, 1, 0, 3).reshape(n, P, DC * 512)

    packs, pars = [], []
    for l in range(DEPTH):
        w = a["w_in"][l]
        small = _np.zeros((D, 512), w.dtype)
        small[:, 0:8] = w[:, 2048:2056]
        small[:, 8:16] = w[:, 3592:3600]
        parts = [w[:, 0:2048], w[:, 2056:3592], small, a["w_out"][l], a["w_mq"][l], a["w_mkv"][l], a["w_mo"][l], a["w_pq"][l]]
        packs.append(_np.concatenate([groups(p) for p in parts]).reshape(N_PAIRS, 2, P, DC * 512))

        def col(v):
            return v.reshape(-1, P).T

        def row(v):
            return _np.broadcast_to(v, (P, v.shape[0]))

        conv = a["conv_w"][l][:, 0, :].reshape(CONV_K, 12, P).transpose(2, 1, 0).reshape(P, 12 * CONV_K)
        pars.append(_np.concatenate([
            col(a["mix_norm"][l]), col(a["xattn_norm"][l]), col(a["mem_norm"][l]), col(a["ffn_norm"][l]), conv,
            col(a["gdn_out_norm"][l]), col(_np.tile(a["fox_q_norm"][l], 2)), col(_np.tile(a["fox_k_norm"][l], 2)),
            col(a["mq_norm"][l]), col(a["mk_norm"][l]), row(a["dt_bias"][l]), row(a["a_log"][l]), row(a["fox_f_bias"][l])], axis=1))
    arrays = {
        "x": a["x"][0], "mem": a["mem"][0], "weights": _np.stack(packs), "params": _np.stack(pars), "consts": constants(),
        "keys": a["sub_keys"].transpose(0, 4, 2, 1, 3).reshape(DEPTH, P, 16 * P),
        "expert_u": a["expert_u"].reshape(DEPTH, NEXP_HI, P, DC, P).transpose(0, 1, 4, 3, 2).reshape(DEPTH, NEXP_HI, P, DC * P),
        "expert_v": a["expert_v"],
    }
    nc = _bacc.Bacc("TRN2", target_bir_lowering=False, num_devices=1)
    feeds, args = {}, []
    for name, v in arrays.items():
        v = _np.ascontiguousarray(v)
        feeds[f"in_{name}"] = v
        args.append(nc.dram_tensor(f"in_{name}", v.shape, _mybir.dt.from_np(v.dtype), kind="ExternalInput").ap())
    out = nc.dram_tensor("out", (SEQ, D), _mybir.dt.float32, kind="ExternalOutput").ap()
    trunk_kernel(nc, *args, out)
    r = _run(nc, [feeds], core_ids=[0])
    return r.results[0]["out"].reshape(1, SEQ, D)
```

```python
import concourse.bass as bass
import numpy as np
from concourse import mybir
from contextlib import ExitStack

P = 128
D = 1024
SEQ = 512
DEPTH = 2
NT = SEQ // P
DC = D // P
CH = 64
GH = 4
FH = 8
FD = 64
MEM = 256
MT = MEM // P
MH = 4
PH = 8
TOPK = 16
CONV_K = 4
NEXP_HI = 128
EPS = 1e-6
N_PAIRS = 11
PAIR_VS, PAIR_OUT, PAIR_MQ, PAIR_MK, PAIR_MV, PAIR_MO, PAIR_PQ = 3, 4, 5, 6, 7, 8, 9
NEG = -1e30
HOT = 4
HOTS = P // HOT
GATE_CHUNKS = 4
SAVED = 64
U_PER_T = SAVED // NT
U_SPREAD = 4
QUAD = 4

PC = {}
_at = 0
for _name, _n in (("mix", DC), ("xattn", DC), ("mem", DC), ("ffn", DC), ("conv", 12 * CONV_K), ("gdn_out", 1),
                  ("fox_q", 1), ("fox_k", 1), ("mq", 2), ("mk", 2), ("dt", GH), ("a_log", GH), ("f_bias", FH)):
    PC[_name] = _at
    _at += _n
NPAR = _at

LEVELS = 6
NROW = 24
CC = {}
_at = 0
for _name, _n in (("ident", P), ("ones", P), ("tri_chunk", P), ("tri", P), ("strict", P),
                  ("level", LEVELS * P), ("causal", P), ("iota", P), ("row", 2 * NROW - 1), ("row2", 2 * NROW - 2), ("bias", 6)):
    CC[_name] = _at
    _at += _n
NCONST = _at


def constants():
    r = np.arange(P)
    a, b = r[:, None], r[None, :]
    same = (a // CH) == (b // CH)
    c = np.zeros((P, NCONST), np.float32)

    def put(name, m):
        c[:m.shape[0], CC[name]:CC[name] + m.shape[1]] = m

    put("ident", np.eye(P))
    put("ones", np.ones((P, P)))
    put("tri_chunk", same & (a <= b))
    put("tri", a <= b)
    put("strict", same & (a > b))
    put("level", np.concatenate([(a // (2 * m) == b // (2 * m)) & (a % (2 * m) >= m) & (b % (2 * m) < m)
                                 for m in (1, 2, 4, 8, 16, 32)], axis=1))
    put("causal", np.where(b <= a, 0.0, NEG))
    put("iota", np.broadcast_to(b, (P, P)))
    put("row", np.repeat(np.arange(2 * NROW - 1)[None, :] == NROW - 1, P, axis=0))
    q = np.arange(2 * NROW - 2)[None, :]
    put("row2", np.where(a < FD, q == NROW - 2, q == NROW - 1))
    put("bias", np.broadcast_to(np.array([EPS, 0.0, 0.0, 0.0, 0.0, 0.0]), (P, 6)))
    put_rows = c[0:NROW, CC["bias"]:]
    put_rows[:, 1] = [1.0] * 8 + [1.0 / FD] * 16
    put_rows[:, 2] = [np.log(P ** -0.5)] * 4 + [0.0] * 4 + [np.log(FD ** -0.5)] * 8 + [0.0] * 8
    return c


def trunk_kernel(nc, x, mem, weights, params, consts, keys, expert_u, expert_v, out):
    f32, u32 = mybir.dt.float32, mybir.dt.uint32
    ALU, ACT, AX = mybir.AluOpType, mybir.ActivationFunctionType, mybir.AxisListType
    f32r = mybir.dt.float32r
    gates_dram = nc.dram_tensor("gates_dram", (NEXP_HI, P, SEQ), f32, kind="Internal").ap()
    acts_dram = nc.dram_tensor("acts_dram", (SAVED, P, SEQ), f32, kind="Internal").ap()

    ctx = ExitStack()
    with ctx:
        def sb(name, shape, dt=f32):
            return ctx.enter_context(nc.sbuf_tensor(name, shape, dt))

        def sem(name):
            return ctx.enter_context(nc.semaphore(name))

        X = sb("X", [P, NT, D])
        ARENA = 45096
        WRING = ARENA - 2 * DC * 512
        HT = WRING - DC * SEQ
        base = nc.sbuf_base
        assert base % 32 == 0
        sb("arena", [P, ARENA])
        par = sb("par", [P, NPAR])
        cst = sb("cst", [P, NCONST])
        stats = sb("stats", [P, 256])
        PS = ctx.enter_context(nc.psum_tensor("PS", [P, 8, 512], f32))

        ident = cst[:, CC["ident"]:CC["ident"] + P]
        ones = cst[:, CC["ones"]:CC["ones"] + P]
        tri_chunk = cst[:, CC["tri_chunk"]:CC["tri_chunk"] + P]
        tri = cst[:, CC["tri"]:CC["tri"] + P]
        strict = cst[:, CC["strict"]:CC["strict"] + P]
        causal = cst[:, CC["causal"]:CC["causal"] + P]
        iota = cst[:, CC["iota"]:CC["iota"] + P]
        eps_col = cst[:, CC["bias"]:CC["bias"] + 1]
        row_scale, row_bias = (cst[0:NROW, CC["bias"] + i:CC["bias"] + i + 1] for i in (1, 2))
        zero_col = cst[:, CC["bias"] + 3:CC["bias"] + 4]

        def level(i):
            return cst[:, CC["level"] + i * P:CC["level"] + (i + 1) * P]

        def sel(h, rows, n=P):
            return ident[0:rows, h:h + 1].to_broadcast([rows, n])

        def to_row(i):
            return cst[:, CC["row"] + NROW - 1 - i:CC["row"] + 2 * NROW - 1 - i]

        def to_rows(i):
            return cst[:, CC["row2"] + NROW - 2 - i:CC["row2"] + 2 * NROW - 2 - i]

        def pcol(name, i=0):
            return par[:, PC[name] + i:PC[name] + i + 1]

        def area(name, offset, *dims, dt=f32):
            n = int(np.prod(dims))
            assert offset + n <= ARENA, (name, offset, dims)
            return nc.alloc_sbuf_tensor_at(name, [P, *dims], dt, offset=base + 4 * offset)[:]

        def area_r(name, offset, *dims):
            return area(name, offset, *dims, dt=f32r)

        def along(v, n):
            a = v.shape[1]
            return v.rearrange("p (a o) -> p a o", o=1).to_broadcast([P, a, n])

        def over(v, n):
            b = v.shape[1]
            return v.rearrange("p (o b) -> p o b", o=1).to_broadcast([P, n, b])

        def heads(bank):
            return PS[:, bank, :].rearrange("p (h n) -> p h n", n=P)

        hT = area("hT", HT, DC, SEQ)
        wring = area("wring", WRING, 2, DC, 512)
        hn = area("hn", HT - 3 * D, 2, D)
        junk = area("junk", HT - D, D)
        RW = SEQ + CONV_K - 1
        raw = area("raw", 0, 24, RW)
        o = 24 * RW
        conv = area("conv", o, 12, SEQ); o += 12 * SEQ
        fox_v = area("fox_v", o, NT, 512); o += NT * 512
        gb = area("gb", o, GH, SEQ); o += GH * SEQ
        qk_t = area("qk_t", o, NT, 512); o += NT * 512
        qd = area("qd", o, GH, SEQ); o += GH * SEQ
        tmp = area("tmp", o, 8, 512); o += 8 * 512
        small = area("small", o, NT, 16); o += NT * 16
        kbg = area("kbg", 0, NT, 512)
        kd = area("kd", NT * 512, NT, 512)
        vb = area("vb", 2 * NT * 512, NT, 512)
        A = hT[:, 0:4, :]
        Dinv = hT[:, 4:8, :]
        Einv = gb
        u_tok = conv[:, 4:8, :]
        w_T = conv[:, 8:12, :]
        o_T = kbg
        yT = hT
        state = tmp[:, 0:2, :]
        v_new = tmp[:, 2:4, :]
        rows_T = qk_t[:, 0, :]
        row_T = area("row_T", o, SEQ); o += SEQ
        crow_T = area("crow_T", o, SEQ); o += SEQ
        ss_col = stats[:, 0:14]
        rstd_col = stats[:, 14:28]
        soft = stats[:, 32:96].rearrange("p (t n) -> p t n", n=16)
        la = stats[:, 96:112]
        lf = stats[:, 112:144]
        beta = stats[:, 144:160]
        gcol = stats[:, 160:176]
        beg = stats[:, 176:192]
        esuf = stats[:, 192:208]
        ccol = stats[:, 208:240]
        glast = sb("glast", [P, GH, SEQ // CH])
        nmax = sb("nmax", [P, 32])
        rsum = sb("rsum", [P, 32])
        rinv = sb("rinv", [P, 32])
        memx = area("memx", 0, MT, D)
        memT = area("memT", 2048, DC, MEM)
        qx = area("qx", 4096, DC, SEQ)
        kx = area("kx", 8192, DC, MEM)
        vx = area("vx", 10240, MT, D)
        xtmp = area("xtmp", 12288, 8, 512)
        h_hi, h_lo = area_r("h_hi", 0, DC, SEQ), area_r("h_lo", 4096, DC, SEQ)
        qp = area("qp", 8192, 16, SEQ)
        keys_sb = area("keys_sb", 16384, 16, P)
        scores = area("scores", 18432, NT, 16 * P)
        hot_own = area("hot", 8192, 2, 2, HOT * P)

        def hot(t, s):
            return hot_own[:, s] if s < 2 else scores[:, t, (s - 2) * 2 * HOT * P:(s - 1) * 2 * HOT * P].rearrange("p (k n) -> p k n", k=2)

        u_raw = area("u_raw", 10240, 2, DC * P)
        u_hi, u_lo = area_r("u_hi", 12288, 2, DC * P), area_r("u_lo", 14336, 2, DC * P)
        act_ring = area("act_ring", 16384, 2, SEQ)
        picked = area("picked", 17408, 3, P)
        digitf = area("digitf", 17792, 2, P)
        digits = area("digits", 18048, 2, P, dt=u32)
        gstage = area("gstage", 26624, NEXP_HI, P)
        rest = area("rest", 43008, 4, P)
        cand = area("cand", 43520, 2 * P)
        cand2 = area("cand2", 43776, 2 * P)
        v_raw = area("v_raw", 8192, 2, D)
        v_hi, v_lo = area_r("v_hi", 17408, 2 * QUAD, D), area_r("v_lo", 25600, 2 * QUAD, D)
        g_hi, g_lo = area_r("g_hi", 33792, 2 * QUAD, SEQ), area_r("g_lo", 37888, 2 * QUAD, SEQ)
        gate_ring = area("gate_ring", 41984, 2, SEQ)
        saved_ring = area("saved_ring", 43008, 2, SEQ)
        wt_ring = area("wt_ring", 44032, 2, SEQ)
        top = sb("top", [P, 16, TOPK])

        topi = sb("topi", [P, 16, TOPK], u32)
        topf = sb("topf", [P, 16, TOPK])
        best = sb("best", [P, PH, TOPK])
        besti = sb("besti", [P, PH, TOPK], u32)
        pickT = sb("pickT", [P, 3, P])

        x_loaded, const_loaded, out_stored = sem("x_loaded"), sem("const_loaded"), sem("out_stored")
        par_loaded, mem_loaded, keys_loaded = sem("par_loaded"), sem("mem_loaded"), sem("keys_loaded")
        w_loaded = [sem("w_loaded0"), sem("w_loaded1")]
        w_free = [sem("w_free0"), sem("w_free1")]
        layer_left, cleared, layer_entered = sem("layer_left"), sem("cleared"), sem("layer_entered")
        local = []

        def lsem(name):
            s = sem(name)
            local.append(s)
            return s

        stage_done = lsem("stage_done")
        rstd_ready, hn_ready, transposed, gained = lsem("rstd_ready"), lsem("hn_ready"), lsem("transposed"), lsem("gained")
        pad_zeroed, proj_done, raw_stored, conv_done = lsem("pad_zeroed"), lsem("proj_done"), lsem("raw_stored"), lsem("conv_done")
        silu_done = lsem("silu_done")
        softarg, softexp, gate_cols = lsem("softarg"), lsem("softexp"), lsem("gate_cols")
        sq_ready, ss_done, rs_ready, normed = lsem("sq_ready"), lsem("ss_done"), lsem("rs_ready"), lsem("normed")
        cums_done, cums_stored, cols_ready = lsem("cums_done"), lsem("cums_stored"), lsem("cols_ready")
        gb_done, gb_stored = lsem("gb_done"), lsem("gb_stored")
        kq_done, kq_used, diff_ready, decay_ready, mask_ready = (lsem("kq_done"), lsem("kq_used"), lsem("diff_ready"),
                                                                 lsem("decay_ready"), lsem("mask_ready"))
        eg_ready, qd_ready = lsem("eg_ready"), lsem("qd_ready")
        lev_ready, lev_used, p_done, p_stored = lsem("lev_ready"), lsem("lev_used"), lsem("p_done"), lsem("p_stored")
        inv_done, inv_stored = lsem("inv_done"), lsem("inv_stored")
        uw_done, u_stored, w_stored = lsem("uw_done"), lsem("u_stored"), lsem("w_stored")
        state_zero, ws_done, vnew_ready = lsem("state_zero"), lsem("ws_done"), lsem("vnew_ready")
        chunk_done, state_ready, o_stored = lsem("chunk_done"), lsem("state_ready"), lsem("o_stored")
        att_done, max_ready, exp_ready, prob_ready = lsem("att_done"), lsem("max_ready"), lsem("exp_ready"), lsem("prob_ready")
        pt_done, pt_stored, pv_done, o_ready = lsem("pt_done"), lsem("pt_stored"), lsem("pv_done"), lsem("o_ready")
        ot_done, ot_stored = lsem("ot_done"), lsem("ot_stored")
        gemm_done, added = lsem("gemm_done"), lsem("added")
        xg_done, xg_stored = lsem("xg_done"), lsem("xg_stored")
        sc_done, sc_stored = lsem("sc_done"), lsem("sc_stored")
        gate_diff, gate_exp, picks_ready, pickT_done, pickT_stored = (lsem("gate_diff"), lsem("gate_exp"), lsem("picks_ready"),
                                                                      lsem("pickT_done"), lsem("pickT_stored"))
        h_parts = lsem("h_parts")
        hot_ready, spread_done, spread_stored = lsem("hot_ready"), lsem("spread_done"), lsem("spread_stored")
        bc_done = lsem("bc_done")
        gates_out = lsem("gates_out")
        act_saved = [lsem("act_saved0"), lsem("act_saved1")]
        u_loaded = [lsem("u_loaded0"), lsem("u_loaded1")]
        v_loaded = [lsem("v_loaded0"), lsem("v_loaded1")]
        gate_loaded = [lsem("gate_loaded0"), lsem("gate_loaded1")]
        saved_loaded = [lsem("saved_loaded0"), lsem("saved_loaded1")]
        uhi_ready, ulo_ready, vhi_ready, vlo_ready = lsem("uhi_ready"), lsem("ulo_ready"), lsem("vhi_ready"), lsem("vlo_ready")
        act_done, gelu_done, wt_ready, whi_ready, wlo_ready = (lsem("act_done"), lsem("gelu_done"), lsem("wt_ready"),
                                                               lsem("whi_ready"), lsem("wlo_ready"))
        half_free = [lsem("saved_half_free"), lsem("fresh_half_free")]
        y_done, y_added = lsem("y_done"), lsem("y_added")

        (S_NORM1, S_PROJ, S_PREP, S_GATES, S_KQ, S_INV, S_UW, S_SCAN, S_ONORM, S_FOX, S_OUT1, S_NORM2, S_XPROJ, S_XNORM,
         S_XATT, S_OUT2, S_NORM3, S_PQ, S_PICK, S_PEER) = range(20)

        def stage_end(eng, l, k):
            eng.drain().then_inc(stage_done, 1)
            eng.wait_ge(stage_done, 4 * (k + 1))

        def layer_end(eng, l):
            eng.sem_inc(layer_left, 1)
            eng.wait_ge(cleared, l + 1)
            eng.sem_inc(layer_entered, 1)

        SCORE_BANKS = (0, 1, 7)

        block = ctx.enter_context(nc.Block())

        @block.sync
        def _(sp):
            sp.dma_start(X[:], x.rearrange("(t p) d -> p t d", p=P)).then_inc(x_loaded, 16)
            with nc.sync.Fori(0, DEPTH) as l:
                w_layer = weights[bass.ds(l, 1)].rearrange("l q s p n -> (l q) s p n")
                with nc.sync.Fori(0, N_PAIRS) as q:
                    for s in range(2):
                        sp.wait_ge(w_free[s], l * N_PAIRS + q + 1)
                        sp.dma_start(wring[:, s].rearrange("p c n -> p (c n)"),
                                     w_layer[bass.ds(q, 1), s].rearrange("q p n -> (q p) n")).then_inc(w_loaded[s], 16)
                u_layer = expert_u[bass.ds(l, 1)].rearrange("l i p n -> (l i) p n")
                v_layer = expert_v[bass.ds(l, 1)].rearrange("l (i p) n -> p (l i) n", p=P)

                def load_u(n, slot):
                    sp.wait_ge(uhi_ready, n + 1)
                    sp.wait_ge(ulo_ready, n + 1)
                    sp.dma_start(u_raw[:, slot], u_layer[bass.ds(n, 1)].rearrange("i p n -> (i p) n")).then_inc(u_loaded[slot], 16)

                sp.wait_ge(stage_done, 4 * (S_PQ + 1))
                with nc.sync.Fori(0, SAVED // 2) as j:
                    for slot in range(2):
                        load_u(j * 2 + slot, slot)
                sp.wait_ge(stage_done, 4 * (S_PICK + 1))
                with nc.sync.Fori(0, SAVED // QUAD) as g:
                    for k in range(2 * QUAD):
                        fresh, r, slot = k // QUAD, k % QUAD, k % 2
                        if not fresh:
                            load_u(g * QUAD + (SAVED + r), r % 2)
                        tile = g * QUAD + (SAVED * fresh + r)
                        sp.wait_ge(vhi_ready, g * (2 * QUAD) + k + 1)
                        sp.wait_ge(vlo_ready, g * (2 * QUAD) + k + 1)
                        sp.dma_start(v_raw[:, slot], v_layer[:, bass.ds(tile, 1), :].rearrange("p o n -> p (o n)")).then_inc(v_loaded[slot], 16)
                        sp.wait_ge(wt_ready, g * (2 * QUAD) + k + 1)
                        sp.dma_start(gate_ring[:, slot], gates_dram[bass.ds(tile, 1)].rearrange("i p n -> (i p) n")).then_inc(gate_loaded[slot], 16)
                        if not fresh:
                            sp.dma_start(saved_ring[:, slot], acts_dram[bass.ds(tile, 1)].rearrange("i p n -> (i p) n")).then_inc(saved_loaded[slot], 16)
                sp.wait_ge(stage_done, 4 * (S_PEER + 1))
                layer_end(sp, l)
            sp.dma_start(out.rearrange("(t p) d -> p t d", p=P), X[:]).then_inc(out_stored, 16)
            sp.wait_ge(out_stored, 16)

        @block.tensor
        def _(pe):
            mm = nc.tensor.matmul

            def weights_ready(l, q, s):
                pe.wait_ge(w_loaded[s], l * (16 * N_PAIRS) + 16 * (q + 1))

            def norm_transposes(base, tiles):
                for t in range(tiles):
                    k = base + t
                    pe.wait_ge(hn_ready, k + 1)
                    if t >= 2:
                        pe.wait_ge(gained, k - 1)
                    for c in range(DC):
                        last = nc.tensor.transpose(PS[:, 2 * (k % 2) + c // 4, (c % 4) * P:(c % 4 + 1) * P],
                                                   hn[:, k % 2, c * P:(c + 1) * P], ident)
                    last.then_inc(transposed, 1)

            def channel_tile(bank, s, m, src, n, done):
                for c in range(DC):
                    last = mm(PS[:, bank, 0:n], wring[:, s, c, m * P:(m + 1) * P], src[:, c, 0:n], start=c == 0, stop=c == DC - 1)
                last.then_inc(done, 1)
                return last

            def token_tile(bank_ap, s, src, t, cols, done):
                for c in range(DC):
                    last = mm(bank_ap, src[:, c, t * P:(t + 1) * P], wring[:, s, c, 0:cols], start=c == 0, stop=c == DC - 1)
                last.then_inc(done, 1)
                return last

            def out_projection(l, q, n0):
                for s in range(2):
                    weights_ready(l, q, s)
                    for t in range(NT):
                        token_tile(PS[:, s * NT + t, :], s, yT, t, 512, gemm_done)
                    pe.drain().then_inc(w_free[s], 1)

            def row_sums(base, lhsTs, squares):
                for i, lhsT in enumerate(lhsTs):
                    pe.wait_ge(sq_ready, base + i + 1)
                    mm(PS[0:NROW, 0, :], lhsT, squares[:, (base + i) % 2, :], start=i == 0, stop=i == len(lhsTs) - 1).then_inc(ss_done, 1)

            def spread_rows(base, rs_count, heads_of, rows, n=SEQ):
                pe.wait_ge(rs_ready, rs_count)
                for i, lhsTs in enumerate(heads_of):
                    k = base + i
                    if i >= 4:
                        pe.wait_ge(normed, k - 3)
                    part = P // len(lhsTs)
                    for half, lhsT in enumerate(lhsTs):
                        last = mm(PS[half * part:(half + 1) * part, 2 + i % 4, 0:n], lhsT, rows[:, 0:n], start=True, stop=True)
                    last.then_inc(bc_done, 1)

            pe.wait_ge(const_loaded, 16)
            for s in range(2):
                pe.sem_inc(w_free[s], 1)
            with nc.tensor.Fori(0, DEPTH) as l:
                pe.sem_inc(act_done, 2)
                pe.sem_inc(spread_done, 4)
                pe.sem_inc(half_free[0], 1)
                pe.sem_inc(half_free[1], 1)
                norm_transposes(0, NT)
                stage_end(pe, l, S_NORM1)
                with nc.tensor.Fori(0, 3) as q:
                    for s in range(2):
                        weights_ready(l, q, s)
                        for m in range(4):
                            pe.wait_ge(raw_stored, q * 8 + s * 4 + m + 1)
                            channel_tile(s * 4 + m, s, m, hT, SEQ, proj_done)
                        pe.drain().then_inc(w_free[s], 1)
                weights_ready(l, PAIR_VS, 0)
                pe.wait_ge(raw_stored, 8 + 16 + 4)
                for t in range(NT):
                    token_tile(PS[:, t, :], 0, hT, t, 512, proj_done)
                pe.drain().then_inc(w_free[0], 1)
                weights_ready(l, PAIR_VS, 1)
                pe.wait_ge(raw_stored, 8 + 16 + 5)
                for t in range(NT):
                    token_tile(PS[:, 4, t * 16:(t + 1) * 16], 1, hT, t, 16, proj_done)
                pe.drain().then_inc(w_free[1], 1)
                stage_end(pe, l, S_PROJ)
                row_sums(0, [to_row(i) for i in range(8)] + [to_rows(8 + 2 * i) for i in range(8)], tmp[:, 0:2, :])
                spread_rows(0, 1, [[sel(i, NROW)] for i in range(8)]
                            + [[sel(8 + 2 * i + half, NROW, FD) for half in range(2)] for i in range(8)], rows_T[0:NROW, :])
                stage_end(pe, l, S_PREP)
                pe.wait_ge(gate_cols, 1)
                for t in range(NT):
                    la_t, lf_t = la[:, t * GH:(t + 1) * GH], lf[:, t * FH:(t + 1) * FH]
                    mm(PS[:, 0, t * GH:(t + 1) * GH], tri_chunk, la_t, start=True, stop=True)
                    mm(PS[:, 1, t * GH:(t + 1) * GH], strict, la_t, start=True, stop=True)
                    mm(PS[0:GH, 2, t * P:(t + 1) * P], la_t, tri_chunk, start=True, stop=True)
                    for e in range(t + 1):
                        lf_e = lf[:, e * FH:(e + 1) * FH]
                        mm(PS[:, 3, t * FH:(t + 1) * FH], tri if e == t else ones, lf_e, start=e == 0, stop=e == t)
                    for e in range(t + 1):
                        lf_e = lf[:, e * FH:(e + 1) * FH]
                        last = mm(PS[0:FH, 4, t * P:(t + 1) * P], lf_e, tri if e == t else ones, start=e == 0, stop=e == t)
                last.then_inc(cums_done, 1)
                pe.wait_ge(cums_stored, 1)
                for h in range(GH):
                    bank = 5 + h % 3
                    if h >= 3:
                        pe.wait_ge(gb_stored, h - 2)
                    mm(PS[:, bank, :], sel(h, GH), row_T[0:GH, :], start=True, stop=True).then_inc(gb_done, 1)
                stage_end(pe, l, S_GATES)
                for t in range(NT):
                    b = 4 * (t % 2)
                    if t >= 2:
                        pe.wait_ge(kq_used, t - 1)
                    ts = slice(t * P, (t + 1) * P)
                    for h in range(GH):
                        hs = slice(h * P, (h + 1) * P)
                        q_h, k_h, v_h = conv[:, h, ts], conv[:, 4 + h, ts], conv[:, 8 + h, ts]
                        mm(PS[:, b, hs], k_h, k_h, start=True, stop=True)
                        mm(PS[:, b + 1, hs], k_h, q_h, start=True, stop=True)
                        nc.tensor.transpose(PS[:, b + 2, hs], k_h, ident)
                        last = nc.tensor.transpose(PS[:, b + 3, hs], v_h, ident)
                    last.then_inc(kq_done, 1)
                stage_end(pe, l, S_KQ)
                def first_level(t):
                    pe.wait_ge(lev_ready, t + 1)
                    if t >= 2:
                        pe.wait_ge(inv_stored, t - 1)
                    for h in range(GH):
                        last = nc.tensor.transpose(PS[:, 2 + t % 2, h * P:(h + 1) * P], tmp[:, t % 2, h * P:(h + 1) * P], ident)
                    last.then_inc(inv_done, 1)

                def level_product(k):
                    t = k % 4
                    pe.wait_ge(lev_ready, k + 1)
                    pe.wait_ge(inv_stored, k - 3)
                    if k >= 6:
                        pe.wait_ge(p_stored, k - 5)
                    for h in range(GH):
                        hs = slice(h * P, (h + 1) * P)
                        last = mm(PS[:, k % 2, hs], tmp[:, k % 2, hs], Einv[:, t, hs], start=True, stop=True)
                    last.then_inc(p_done, 1)

                for t in range(NT):
                    first_level(t)
                level_product(4)
                for k in range(4, 4 * LEVELS):
                    t = k % 4
                    if k + 1 < 4 * LEVELS:
                        level_product(k + 1)
                    pe.wait_ge(p_stored, k - 3)
                    pe.wait_ge(inv_stored, k - 1)
                    for h in range(GH):
                        hs = slice(h * P, (h + 1) * P)
                        last = mm(PS[:, 2 + k % 2, hs], Dinv[:, t, hs], tmp[:, 2 + k % 2, hs], start=True, stop=True)
                    if k < 4 * (LEVELS - 1):
                        for h in range(GH):
                            hs = slice(h * P, (h + 1) * P)
                            last = mm(PS[:, 4 + k % 2, hs], tmp[:, 2 + k % 2, hs], Dinv[:, t, hs], start=True, stop=True)
                    last.then_inc(inv_done, 1)
                stage_end(pe, l, S_INV)
                for t in range(NT):
                    for h in range(GH):
                        hs = slice(h * P, (h + 1) * P)
                        mm(PS[:, t, hs], Einv[:, t, hs], vb[:, t, hs], start=True, stop=True)
                        last = mm(PS[:, 4 + t, hs], kbg[:, t, hs], Einv[:, t, hs], start=True, stop=True)
                    last.then_inc(uw_done, 1)
                stage_end(pe, l, S_UW)
                for n in range(SEQ // CH):
                    t, r0 = n // 2, (n % 2) * CH
                    rows = slice(r0, r0 + CH)
                    cur = state[:, n % 2, :]
                    pe.wait_ge(state_ready, n + 1)
                    if n >= 2:
                        pe.wait_ge(o_stored, n - 1)
                    for h in range(GH):
                        hs = slice(h * P, (h + 1) * P)
                        last = mm(PS[:, n % 2, hs], w_T[:, h, t * P:(t + 1) * P], cur[:, hs], start=True, stop=True)
                    last.then_inc(ws_done, 1)
                    pe.wait_ge(vnew_ready, n + 1)
                    for h in range(GH):
                        hs = slice(h * P, (h + 1) * P)
                        last = mm(PS[:, 2 + n % 2, hs], kd[rows, t, hs], v_new[rows, n % 2, hs], start=True, stop=True)
                    last.then_inc(chunk_done, 1)
                    for h in range(GH):
                        hs = slice(h * P, (h + 1) * P)
                        oc = PS[:, 4 + n % 2, h * CH:(h + 1) * CH]
                        mm(oc, cur[:, hs], qd[:, h, n * CH:(n + 1) * CH], start=True, stop=False)
                        last = mm(oc, v_new[rows, n % 2, hs], qk_t[rows, t, h * P + r0:h * P + r0 + CH], start=False, stop=True)
                    last.then_inc(chunk_done, 1)
                stage_end(pe, l, S_SCAN)
                row_sums(16, [to_row(i) for i in range(GH)], tmp[:, 0:2, :])
                spread_rows(16, 2, [[sel(i, NROW)] for i in range(GH)], rows_T[0:NROW, :])
                stage_end(pe, l, S_ONORM)
                def fox_scores(i):
                    t, h = i // FH, i % FH
                    rows = slice((h % 2) * FD, (h % 2) * FD + FD)
                    n, bank = (t + 1) * P, SCORE_BANKS[i % 3]
                    if i >= 3:
                        pe.wait_ge(max_ready, i - 2)
                    mm(PS[:, bank, 0:n], raw[rows, 16 + h // 2, 3 + t * P:3 + (t + 1) * P],
                       raw[rows, 20 + h // 2, 3:3 + n], start=True, stop=False)
                    mm(PS[:, bank, 0:n], sel(h, FH), crow_T[0:FH, 0:n], start=False, stop=True).then_inc(att_done, 1)

                def fox_values(i):
                    t, h = i // FH, i % FH
                    pe.wait_ge(pt_stored, i + 1)
                    if h == 0 and t >= 2:
                        pe.wait_ge(o_ready, t - 1)
                    for j in range(t + 1):
                        last = mm(PS[:, 4 + t % 2, h * FD:(h + 1) * FD], tmp[:, 2 + i % 2, j * P:(j + 1) * P],
                                  fox_v[:, j, h * FD:(h + 1) * FD], start=j == 0, stop=j == t)
                    last.then_inc(pv_done, 1)

                def fox_output(t):
                    pe.wait_ge(o_ready, t + 1)
                    if t:
                        pe.wait_ge(ot_stored, t)
                    for c in range(4):
                        last = nc.tensor.transpose(PS[:, 6, c * P:(c + 1) * P], tmp[:, 4 + t % 2, c * P:(c + 1) * P], ident)
                    last.then_inc(ot_done, 1)

                fox_scores(0)
                fox_scores(1)
                for i in range(NT * FH):
                    t = i // FH
                    if i + 2 < NT * FH:
                        fox_scores(i + 2)
                    pe.wait_ge(exp_ready, i + 1)
                    if i >= 2:
                        pe.wait_ge(pt_stored, i - 1)
                    for j in range(t + 1):
                        last = nc.tensor.transpose(PS[:, 2 + i % 2, j * P:(j + 1) * P], tmp[:, i % 2, j * P:(j + 1) * P], ident)
                    last.then_inc(pt_done, 1)
                    if i:
                        fox_values(i - 1)
                    if i % FH == 3 and t:
                        fox_output(t - 1)
                fox_values(NT * FH - 1)
                fox_output(NT - 1)
                stage_end(pe, l, S_FOX)
                out_projection(l, PAIR_OUT, 0)
                stage_end(pe, l, S_OUT1)
                norm_transposes(NT, NT)
                norm_transposes(2 * NT, MT)
                stage_end(pe, l, S_NORM2)
                for s in range(2):
                    weights_ready(l, PAIR_MQ, s)
                    for m in range(4):
                        channel_tile(s * 4 + m, s, m, hT, SEQ, xg_done)
                    pe.drain().then_inc(w_free[s], 1)
                for s in range(2):
                    weights_ready(l, PAIR_MK, s)
                    for m in range(4):
                        pe.wait_ge(xg_stored, s * 4 + m + 1)
                        channel_tile(s * 4 + m, s, m, memT, MEM, xg_done)
                    pe.drain().then_inc(w_free[s], 1)
                for s in range(2):
                    weights_ready(l, PAIR_MV, s)
                    for m in range(MT):
                        pe.wait_ge(xg_stored, 8 + s * 2 + m + 1)
                        token_tile(PS[:, s * 2 + m, :], s, memT, m, 512, xg_done)
                    pe.drain().then_inc(w_free[s], 1)
                stage_end(pe, l, S_XPROJ)
                for i in range(2 * MH):
                    n = SEQ if i < MH else MEM
                    k = 20 + i
                    pe.wait_ge(sq_ready, k + 1)
                    for e in range(2):
                        last = mm(PS[0:NROW, i // MH, 0:n], to_row(i % MH), xtmp[:, 2 * (k % 2) + e, 0:n],
                                  start=i % MH == 0 and e == 0, stop=i % MH == MH - 1 and e == 1)
                    last.then_inc(ss_done, 1)
                spread_rows(20, 3, [[sel(i, NROW)] for i in range(MH)], xtmp[0:NROW, 4, :])
                for i in range(MH):
                    pe.wait_ge(normed, 20 + i + 1)
                    mm(PS[:, 2 + i % 4, 0:MEM], sel(i, NROW), xtmp[0:NROW, 5, 0:MEM], start=True, stop=True).then_inc(bc_done, 1)
                stage_end(pe, l, S_XNORM)

                FI = NT * FH

                def mem_scores(i):
                    t, h = i // MH, i % MH
                    if i >= 3:
                        pe.wait_ge(exp_ready, FI + i - 2)
                    for e in range(2):
                        last = mm(PS[:, SCORE_BANKS[i % 3], 0:MEM], qx[:, 2 * h + e, t * P:(t + 1) * P], kx[:, 2 * h + e, :], start=e == 0, stop=e == 1)
                    last.then_inc(att_done, 1)

                def mem_values(i):
                    t, h = i // MH, i % MH
                    pe.wait_ge(pt_stored, FI + i + 1)
                    if i >= 2:
                        pe.wait_ge(ot_stored, NT + i - 1)
                    for e in range(2):
                        for j in range(MT):
                            last = mm(PS[:, 4 + i % 2, e * P:(e + 1) * P], vx[:, j, (2 * h + e) * P:(2 * h + e + 1) * P],
                                      xtmp[:, 2 + i % 2, j * P:(j + 1) * P], start=j == 0, stop=j == MT - 1)
                    last.then_inc(ot_done, 1)

                mem_scores(0)
                mem_scores(1)
                for i in range(NT * MH):
                    if i + 2 < NT * MH:
                        mem_scores(i + 2)
                    pe.wait_ge(prob_ready, i + 1)
                    if i >= 2:
                        pe.wait_ge(pt_stored, FI + i - 1)
                    for j in range(MT):
                        last = nc.tensor.transpose(PS[:, 2 + i % 2, j * P:(j + 1) * P], xtmp[:, 6 * (i % 3 == 2) + i % 3 % 2, j * P:(j + 1) * P], ident)
                    last.then_inc(pt_done, 1)
                    if i:
                        mem_values(i - 1)
                mem_values(NT * MH - 1)
                stage_end(pe, l, S_XATT)
                out_projection(l, PAIR_MO, 8)
                stage_end(pe, l, S_OUT2)
                norm_transposes(2 * NT + MT, NT)
                stage_end(pe, l, S_NORM3)
                for q in range(2):
                    for s in range(2):
                        weights_ready(l, PAIR_PQ + q, s)
                        for m in range(4):
                            if q:
                                pe.wait_ge(xg_stored, 20 + s * 4 + m + 1)
                            channel_tile(s * 4 + m, s, m, hT, SEQ, xg_done)
                        pe.drain().then_inc(w_free[s], 1)
                pe.wait_ge(keys_loaded, l * 16 + 16)
                pe.wait_ge(xg_stored, 36)
                for t in range(NT):
                    if t >= 2:
                        pe.wait_ge(sc_stored, t - 1)
                    for k in range(16):
                        last = mm(PS[:, 4 * (t % 2) + k // 4, (k % 4) * P:(k % 4 + 1) * P], qp[:, k, t * P:(t + 1) * P], keys_sb[:, k, :],
                                  start=True, stop=True)
                    last.then_inc(sc_done, 1)
                stage_end(pe, l, S_PQ)

                def parts_product(bank_ap, a_hi, a_lo, b_hi, b_lo, first, final):
                    mm(bank_ap, a_hi, b_hi, start=first, stop=False)
                    mm(bank_ap, a_hi, b_lo, start=False, stop=False)
                    return mm(bank_ap, a_lo, b_hi, start=False, stop=final)

                def expert_acts(n, slot):
                    pe.wait_ge(uhi_ready, n + 3)
                    pe.wait_ge(ulo_ready, n + 3)
                    pe.wait_ge(gelu_done, n + 1)
                    for c in range(DC):
                        cs = slice(c * P, (c + 1) * P)
                        last = parts_product(PS[:, slot, :], u_hi[:, slot, cs], u_lo[:, slot, cs], h_hi[:, c, :], h_lo[:, c, :],
                                             c == 0, c == DC - 1)
                    last.then_inc(act_done, 1)

                for t in range(NT):
                    with nc.tensor.Fori(0, (U_PER_T - U_SPREAD) // 2) as j:
                        for slot in range(2):
                            expert_acts(j * 2 + (t * U_PER_T + slot), slot)
                    pe.wait_ge(picks_ready, t + 1)
                    for k in range(3):
                        last = nc.tensor.transpose(PS[:, 4, k * P:(k + 1) * P], picked[:, k, :], ident)
                    last.then_inc(pickT_done, 1)
                    with nc.tensor.Fori(0, U_SPREAD // 2) as j:
                        for slot in range(2):
                            expert_acts(j * 2 + ((t + 1) * U_PER_T - U_SPREAD + slot), slot)
                            for m in range(HOTS // U_SPREAD):
                                step = j * (2 * HOTS // U_SPREAD) + (t * HOTS + slot * (HOTS // U_SPREAD) + m)
                                pe.wait_ge(hot_ready, step + 1)
                                pe.wait_ge(spread_stored, step + 1)
                                for e in range(HOT):
                                    es = slice(e * P, (e + 1) * P)
                                    last = mm(PS[:, 5 + m % 2, es], hot(t, m % 4)[:, 1, es], hot(t, m % 4)[:, 0, es], start=True, stop=True)
                                last.then_inc(spread_done, 1)
                stage_end(pe, l, S_PICK)
                with nc.tensor.Fori(0, SAVED // QUAD) as g:
                    for r in range(QUAD):
                        expert_acts(g * QUAD + (SAVED + r), r % 2)
                    for fresh in range(2):
                        for i in range(2 * NT):
                            t, half = i // 2, i % 2
                            pe.wait_ge(y_added, g * (4 * NT) + fresh * 2 * NT + i + 1)
                            for r in range(QUAD):
                                k = fresh * QUAD + r
                                if i == 0:
                                    pe.wait_ge(vhi_ready, g * (2 * QUAD) + k + 3)
                                    pe.wait_ge(vlo_ready, g * (2 * QUAD) + k + 3)
                                    pe.wait_ge(whi_ready, g * (2 * QUAD) + k + 1)
                                    pe.wait_ge(wlo_ready, g * (2 * QUAD) + k + 3)
                                ts, hs = slice(t * P, (t + 1) * P), slice(half * 512, (half + 1) * 512)
                                last = parts_product(PS[:, 2 + i % 4, :], g_hi[:, k, ts], g_lo[:, k, ts], v_hi[:, k, hs], v_lo[:, k, hs],
                                                     r == 0, r == QUAD - 1)
                            last.then_inc(y_done, 1)
                        pe.drain().then_inc(half_free[fresh], 1)
                stage_end(pe, l, S_PEER)
                layer_end(pe, l)

        @block.scalar
        def _(act):
            fn = nc.scalar.activation

            def rstd(base, src, tiles):
                for t in range(tiles):
                    k = base + t
                    fn(junk, src[:, t, :], ACT.Square, accum_out=ss_col[:, k:k + 1])
                    act.drain()
                    fn(rstd_col[:, k:k + 1], ss_col[:, k:k + 1], ACT.Ln, bias=eps_col, scale=1.0 / D)
                    act.drain()
                    fn(rstd_col[:, k:k + 1], rstd_col[:, k:k + 1], ACT.Exp, bias=zero_col, scale=-0.5).then_inc(rstd_ready, 1)

            def inv_norms(dst, src, scale, bias):
                fn(dst, src, ACT.Ln, bias=eps_col[0:dst.shape[0]], scale=scale)
                act.drain()
                fn(dst, dst, ACT.Exp, bias=bias, scale=-0.5)

            act.dma_start(cst[:], consts).then_inc(const_loaded, 16)
            act.wait_ge(const_loaded, 16)
            act.wait_ge(x_loaded, 16)
            with nc.scalar.Fori(0, DEPTH) as l:
                act.dma_start(par[:], params[bass.ds(l, 1)].rearrange("l p n -> (l p) n")).then_inc(par_loaded, 16)
                act.wait_ge(par_loaded, l * 16 + 16)
                act.sem_inc(raw_stored, 8)
                act.sem_inc(gelu_done, 2)
                act.sem_inc(uhi_ready, 2)
                act.sem_inc(vhi_ready, 2)
                act.sem_inc(spread_stored, 2)
                rstd(0, X, NT)
                stage_end(act, l, S_NORM1)
                with nc.scalar.Fori(0, 3) as q:
                    for b in range(8):
                        act.wait_ge(proj_done, q * 8 + b + 1)
                        fn(raw[:, bass.ds(q * 8 + b, 1), 3:RW].rearrange("p o n -> p (o n)"), PS[:, b, :], ACT.Copy).then_inc(raw_stored, 1)
                for t in range(NT):
                    act.wait_ge(proj_done, 24 + t + 1)
                    fn(fox_v[:, t, :], PS[:, t, :], ACT.Copy)
                act.wait_ge(proj_done, 24 + 2 * NT)
                fn(small.rearrange("p t n -> p (t n)"), PS[:, 4, 0:NT * 16], ACT.Copy)
                fn(raw[:, 12:16, 3:RW], raw[:, 12:16, 3:RW], ACT.Silu)
                for k in range(3):
                    act.wait_ge(conv_done, 4 * (k + 1))
                    fn(conv[:, 4 * k:4 * (k + 1), :], conv[:, 4 * k:4 * (k + 1), :], ACT.Silu)
                stage_end(act, l, S_PROJ)
                act.wait_ge(softarg, 1)
                fn(soft[:, :, :], soft[:, :, :], ACT.Exp, bias=zero_col, scale=-1.0)
                act.drain()
                fn(soft[:, :, 0:4], soft[:, :, 0:4], ACT.Ln, bias=1.0)
                fn(soft[:, :, 8:16], soft[:, :, 8:16], ACT.Ln, bias=1.0)
                fn(nmax[:, 0:GH], par[:, PC["a_log"]:PC["a_log"] + GH], ACT.Exp)
                act.drain().then_inc(softexp, 1)
                act.wait_ge(ss_done, 16)
                inv_norms(rows_T[0:NROW, :], PS[0:NROW, 0, :], row_scale, row_bias)
                act.drain().then_inc(rs_ready, 1)
                stage_end(act, l, S_PREP)
                act.wait_ge(cums_done, 1)
                fn(row_T[0:GH, :], PS[0:GH, 2, :], ACT.Copy)
                fn(crow_T[0:FH, :], PS[0:FH, 4, :], ACT.Copy, scale=-1.0)
                act.drain().then_inc(cums_stored, 1)
                fn(beg, PS[:, 0, 0:16], ACT.Exp)
                fn(esuf, PS[:, 1, 0:16], ACT.Exp)
                fn(gcol, PS[:, 0, 0:16], ACT.Copy)
                fn(ccol, PS[:, 3, 0:32], ACT.Copy)
                act.drain().then_inc(cols_ready, 1)
                for h in range(GH):
                    act.wait_ge(gb_done, h + 1)
                    fn(gb[:, h, :], PS[:, 5 + h % 3, :], ACT.Copy)
                    fn(tmp[:, h % 2 + 0, :], PS[:, 5 + h % 3, :], ACT.Exp) if False else None
                    act.drain().then_inc(gb_stored, 1)
                fn(glast[:, :, :], gb[:, :, CH - 1:SEQ:CH], ACT.Exp)
                stage_end(act, l, S_GATES)
                for t in range(NT):
                    act.wait_ge(diff_ready, t + 1)
                    fn(tmp[:, 0, :], tmp[:, 0, :], ACT.Exp, bias=zero_col, scale=-1.0)
                    fn(tmp[:, 1, :], tmp[:, 1, :], ACT.Exp)
                    act.drain().then_inc(decay_ready, 1)
                for h in range(GH):
                    if h >= 2:
                        act.wait_ge(qd_ready, h - 1)
                    fn(tmp[:, 6 + h % 2, :], gb[:, h, :], ACT.Exp).then_inc(eg_ready, 1)
                stage_end(act, l, S_KQ)
                for k in range(4, 4 * LEVELS):
                    act.wait_ge(p_done, k - 3)
                    if k >= 6:
                        act.wait_ge(inv_done, k - 1)
                    fn(tmp[:, 2 + k % 2, :], PS[:, k % 2, :], ACT.Copy).then_inc(p_stored, 1)
                stage_end(act, l, S_INV)
                for t in range(NT):
                    act.wait_ge(uw_done, t + 1)
                    fn(u_tok[:, t, :], PS[:, t, :], ACT.Copy)
                stage_end(act, l, S_UW)
                for n in range(SEQ // CH):
                    act.wait_ge(chunk_done, 2 * n + 2)
                    fn(o_T.rearrange("p h n -> p h n")[:, :, n * CH:(n + 1) * CH],
                       PS[:, 4 + n % 2, 0:GH * CH].rearrange("p (h n) -> p h n", n=CH), ACT.Copy).then_inc(o_stored, 1)
                stage_end(act, l, S_SCAN)
                act.wait_ge(ss_done, 16 + GH)
                inv_norms(rows_T[0:NROW, :], PS[0:NROW, 0, :], 1.0 / P, zero_col[0:NROW])
                act.drain().then_inc(rs_ready, 1)
                stage_end(act, l, S_ONORM)
                def fox_transposed(i):
                    n = (i // FH + 1) * P
                    act.wait_ge(pt_done, i + 1)
                    if i >= 2:
                        act.wait_ge(pv_done, i - 1)
                    fn(tmp[:, 2 + i % 2, 0:n], PS[:, 2 + i % 2, 0:n], ACT.Copy).then_inc(pt_stored, 1)

                def fox_out(t):
                    act.wait_ge(ot_done, t + 1)
                    fn(yT[:, 4:8, t * P:(t + 1) * P], heads(6), ACT.Copy).then_inc(ot_stored, 1)

                for i in range(NT * FH):
                    t, h = i // FH, i % FH
                    n = (t + 1) * P
                    act.wait_ge(max_ready, i + 1)
                    if i >= 2:
                        act.wait_ge(pt_done, i - 1)
                    fn(tmp[:, i % 2, 0:n], tmp[:, 6 + i % 2, 0:n], ACT.Exp, bias=nmax[:, i:i + 1],
                       accum_out=rsum[:, i:i + 1]).then_inc(exp_ready, 1)
                    if i:
                        fox_transposed(i - 1)
                    if i % FH == 5 and t:
                        fox_out(t - 1)
                fox_transposed(NT * FH - 1)
                fox_out(NT - 1)
                stage_end(act, l, S_FOX)
                stage_end(act, l, S_OUT1)
                rstd(NT, X, NT)
                act.wait_ge(mem_loaded, l * 16 + 16)
                rstd(2 * NT, memx, MT)
                stage_end(act, l, S_NORM2)
                for b in range(8):
                    act.wait_ge(xg_done, b + 1)
                    fn(qx[:, b, :], PS[:, b, :], ACT.Copy).then_inc(xg_stored, 1)
                for b in range(8):
                    act.wait_ge(xg_done, 8 + b + 1)
                    fn(kx[:, b, :], PS[:, b, 0:MEM], ACT.Copy).then_inc(xg_stored, 1)
                for b in range(4):
                    act.wait_ge(xg_done, 16 + b + 1)
                    fn(vx[:, b % 2, (b // 2) * 512:(b // 2 + 1) * 512], PS[:, b, :], ACT.Copy).then_inc(xg_stored, 1)
                stage_end(act, l, S_XPROJ)
                act.wait_ge(ss_done, 20 + 2 * MH)
                for i, n in enumerate((SEQ, MEM)):
                    inv_norms(xtmp[0:NROW, 4 + i, 0:n], PS[0:NROW, i, 0:n], 1.0 / (2 * P), zero_col[0:NROW])
                act.drain().then_inc(rs_ready, 1)
                stage_end(act, l, S_XNORM)
                FI = NT * FH

                def mem_transposed(i):
                    act.wait_ge(pt_done, FI + i + 1)
                    if i >= 2:
                        act.wait_ge(ot_done, NT + i - 1)
                    fn(xtmp[:, 2 + i % 2, 0:MEM], PS[:, 2 + i % 2, 0:MEM], ACT.Copy).then_inc(pt_stored, 1)

                def mem_out(i):
                    t, h = i // MH, i % MH
                    act.wait_ge(ot_done, NT + i + 1)
                    fn(yT[:, 2 * h:2 * h + 2, t * P:(t + 1) * P], PS[:, 4 + i % 2, 0:MEM].rearrange("p (e n) -> p e n", n=P),
                       ACT.Copy).then_inc(ot_stored, 1)

                n_items = NT * MH
                for i in range(n_items + 2):
                    if i < n_items:
                        act.wait_ge(max_ready, FI + i + 1)
                        if i >= 3:
                            act.wait_ge(pt_done, FI + i - 2)
                        fn(xtmp[:, 6 * (i % 3 == 2) + i % 3 % 2, 0:MEM], PS[:, SCORE_BANKS[i % 3], 0:MEM], ACT.Exp, bias=nmax[:, i:i + 1],
                           scale=(2 * P) ** -0.5, accum_out=rsum[:, i:i + 1]).then_inc(exp_ready, 1)
                    if 1 <= i <= n_items:
                        mem_transposed(i - 1)
                    if i >= 2:
                        mem_out(i - 2)
                stage_end(act, l, S_XATT)
                stage_end(act, l, S_OUT2)
                rstd(2 * NT + MT, X, NT)
                stage_end(act, l, S_NORM3)
                for b in range(16):
                    act.wait_ge(xg_done, 20 + b + 1)
                    fn(qp[:, b, :], PS[:, b % 8, :], ACT.Copy).then_inc(xg_stored, 1)
                    if b < DC:
                        fn(h_hi[:, b, :], hT[:, b, :], ACT.Copy).then_inc(h_parts, 1)
                for t in range(NT):
                    act.wait_ge(sc_done, t + 1)
                    fn(scores[:, t, :], PS[:, 4 * (t % 2):4 * (t % 2) + 4, :].rearrange("p b n -> p (b n)"), ACT.Copy).then_inc(sc_stored, 1)
                stage_end(act, l, S_PQ)

                def split_u(n, half_n, slot):
                    act.wait_ge(u_loaded[slot], half_n * 16 + 16)
                    act.wait_ge(act_done, n + 1)
                    fn(u_hi[:, slot, :], u_raw[:, slot, :], ACT.Copy).then_inc(uhi_ready, 1)

                def gelu(n, slot):
                    act.wait_ge(act_done, n + 3)
                    fn(act_ring[:, slot, :], PS[:, slot, :], ACT.Gelu_apprx_tanh).then_inc(gelu_done, 1)

                def gelu_saved(n, half_n, slot, first=False):
                    if not first:
                        act.wait_ge(act_saved[slot], half_n * 16)
                    gelu(n, slot)
                    act.wait_ge(gelu_done, n + 3)
                    act.dma_start(acts_dram[bass.ds(n, 1)].rearrange("i p n -> (i p) n"), act_ring[:, slot]).then_inc(act_saved[slot], 16)

                def acts_pair(j, first=False, second=False):
                    split_u(j * 2, j, 0)
                    if not first:
                        gelu_saved(j * 2 - 1, j - 1, 1, second)
                    split_u(j * 2 + 1, j, 1)
                    gelu_saved(j * 2, j, 0, first)

                def gates_store(t, i):
                    n = NEXP_HI // GATE_CHUNKS
                    act.dma_start(gates_dram[bass.ds(i * n, n), :, t * P:(t + 1) * P].rearrange("i j t -> j i t"),
                                  gstage[:, bass.ds(i * n, n), :]).then_inc(gates_out, 16)

                for t in range(NT):
                    j0 = t * U_PER_T // 2
                    pairs = (U_PER_T - U_SPREAD) // 2
                    if t == 0:
                        acts_pair(0, first=True)
                        acts_pair(1, second=True)
                    else:
                        with nc.scalar.Fori(0, GATE_CHUNKS) as j:
                            gates_store(t - 1, j)
                            acts_pair(j + j0)
                    with nc.scalar.Fori(2 if t == 0 else GATE_CHUNKS, pairs) as j:
                        acts_pair(j + j0)
                    act.wait_ge(gate_diff, t + 1)
                    fn(picked[:, 2, :], picked[:, 2, :], ACT.Exp).then_inc(gate_exp, 1)
                    act.wait_ge(pickT_done, t + 1)
                    fn(pickT[:, 0:3, :].rearrange("p k n -> p (k n)"), PS[:, 4, 0:3 * P], ACT.Copy).then_inc(pickT_stored, 1)
                    if t:
                        act.wait_ge(gates_out, 16 * GATE_CHUNKS * t)
                    with nc.scalar.Fori(0, U_SPREAD // 2) as j:
                        for slot in range(2):
                            jj = j + (j0 + pairs)
                            if slot == 0:
                                split_u(jj * 2, jj, 0)
                                gelu_saved(jj * 2 - 1, jj - 1, 1)
                            else:
                                split_u(jj * 2 + 1, jj, 1)
                                gelu_saved(jj * 2, jj, 0)
                            for m in range(HOTS // U_SPREAD):
                                step = j * (2 * HOTS // U_SPREAD) + (slot * (HOTS // U_SPREAD) + m)
                                act.wait_ge(spread_done, step + (t * HOTS + 5))
                                fn(gstage[:, :, bass.ds(step * HOT, HOT)],
                                   PS[:, 5 + m % 2, :].rearrange("p (e i) -> p i e", i=P), ACT.Copy).then_inc(spread_stored, 1)
                    act.wait_ge(spread_stored, 2 + (t + 1) * HOTS)
                for i in range(GATE_CHUNKS):
                    gates_store(NT - 1, i)
                gelu_saved(SAVED - 1, SAVED // 2 - 1, 1)
                act.wait_ge(gates_out, 16 * GATE_CHUNKS * NT)
                for slot in range(2):
                    act.wait_ge(act_saved[slot], 16 * SAVED // 2)
                stage_end(act, l, S_PICK)
                with nc.scalar.Fori(0, SAVED // QUAD) as g:
                    def split_v(k):
                        act.wait_ge(v_loaded[k % 2], g * (16 * QUAD) + 16 * (k // 2) + 16)
                        act.wait_ge(half_free[k // QUAD], g + 1)
                        fn(v_hi[:, k, :], v_raw[:, k % 2, :], ACT.Copy).then_inc(vhi_ready, 1)

                    def split_w(k):
                        act.wait_ge(wt_ready, g * (2 * QUAD) + k + 3)
                        act.wait_ge(half_free[k // QUAD], g + 1)
                        fn(g_hi[:, k, :], wt_ring[:, k % 2, :], ACT.Copy).then_inc(whi_ready, 1)

                    def split_fresh_u(r):
                        split_u(g * QUAD + (SAVED + r), g * (QUAD // 2) + (SAVED + r) // 2, r % 2)

                    def gelu_fresh(r):
                        act.wait_ge(wt_ready, g * (2 * QUAD) + (QUAD + r + 1 if r >= 2 else r + 1))
                        gelu(g * QUAD + (SAVED + r), r % 2)

                    split_fresh_u(0)
                    split_fresh_u(1)
                    for k in range(QUAD):
                        split_v(k)
                    gelu_fresh(0)
                    split_fresh_u(2)
                    split_w(0)
                    split_w(1)
                    gelu_fresh(1)
                    split_fresh_u(3)
                    split_w(2)
                    split_w(3)
                    split_v(4)
                    gelu_fresh(2)
                    split_w(4)
                    split_v(5)
                    split_w(5)
                    gelu_fresh(3)
                    split_v(6)
                    split_w(6)
                    split_v(7)
                    split_w(7)
                stage_end(act, l, S_PEER)
                layer_end(act, l)

        @block.vector
        def _(dve):
            v = nc.vector

            def norm(base, src, tiles, gain, dst):
                def evacuate(t):
                    k = base + t
                    dve.wait_ge(transposed, k + 1)
                    for half in range(2):
                        last = v.tensor_tensor(dst[:, 4 * half:4 * half + 4, t * P:(t + 1) * P], heads(2 * (k % 2) + half),
                                               along(par[:, PC[gain] + 4 * half:PC[gain] + 4 * half + 4], P), ALU.mult)
                    last.then_inc(gained, 1)

                for t in range(tiles):
                    k = base + t
                    dve.wait_ge(rstd_ready, k + 1)
                    if k >= 2:
                        dve.wait_ge(transposed, k - 1)
                    v.tensor_scalar(hn[:, k % 2, :], src[:, t, :], rstd_col[:, k:k + 1], None, ALU.mult).then_inc(hn_ready, 1)
                    if t:
                        evacuate(t - 1)
                evacuate(tiles - 1)

            def add_residual(base):
                for s in range(2):
                    for t in range(NT):
                        dve.wait_ge(gemm_done, base + s * NT + t + 1)
                        xs = X[:, t, s * 512:(s + 1) * 512]
                        v.tensor_tensor(xs, PS[:, s * NT + t, :], xs, ALU.add)

            def norm_items(base, items, apply, buf):
                for i, item in enumerate(items):
                    if i >= 2:
                        dve.wait_ge(ss_done, base + i - 1)
                    v.tensor_tensor(buf[:, (base + i) % 2, :], item, item, ALU.mult).then_inc(sq_ready, 1)
                for i in range(len(items)):
                    dve.wait_ge(bc_done, base + i + 1)
                    apply(i, PS[:, 2 + i % 4, :])

            dve.wait_ge(const_loaded, 16)
            dve.wait_ge(x_loaded, 16)
            with nc.vector.Fori(0, DEPTH) as l:
                dve.wait_ge(par_loaded, l * 16 + 16)
                dve.sem_inc(y_added, 4)
                dve.sem_inc(wt_ready, 2)
                dve.sem_inc(wlo_ready, 2)
                norm(0, X, NT, "mix", hT)
                stage_end(dve, l, S_NORM1)
                dve.wait_ge(pad_zeroed, 1)
                with v.Fori(0, 12) as m:
                    dve.wait_ge(raw_stored, m + 9)
                    row = raw[:, bass.ds(m, 1), :].rearrange("p o n -> p (o n)")
                    dst = conv[:, bass.ds(m, 1), :].rearrange("p o n -> p (o n)")

                    def tap(j):
                        return par[:, bass.ds(m * CONV_K + PC["conv"] + j, 1)]

                    v.tensor_scalar(dst, row[:, 0:SEQ], tap(0), None, ALU.mult)
                    for j in range(1, CONV_K):
                        dve.drain()
                        last = v.scalar_tensor_tensor(dst, row[:, j:j + SEQ], tap(j), dst, ALU.mult, ALU.add)
                    last.then_inc(conv_done, 1)
                stage_end(dve, l, S_PROJ)
                dtb = over(par[:, PC["dt"]:PC["dt"] + GH], NT)
                fbb = over(par[:, PC["f_bias"]:PC["f_bias"] + FH], NT)
                v.tensor_tensor(small[:, :, 0:4], small[:, :, 0:4], dtb, ALU.add)
                v.tensor_tensor(small[:, :, 8:16], small[:, :, 8:16], fbb, ALU.add)
                dve.drain()
                v.tensor_scalar(small[:, :, 8:16], small[:, :, 8:16], -1.0, None, ALU.mult)
                dve.drain()
                v.scalar_tensor_tensor(soft[:, :, 0:4], small[:, :, 0:4], -1.0, small[:, :, 0:4], ALU.mult, ALU.max)
                v.scalar_tensor_tensor(soft[:, :, 8:16], small[:, :, 8:16], -1.0, small[:, :, 8:16], ALU.mult, ALU.max)
                v.tensor_copy(soft[:, :, 4:8], small[:, :, 4:8])
                dve.drain().then_inc(softarg, 1)
                dve.wait_ge(softexp, 1)
                v.tensor_scalar(small[:, :, 0:4], small[:, :, 0:4], 0.0, None, ALU.max)
                v.tensor_scalar(small[:, :, 8:16], small[:, :, 8:16], 0.0, None, ALU.max)
                v.tensor_scalar(soft[:, :, 4:8], soft[:, :, 4:8], 1.0, None, ALU.add)
                dve.drain()
                v.tensor_tensor(small[:, :, 0:4], small[:, :, 0:4], soft[:, :, 0:4], ALU.add)
                v.tensor_tensor(small[:, :, 8:16], small[:, :, 8:16], soft[:, :, 8:16], ALU.add)
                v.reciprocal(beta.rearrange("p (t h) -> p t h", h=GH), soft[:, :, 4:8])
                dve.drain()
                v.tensor_tensor(small[:, :, 0:4], small[:, :, 0:4], over(nmax[:, 0:GH], NT), ALU.mult)
                v.tensor_scalar(lf.rearrange("p (t h) -> p t h", h=FH), small[:, :, 8:16], -1.0, None, ALU.mult)
                dve.drain()
                v.tensor_scalar(la.rearrange("p (t h) -> p t h", h=GH), small[:, :, 0:4], -1.0, None, ALU.mult)
                dve.drain().then_inc(gate_cols, 1)
                qk_items = [conv[:, i, :] for i in range(8)] + [raw[:, 16 + i, 3:RW] for i in range(8)]

                def apply_qk(i, rs):
                    x_i = qk_items[i]
                    if i < 8:
                        v.tensor_tensor(x_i, x_i, rs, ALU.mult).then_inc(normed, 1)
                    else:
                        v.scalar_tensor_tensor(x_i, x_i, pcol("fox_q" if i < 12 else "fox_k"), rs, ALU.mult, ALU.mult).then_inc(normed, 1)

                norm_items(0, qk_items, apply_qk, tmp[:, 0:2, :])
                stage_end(dve, l, S_PREP)
                dve.wait_ge(cols_ready, 1)
                v.tensor_tensor(beg, beg, beta, ALU.mult)
                stage_end(dve, l, S_GATES)
                for t in range(NT):
                    b = 4 * (t % 2)
                    dve.wait_ge(kq_done, t + 1)
                    cols = slice(t * GH, (t + 1) * GH)

                    def grid(a):
                        return a[:, t, :].rearrange("p (h n) -> p h n", n=P)

                    v.tensor_tensor(grid(kbg), heads(b + 2), along(beg[:, cols], P), ALU.mult)
                    v.tensor_tensor(grid(kd), heads(b + 2), along(esuf[:, cols], P), ALU.mult)
                    v.tensor_tensor(grid(vb), heads(b + 3), along(beta[:, cols], P), ALU.mult)
                    dve.wait_ge(mask_ready, t + 1)
                    v.tensor_tensor(A[:, t, :], PS[:, b, :], tmp[:, 2, :], ALU.mult)
                    v.tensor_tensor(qk_t[:, t, :], PS[:, b + 1, :], tmp[:, 3, :], ALU.mult)
                    dve.drain().then_inc(kq_used, 1)
                stage_end(dve, l, S_KQ)

                def grid_t(a, t):
                    return a[:, t, :].rearrange("p (h n) -> p h n", n=P)

                for t in range(NT):
                    dve.wait_ge(lev_ready, t + 1)
                    v.tensor_tensor(grid_t(Dinv, t), over(ident, GH), grid_t(tmp, t % 2), ALU.subtract)
                    dve.wait_ge(inv_done, t + 1)
                    v.tensor_tensor(grid_t(Einv, t), over(ident, GH), heads(2 + t % 2), ALU.subtract)
                    dve.drain().then_inc(inv_stored, 1)
                for k in range(4, 4 * LEVELS):
                    t = k % 4
                    dve.wait_ge(inv_done, k + 1)
                    v.tensor_tensor(Einv[:, t, :], Einv[:, t, :], PS[:, 2 + k % 2, :], ALU.subtract)
                    if k < 4 * (LEVELS - 1):
                        v.tensor_tensor(Dinv[:, t, :], Dinv[:, t, :], PS[:, 4 + k % 2, :], ALU.subtract)
                    dve.drain().then_inc(inv_stored, 1)
                stage_end(dve, l, S_INV)
                for t in range(NT):
                    dve.wait_ge(uw_done, t + 1)
                    v.tensor_copy(w_T[:, :, t * P:(t + 1) * P], heads(4 + t))
                v.memset(state[:, 0, :], 0.0)
                dve.drain().then_inc(state_ready, 1)
                stage_end(dve, l, S_UW)
                for n in range(SEQ // CH):
                    t, r0 = n // 2, (n % 2) * CH
                    rows = slice(r0, r0 + CH)
                    dve.wait_ge(ws_done, n + 1)
                    v.tensor_tensor(v_new[rows, n % 2, :], u_tok[rows, t, :], PS[rows, n % 2, :], ALU.subtract).then_inc(vnew_ready, 1)
                    dve.wait_ge(chunk_done, 2 * n + 1)
                    if n:
                        dve.wait_ge(chunk_done, 2 * n)
                    for h in range(GH):
                        hs = slice(h * P, (h + 1) * P)
                        last = v.scalar_tensor_tensor(state[:, (n + 1) % 2, hs], state[:, n % 2, hs], glast[:, h, n:n + 1],
                                                      PS[:, 2 + n % 2, hs], ALU.mult, ALU.add)
                    dve.drain().then_inc(state_ready, 1)
                stage_end(dve, l, S_SCAN)

                def apply_o(i, rs):
                    v.scalar_tensor_tensor(yT[:, i, :], o_T[:, i, :], pcol("gdn_out"), rs, ALU.mult, ALU.mult)
                    dve.drain()
                    v.tensor_tensor(yT[:, i, :], yT[:, i, :], raw[:, 12 + i, 3:RW], ALU.mult).then_inc(normed, 1)

                norm_items(16, [o_T[:, i, :] for i in range(4)], apply_o, tmp[:, 0:2, :])
                stage_end(dve, l, S_ONORM)

                def fox_close(t):
                    v.reciprocal(rinv[:, t * FH:(t + 1) * FH], rsum[:, t * FH:(t + 1) * FH])
                    dve.drain()
                    dve.wait_ge(pv_done, (t + 1) * FH)
                    if t >= 2:
                        dve.wait_ge(ot_done, t - 1)
                    v.tensor_tensor(tmp[:, 4 + t % 2, :].rearrange("p (h n) -> p h n", n=FD),
                                    PS[:, 4 + t % 2, :].rearrange("p (h n) -> p h n", n=FD),
                                    along(rinv[:, t * FH:(t + 1) * FH], FD), ALU.mult).then_inc(o_ready, 1)

                for i in range(NT * FH):
                    t, h = i // FH, i % FH
                    n = (t + 1) * P
                    s_i = tmp[:, 6 + i % 2, :]
                    dve.wait_ge(att_done, i + 1)
                    if i >= 2:
                        dve.wait_ge(exp_ready, i - 1)
                    v.tensor_scalar(s_i[:, 0:n], PS[:, SCORE_BANKS[i % 3], 0:n], ccol[:, i:i + 1], None, ALU.add)
                    dve.drain()
                    v.tensor_tensor(s_i[:, n - P:n], s_i[:, n - P:n], causal, ALU.add)
                    dve.drain()
                    v.tensor_reduce(nmax[:, i:i + 1], s_i[:, 0:n], AX.X, ALU.max, negate=True).then_inc(max_ready, 1)
                    if i % FH == 2 and t:
                        fox_close(t - 1)
                dve.wait_ge(exp_ready, NT * FH)
                fox_close(NT - 1)
                stage_end(dve, l, S_FOX)
                add_residual(0)
                stage_end(dve, l, S_OUT1)
                norm(NT, X, NT, "xattn", hT)
                norm(2 * NT, memx, MT, "mem", memT)
                stage_end(dve, l, S_NORM2)
                stage_end(dve, l, S_XPROJ)

                def x_square(i):
                    k = 20 + i
                    src = (qx if i < MH else kx)[:, 2 * (i % MH):2 * (i % MH) + 2, :]
                    n = SEQ if i < MH else MEM
                    if i >= 2:
                        dve.wait_ge(ss_done, k - 1)
                    v.tensor_tensor(xtmp[:, 2 * (k % 2):2 * (k % 2) + 2, 0:n], src, src, ALU.mult).then_inc(sq_ready, 1)

                for i in range(2 * MH):
                    x_square(i)
                for i in range(2 * MH):
                    n = SEQ if i < MH else MEM
                    dve.wait_ge(bc_done, 20 + i + 1)
                    for e in range(2):
                        t_e = (qx if i < MH else kx)[:, 2 * (i % MH) + e, :]
                        last = v.scalar_tensor_tensor(t_e, t_e, pcol("mq" if i < MH else "mk", e), PS[:, 2 + i % 4, 0:n], ALU.mult, ALU.mult)
                    dve.drain().then_inc(normed, 1)
                stage_end(dve, l, S_XNORM)
                FI = NT * FH

                def mem_normalise(i):
                    p_i = xtmp[:, 6 * (i % 3 == 2) + i % 3 % 2, 0:MEM]
                    dve.wait_ge(exp_ready, FI + i + 1)
                    v.reciprocal(rinv[:, i:i + 1], rsum[:, i:i + 1])
                    dve.drain()
                    v.tensor_scalar(p_i, p_i, rinv[:, i:i + 1], None, ALU.mult).then_inc(prob_ready, 1)

                for i in range(NT * MH):
                    dve.wait_ge(att_done, FI + i + 1)
                    v.tensor_reduce(nmax[:, i:i + 1], PS[:, SCORE_BANKS[i % 3], 0:MEM], AX.X, ALU.max, negate=True)
                    dve.drain()
                    v.tensor_scalar(nmax[:, i:i + 1], nmax[:, i:i + 1], (2 * P) ** -0.5, None, ALU.mult).then_inc(max_ready, 1)
                    if i:
                        mem_normalise(i - 1)
                mem_normalise(NT * MH - 1)
                stage_end(dve, l, S_XATT)
                add_residual(8)
                stage_end(dve, l, S_OUT2)
                norm(2 * NT + MT, X, NT, "ffn", hT)
                stage_end(dve, l, S_NORM3)
                for c in range(DC):
                    dve.wait_ge(h_parts, c + 1)
                    v.tensor_tensor(h_lo[:, c, :], hT[:, c, :], h_hi[:, c, :].bitcast(f32), ALU.subtract)
                stage_end(dve, l, S_PQ)

                def top16(values, scratch, best_v, best_i):
                    v.max(best_v[:, 0:8], values)
                    dve.drain()
                    v.match_replace(scratch, best_v[:, 0:8], values, NEG)
                    v.max_index(best_i[:, 0:8], best_v[:, 0:8], values)
                    dve.drain()
                    v.max(best_v[:, 8:16], scratch)
                    dve.drain()
                    v.max_index(best_i[:, 8:16], best_v[:, 8:16], scratch)

                for t in range(NT):
                    for k in range(16):
                        top16(scores[:, t, k * P:(k + 1) * P], rest[:, k % 4, :], top[:, k, :], topi[:, k, :])
                    dve.drain()
                    v.tensor_copy(topf[:], topi[:])
                    for h in range(PH):
                        v.tensor_tensor(cand.rearrange("p (a b) -> p a b", b=TOPK), along(top[:, 2 * h, :], TOPK),
                                        over(top[:, 2 * h + 1, :], TOPK), ALU.add)
                        dve.drain()
                        top16(cand, cand2, best[:, h, :], besti[:, h, :])
                    dve.drain()
                    flat = besti[:].rearrange("p h k -> p (h k)")
                    v.tensor_scalar(digits[:, 0, :], flat, 4, None, ALU.logical_shift_right)
                    v.tensor_scalar(digits[:, 1, :], flat, 15, None, ALU.bitwise_and)
                    if t:
                        dve.wait_ge(pickT_done, t)
                    v.tensor_tensor(picked[:, 2, :].rearrange("p (h k) -> p h k", k=TOPK), best[:], 
                                    best[:, :, 0:1].to_broadcast([P, PH, TOPK]), ALU.subtract)
                    dve.drain().then_inc(gate_diff, 1)
                    v.tensor_copy(digitf[:], digits[:])
                    dve.drain()
                    for side in range(2):
                        side_hot = scores[:, t, :].rearrange("p (k a) -> p k a", a=TOPK)
                        v.tensor_tensor(side_hot, along(digitf[:, side, :], TOPK), over(iota[:, 0:TOPK], P), ALU.is_equal)
                        dve.drain()
                        for h in range(PH):
                            v.tensor_tensor(side_hot[:, h * TOPK:(h + 1) * TOPK, :], side_hot[:, h * TOPK:(h + 1) * TOPK, :],
                                            over(topf[:, 2 * h + side, :], TOPK), ALU.mult)
                        dve.drain()
                        v.tensor_reduce(picked[:, side, :], side_hot, AX.X, ALU.add)
                        dve.drain()
                    dve.wait_ge(gate_exp, t + 1)
                    gate = picked[:, 2, :].rearrange("p (h k) -> p h k", k=TOPK)
                    v.tensor_reduce(rsum[:, 0:PH], gate, AX.X, ALU.add)
                    dve.drain()
                    v.reciprocal(rinv[:, 0:PH], rsum[:, 0:PH])
                    dve.drain()
                    v.tensor_tensor(gate, gate, along(rinv[:, 0:PH], TOPK), ALU.mult)
                    dve.drain().then_inc(picks_ready, 1)
                    dve.wait_ge(pickT_stored, t + 1)
                    with v.Fori(0, HOTS // 4) as j:
                        for k in range(4):
                            dve.wait_ge(spread_done, j * 4 + (t * HOTS + k + 1))
                            for e in range(HOT):
                                es = slice(e * P, (e + 1) * P)
                                hi_key, lo_key, gate_col = (pickT[:, r, bass.ds(j * (4 * HOT) + k * HOT + e, 1)] for r in range(3))
                                v.tensor_scalar(hot(t, k)[:, 0, es], iota, hi_key, gate_col, ALU.is_equal, ALU.mult)
                                last = v.tensor_scalar(hot(t, k)[:, 1, es], iota, lo_key, None, ALU.is_equal)
                            last.then_inc(hot_ready, 1)
                stage_end(dve, l, S_PICK)
                with v.Fori(0, SAVED // QUAD) as g:
                    def gated_acts(k):
                        fresh, r, slot = k // QUAD, k % QUAD, k % 2
                        dve.wait_ge(gate_loaded[slot], g * (16 * QUAD) + 16 * (k // 2) + 16)
                        if fresh:
                            dve.wait_ge(gelu_done, g * QUAD + (SAVED + r + 3))
                        else:
                            dve.wait_ge(saved_loaded[slot], g * (8 * QUAD) + 16 * (r // 2) + 16)
                        dve.wait_ge(wlo_ready, g * (2 * QUAD) + k + 1)
                        src = act_ring if fresh else saved_ring
                        v.tensor_tensor(wt_ring[:, slot, :], src[:, slot, :], gate_ring[:, slot, :], ALU.mult).then_inc(wt_ready, 1)

                    def low_part(k):
                        dve.wait_ge(whi_ready, g * (2 * QUAD) + k + 1)
                        v.tensor_tensor(g_lo[:, k, :], wt_ring[:, k % 2, :], g_hi[:, k, :].bitcast(f32), ALU.subtract).then_inc(wlo_ready, 1)

                    gated_acts(0)
                    for k in range(1, 2 * QUAD):
                        gated_acts(k)
                        low_part(k - 1)
                    low_part(2 * QUAD - 1)
                    for i in range(4 * NT):
                        t, half = (i % (2 * NT)) // 2, i % 2
                        dve.wait_ge(y_done, g * (4 * NT) + i + 1)
                        xs = X[:, t, half * 512:(half + 1) * 512]
                        v.tensor_tensor(xs, PS[:, 2 + i % 4, :], xs, ALU.add).then_inc(y_added, 1)
                stage_end(dve, l, S_PEER)
                layer_end(dve, l)

        @block.gpsimd
        def _(pool):
            g = nc.gpsimd
            pool.wait_ge(const_loaded, 16)
            with g.Fori(0, DEPTH) as l:
                pool.sem_inc(ulo_ready, 2)
                pool.sem_inc(vlo_ready, 2)
                stage_end(pool, l, S_NORM1)
                g.memset(raw[:, 0:12, 0:CONV_K - 1], 0.0).then_inc(pad_zeroed, 1)
                stage_end(pool, l, S_PROJ)
                stage_end(pool, l, S_PREP)
                stage_end(pool, l, S_GATES)
                for t in range(NT):
                    cols = slice(t * GH, (t + 1) * GH)

                    def grid(i):
                        return tmp[:, i, :].rearrange("p (h n) -> p h n", n=P)

                    g.tensor_tensor(grid(4), gb[:, :, t * P:(t + 1) * P], along(gcol[:, cols], P), ALU.subtract)
                    g.tensor_tensor(grid(5), over(strict, GH), along(beta[:, cols], P), ALU.mult)
                    pool.drain()
                    g.tensor_scalar(tmp[:, 0, :], tmp[:, 4, :], 0.0, None, ALU.max)
                    g.tensor_scalar(tmp[:, 1, :], tmp[:, 4, :], 0.0, None, ALU.min)
                    pool.drain().then_inc(diff_ready, 1)
                    if t:
                        pool.wait_ge(kq_used, t)
                    pool.wait_ge(decay_ready, t + 1)
                    g.tensor_tensor(tmp[:, 2, :], tmp[:, 0, :], tmp[:, 5, :], ALU.mult)
                    g.tensor_tensor(grid(3), grid(1), over(tri_chunk, GH), ALU.mult)
                    pool.drain().then_inc(mask_ready, 1)
                for h in range(GH):
                    pool.wait_ge(eg_ready, h + 1)
                    g.tensor_tensor(qd[:, h, :], conv[:, h, :], tmp[:, 6 + h % 2, :], ALU.mult).then_inc(qd_ready, 1)
                stage_end(pool, l, S_KQ)
                for k in range(4 * LEVELS):
                    t = k % 4
                    if k >= 2:
                        if k < 6:
                            pool.wait_ge(inv_stored, k - 1)
                        else:
                            pool.wait_ge(p_done, k - 5)
                    g.tensor_tensor(tmp[:, k % 2, :].rearrange("p (h n) -> p h n", n=P),
                                    A[:, t, :].rearrange("p (h n) -> p h n", n=P), over(level(k // 4), GH), ALU.mult).then_inc(lev_ready, 1)
                stage_end(pool, l, S_INV)
                for k in (S_UW, S_SCAN, S_ONORM, S_FOX):
                    stage_end(pool, l, k)
                pool.dma_start(memx[:], mem.rearrange("(t p) d -> p t d", p=P)).then_inc(mem_loaded, 16)
                for k in (S_OUT1, S_NORM2, S_XPROJ, S_XNORM, S_XATT, S_OUT2, S_NORM3):
                    stage_end(pool, l, k)
                pool.dma_start(keys_sb.rearrange("p k n -> p (k n)"), keys[bass.ds(l, 1)].rearrange("l p n -> (l p) n")).then_inc(keys_loaded, 16)
                stage_end(pool, l, S_PQ)

                def split_u(n, slot):
                    pool.wait_ge(uhi_ready, n + 3)
                    g.tensor_tensor(u_lo[:, slot, :], u_raw[:, slot, :], u_hi[:, slot, :].bitcast(f32), ALU.subtract).then_inc(ulo_ready, 1)

                with g.Fori(0, SAVED // 2) as j:
                    for slot in range(2):
                        split_u(j * 2 + slot, slot)
                stage_end(pool, l, S_PICK)
                with g.Fori(0, SAVED // QUAD) as q:
                    def split_v(k):
                        pool.wait_ge(vhi_ready, q * (2 * QUAD) + k + 3)
                        g.tensor_tensor(v_lo[:, k, :], v_raw[:, k % 2, :], v_hi[:, k, :].bitcast(f32), ALU.subtract).then_inc(vlo_ready, 1)

                    for r in range(QUAD):
                        split_u(q * QUAD + (SAVED + r), r % 2)
                        if r:
                            split_v(r if r > 1 else 0)
                        if r == 1:
                            split_v(1)
                    for k in range(QUAD, 2 * QUAD):
                        split_v(k)
                stage_end(pool, l, S_PEER)
                pool.wait_ge(layer_left, 4 * l + 4)
                pool.sem_inc(layer_entered, 1)
                for s in local:
                    pool.sem_clear(s)
                pool.sem_inc(cleared, 1)


def kernel(**inputs):
    import numpy as _np
    import concourse.bacc as _bacc
    from concourse import mybir as _mybir
    from concourse.bass_utils import run_bass_kernel_spmd as _run

    a = {k: _np.asarray(v) for k, v in inputs.items()}

    def groups(w):
        n = w.shape[1] // 512
        return w.reshape(DC, P, n, 512).transpose(2, 1, 0, 3).reshape(n, P, DC * 512)

    packs, pars = [], []
    for l in range(DEPTH):
        w = a["w_in"][l]
        small = _np.zeros((D, 512), w.dtype)
        small[:, 0:8] = w[:, 2048:2056]
        small[:, 8:16] = w[:, 3592:3600]
        parts = [w[:, 0:2048], w[:, 2056:3592], small, a["w_out"][l], a["w_mq"][l], a["w_mkv"][l], a["w_mo"][l], a["w_pq"][l]]
        packs.append(_np.concatenate([groups(p) for p in parts]).reshape(N_PAIRS, 2, P, DC * 512))

        def col(v):
            return v.reshape(-1, P).T

        def row(v):
            return _np.broadcast_to(v, (P, v.shape[0]))

        conv = a["conv_w"][l][:, 0, :].reshape(CONV_K, 12, P).transpose(2, 1, 0).reshape(P, 12 * CONV_K)
        pars.append(_np.concatenate([
            col(a["mix_norm"][l]), col(a["xattn_norm"][l]), col(a["mem_norm"][l]), col(a["ffn_norm"][l]), conv,
            col(a["gdn_out_norm"][l]), col(_np.tile(a["fox_q_norm"][l], 2)), col(_np.tile(a["fox_k_norm"][l], 2)),
            col(a["mq_norm"][l]), col(a["mk_norm"][l]), row(a["dt_bias"][l]), row(a["a_log"][l]), row(a["fox_f_bias"][l])], axis=1))
    arrays = {
        "x": a["x"][0], "mem": a["mem"][0], "weights": _np.stack(packs), "params": _np.stack(pars), "consts": constants(),
        "keys": a["sub_keys"].transpose(0, 4, 2, 1, 3).reshape(DEPTH, P, 16 * P),
        "expert_u": a["expert_u"].reshape(DEPTH, NEXP_HI, P, DC, P).transpose(0, 1, 4, 3, 2).reshape(DEPTH, NEXP_HI, P, DC * P),
        "expert_v": a["expert_v"],
    }
    nc = _bacc.Bacc("TRN2", target_bir_lowering=False, num_devices=1)
    feeds, args = {}, []
    for name, v in arrays.items():
        v = _np.ascontiguousarray(v)
        feeds[f"in_{name}"] = v
        args.append(nc.dram_tensor(f"in_{name}", v.shape, _mybir.dt.from_np(v.dtype), kind="ExternalInput").ap())
    out = nc.dram_tensor("out", (SEQ, D), _mybir.dt.float32, kind="ExternalOutput").ap()
    trunk_kernel(nc, *args, out)
    r = _run(nc, [feeds], core_ids=[0])
    return r.results[0]["out"].reshape(1, SEQ, D)
```
